# Optimizing a Trainium2 kernel written in Bass

```python
import math
import jax
import jax.numpy as jnp
from jax import lax
import numpy as np

D_MODEL = 1024
BATCH = 1
SEQ = 256
DEPTH = 2

GRID_W = 64
CTX_LEN = 256
HEAD_DIM = 64
ROPE_THETA = 10000.0
NORM_EPS = 1e-6
Q_BLOCK = 128
NEG_INF = -1e30
ADA_CHUNKS = 6

NA_HEADS = 8
NA_WIN_H = 8
NA_WIN_W = 16
DIFF_HEADS = 4
DIFF_V_DIM = 2 * HEAD_DIM
GQA_Q_HEADS = 8
GQA_KV_HEADS = 2
GQA_GROUP = GQA_Q_HEADS // GQA_KV_HEADS
MLA_HEADS = 8
MLA_NOPE = 64
MLA_ROPE = 32
MLA_QK = MLA_NOPE + MLA_ROPE
MLA_V = 64
MLA_Q_RANK = 256
MLA_KV_RANK = 128
D_FF = 2816
N_EXPERTS = 8
TOP_K = 2
D_FF_EXPERT = 3584
MOE_BLOCK = 128

N_EVEN = (DEPTH + 1) // 2
N_ODD = DEPTH // 2

EVEN_COLS = (NA_HEADS * HEAD_DIM, NA_HEADS * HEAD_DIM, NA_HEADS * HEAD_DIM,
             DIFF_HEADS * 2 * HEAD_DIM, DIFF_HEADS * 2 * HEAD_DIM, DIFF_HEADS * DIFF_V_DIM)
ODD_COLS = (GQA_Q_HEADS * HEAD_DIM, GQA_KV_HEADS * HEAD_DIM, GQA_KV_HEADS * HEAD_DIM,
            MLA_Q_RANK, MLA_KV_RANK, MLA_ROPE)
EVEN_IN = sum(EVEN_COLS)
ODD_IN = sum(ODD_COLS)
EVEN_SPLITS = tuple(int(s) for s in np.cumsum(EVEN_COLS)[:-1])
ODD_SPLITS = tuple(int(s) for s in np.cumsum(ODD_COLS)[:-1])
EVEN_OUT = NA_HEADS * HEAD_DIM + DIFF_HEADS * DIFF_V_DIM
ODD_OUT = GQA_Q_HEADS * HEAD_DIM + MLA_HEADS * MLA_V

kernel_name = 'hybrid_na_diff_gqa_mla_moe_dit'

def rms_norm(x, g):
    xf = x.astype(jnp.float32)
    y = xf * lax.rsqrt(jnp.mean(xf * xf, axis=-1, keepdims=True) + NORM_EPS)
    return (y * g.astype(jnp.float32)).astype(x.dtype)

def modulate(h, shift, scale):
    return h * (1.0 + scale) + shift

def rope_1d(x, pos):
    half = x.shape[-1] // 2
    freqs = ROPE_THETA ** (-jnp.arange(half, dtype=jnp.float32) / half)
    ang = pos.astype(jnp.float32)[:, None] * freqs[None, :]
    cos = jnp.cos(ang).astype(x.dtype)
    sin = jnp.sin(ang).astype(x.dtype)
    x1, x2 = x[..., :half], x[..., half:]
    return jnp.concatenate([x1 * cos - x2 * sin, x1 * sin + x2 * cos], axis=-1)

def rope_2d(x, rows, cols):
    half = x.shape[-1] // 2
    return jnp.concatenate([rope_1d(x[..., :half], rows), rope_1d(x[..., half:], cols)], axis=-1)

def split_heads(t, n_heads, d):
    B, S, _ = t.shape
    return t.reshape(B, S, n_heads, d).transpose(0, 2, 1, 3)

def merge_heads(o):
    B, S = o.shape[0], o.shape[-2]
    return jnp.moveaxis(o, -2, 1).reshape(B, S, -1)

def over_query_blocks(fn, q):
    *lead, S, d = q.shape
    nb = S // Q_BLOCK
    qb = jnp.moveaxis(q.reshape(*lead, nb, Q_BLOCK, d), -3, 0)
    ob = jnp.moveaxis(lax.map(fn, qb), 0, -3)
    return ob.reshape(*ob.shape[:-3], S, ob.shape[-1])

def softmax_attend(q, k, v, scale):
    s = jnp.einsum('bhgqd,bhkd->bhgqk', q, k).astype(jnp.float32) * scale
    p = jax.nn.softmax(s, axis=-1).astype(v.dtype)
    return jnp.einsum('bhgqk,bhkd->bhgqd', p, v)

def diff_attend(q, k, v, lam, scale):
    s = jnp.einsum('bhmqd,bhmkd->bhmqk', q, k).astype(jnp.float32) * scale
    p = jax.nn.softmax(s, axis=-1)
    pd = (p[:, :, 0] - lam * p[:, :, 1]).astype(v.dtype)
    return jnp.einsum('bhqk,bhkd->bhqd', pd, v)

def neighbourhood_attention(q, k, v, k_ctx, v_ctx, rpb, scale):
    B, H, S, d = q.shape
    rows_n = S // GRID_W
    kh = min(NA_WIN_H, rows_n)
    qg = q.reshape(B, H, rows_n, GRID_W, d)
    kg = k.reshape(B, H, rows_n, GRID_W, d)
    vg = v.reshape(B, H, rows_n, GRID_W, d)
    col = jnp.arange(GRID_W)
    c0 = jnp.clip(col - NA_WIN_W // 2, 0, GRID_W - NA_WIN_W)
    col_in = (col[None, :] >= c0[:, None]) & (col[None, :] < c0[:, None] + NA_WIN_W)
    mask = jnp.broadcast_to(col_in[:, None, :], (GRID_W, kh, GRID_W)).reshape(GRID_W, kh * GRID_W)
    dc = jnp.clip(col[None, :] - col[:, None], -(NA_WIN_W - 1), NA_WIN_W - 1) + NA_WIN_W - 1
    n_lat = kh * GRID_W

    def one_row(r):
        r0 = jnp.clip(r - kh // 2, 0, rows_n - kh)
        kb = lax.dynamic_slice_in_dim(kg, r0, kh, axis=2).reshape(B, H, n_lat, d)
        vb = lax.dynamic_slice_in_dim(vg, r0, kh, axis=2).reshape(B, H, n_lat, d)
        qr = lax.dynamic_index_in_dim(qg, r, axis=2, keepdims=False)
        dr = r0 + jnp.arange(kh) - r + NA_WIN_H - 1
        bias = rpb[:, dr[None, :, None], dc[:, None, :]].reshape(H, GRID_W, n_lat)
        s_lat = jnp.einsum('bhqd,bhkd->bhqk', qr, kb).astype(jnp.float32) * scale + bias.astype(jnp.float32)
        s_lat = jnp.where(mask, s_lat, NEG_INF)
        s_ctx = jnp.einsum('bhqd,bhkd->bhqk', qr, k_ctx).astype(jnp.float32) * scale
        p = jax.nn.softmax(jnp.concatenate([s_lat, s_ctx], axis=-1), axis=-1).astype(v.dtype)
        return (jnp.einsum('bhqk,bhkd->bhqd', p[..., :n_lat], vb)
                + jnp.einsum('bhqk,bhkd->bhqd', p[..., n_lat:], v_ctx))

    o = lax.map(one_row, jnp.arange(rows_n))
    return jnp.moveaxis(o, 0, 2).reshape(B, H, S, d)

def even_project(t, w_in, na_q_g, na_k_g, diff_q_g, diff_k_g):
    B, S, _ = t.shape
    qa, ka, va, qb, kb, vb = jnp.split(t @ w_in, EVEN_SPLITS, axis=-1)
    qa = rms_norm(split_heads(qa, NA_HEADS, HEAD_DIM), na_q_g)
    ka = rms_norm(split_heads(ka, NA_HEADS, HEAD_DIM), na_k_g)
    va = split_heads(va, NA_HEADS, HEAD_DIM)
    qb = rms_norm(qb.reshape(B, S, DIFF_HEADS, 2, HEAD_DIM).transpose(0, 2, 3, 1, 4), diff_q_g)
    kb = rms_norm(kb.reshape(B, S, DIFF_HEADS, 2, HEAD_DIM).transpose(0, 2, 3, 1, 4), diff_k_g)
    vb = split_heads(vb, DIFF_HEADS, DIFF_V_DIM)
    return qa, ka, va, qb, kb, vb

def even_mixer(h, hc, w_in, w_out, na_q_g, na_k_g, na_rpb, diff_q_g, diff_k_g,
               lq1, lk1, lq2, lk2, subln_g, layer_idx, need_ctx):
    S = h.shape[1]
    pos = jnp.arange(S)
    rows, cols = pos // GRID_W, pos % GRID_W
    scale = HEAD_DIM ** -0.5
    lam_init = 0.8 - 0.6 * math.exp(-0.3 * layer_idx)
    lam = (jnp.exp(jnp.sum(lq1.astype(jnp.float32) * lk1.astype(jnp.float32)))
           - jnp.exp(jnp.sum(lq2.astype(jnp.float32) * lk2.astype(jnp.float32))) + lam_init)
    qa, ka, va, qb, kb, vb = even_project(h, w_in, na_q_g, na_k_g, diff_q_g, diff_k_g)
    qca, kca, vca, qcb, kcb, vcb = even_project(hc, w_in, na_q_g, na_k_g, diff_q_g, diff_k_g)
    out_a = neighbourhood_attention(qa, ka, va, kca, vca, na_rpb, scale)
    qb = rope_2d(qb, rows, cols)
    kb = rope_2d(kb, rows, cols)
    kb_all = jnp.concatenate([kb, kcb], axis=3)
    vb_all = jnp.concatenate([vb, vcb], axis=2)
    out_b = over_query_blocks(lambda qi: diff_attend(qi, kb_all, vb_all, lam, scale), qb)
    out_b = rms_norm(out_b, subln_g) * (1.0 - lam_init)
    y = jnp.concatenate([merge_heads(out_a), merge_heads(out_b)], axis=-1) @ w_out
    if not need_ctx:
        return y, None
    oca = softmax_attend(qca[:, :, None], kca, vca, scale)[:, :, 0]
    ocb = rms_norm(diff_attend(qcb, kcb, vcb, lam, scale), subln_g) * (1.0 - lam_init)
    yc = jnp.concatenate([merge_heads(oca), merge_heads(ocb)], axis=-1) @ w_out
    return y, yc

def odd_project(t, w_in, gqa_q_g, gqa_k_g, cq_g, w_uq, ckv_g, w_ukv, mla_q_g, mla_k_g):
    B, S, _ = t.shape
    qc, kc, vc, cq, ckv, kr = jnp.split(t @ w_in, ODD_SPLITS, axis=-1)
    qc = rms_norm(qc.reshape(B, S, GQA_KV_HEADS, GQA_GROUP, HEAD_DIM).transpose(0, 2, 3, 1, 4), gqa_q_g)
    kc = rms_norm(split_heads(kc, GQA_KV_HEADS, HEAD_DIM), gqa_k_g)
    vc = split_heads(vc, GQA_KV_HEADS, HEAD_DIM)
    qd = split_heads(rms_norm(cq, cq_g) @ w_uq, MLA_HEADS, MLA_QK)
    kv = split_heads(rms_norm(ckv, ckv_g) @ w_ukv, MLA_HEADS, MLA_NOPE + MLA_V)
    kr = jnp.broadcast_to(split_heads(kr, 1, MLA_ROPE), (B, MLA_HEADS, S, MLA_ROPE))
    kd = jnp.concatenate([kv[..., :MLA_NOPE], kr], axis=-1)
    vd = kv[..., MLA_NOPE:]
    return qc, kc, vc, rms_norm(qd, mla_q_g), rms_norm(kd, mla_k_g), vd

def odd_mixer(h, hc, w_in, w_out, gqa_q_g, gqa_k_g, cq_g, w_uq, ckv_g, w_ukv, mla_q_g, mla_k_g, need_ctx):
    S = h.shape[1]
    pos = jnp.arange(S)
    rows, cols = pos // GRID_W, pos % GRID_W
    qc, kc, vc, qd, kd, vd = odd_project(h, w_in, gqa_q_g, gqa_k_g, cq_g, w_uq, ckv_g, w_ukv, mla_q_g, mla_k_g)
    qcc, kcc, vcc, qcd, kcd, vcd = odd_project(hc, w_in, gqa_q_g, gqa_k_g, cq_g, w_uq, ckv_g, w_ukv, mla_q_g, mla_k_g)
    scale_c = HEAD_DIM ** -0.5
    qc = rope_2d(qc, rows, cols)
    kc_all = jnp.concatenate([rope_2d(kc, rows, cols), kcc], axis=2)
    vc_all = jnp.concatenate([vc, vcc], axis=2)
    out_c = over_query_blocks(lambda qi: softmax_attend(qi, kc_all, vc_all, scale_c), qc)
    scale_d = MLA_QK ** -0.5

    def rope_mla(t):
        return jnp.concatenate([t[..., :MLA_NOPE], rope_2d(t[..., MLA_NOPE:], rows, cols)], axis=-1)

    qd = rope_mla(qd)[:, :, None]
    kd_all = jnp.concatenate([rope_mla(kd), kcd], axis=2)
    vd_all = jnp.concatenate([vd, vcd], axis=2)
    out_d = over_query_blocks(lambda qi: softmax_attend(qi, kd_all, vd_all, scale_d), qd)
    y = jnp.concatenate([merge_heads(out_c), merge_heads(out_d)], axis=-1) @ w_out
    if not need_ctx:
        return y, None
    occ = softmax_attend(qcc, kcc, vcc, scale_c)
    ocd = softmax_attend(qcd[:, :, None], kcd, vcd, scale_d)
    yc = jnp.concatenate([merge_heads(occ), merge_heads(ocd)], axis=-1) @ w_out
    return y, yc

def swiglu(h, w_gate, w_up, w_down):
    return (jax.nn.silu(h @ w_gate) * (h @ w_up)) @ w_down

def moe_swiglu(h, router, w1, w3, w2):
    B, S, D = h.shape
    t = h.reshape(-1, D)
    N = t.shape[0]
    logits = (t @ router).astype(jnp.float32)
    top_val, top_idx = lax.top_k(logits, TOP_K)
    gates = jax.nn.softmax(top_val, axis=-1)
    flat_e = top_idx.reshape(-1)
    flat_tok = jnp.repeat(jnp.arange(N), TOP_K)
    flat_g = gates.reshape(-1)
    order = jnp.argsort(flat_e)
    e_sorted, tok_sorted, g_sorted = flat_e[order], flat_tok[order], flat_g[order]
    counts = jnp.bincount(flat_e, length=N_EXPERTS)
    padded = ((counts + MOE_BLOCK - 1) // MOE_BLOCK) * MOE_BLOCK
    bounds = jnp.cumsum(padded)
    pad_start = bounds - padded
    start = jnp.cumsum(counts) - counts
    dest = pad_start[e_sorted] + jnp.arange(N * TOP_K) - start[e_sorted]
    cap = (-(-(N * TOP_K) // MOE_BLOCK)) * MOE_BLOCK + N_EXPERTS * MOE_BLOCK
    nb = cap // MOE_BLOCK
    slot_tok = jnp.zeros((cap,), jnp.int32).at[dest].set(tok_sorted.astype(jnp.int32))
    slot_g = jnp.zeros((cap,), jnp.float32).at[dest].set(g_sorted)
    block_e = jnp.minimum(jnp.sum(jnp.arange(nb)[:, None] * MOE_BLOCK >= bounds[None, :], axis=1), N_EXPERTS - 1)
    xb = t[slot_tok].reshape(nb, MOE_BLOCK, D)

    def one_block(args):
        xi, e = args
        return (jax.nn.silu(xi @ w1[e]) * (xi @ w3[e])) @ w2[e]

    yb = lax.map(one_block, (xb, block_e)).reshape(cap, D)
    out = jnp.zeros_like(t).at[slot_tok].add(yb * slot_g[:, None].astype(yb.dtype))
    return out.reshape(B, S, D)

def setup_inputs(seed: int = 0) -> dict:
    key = jax.random.key(seed)
    keys = iter(jax.random.split(key, 48))

    def normal(shape, scale):
        return jax.random.normal(next(keys), shape, dtype=jnp.float32) * scale

    def gain(shape):
        return 1.0 + normal(shape, 0.05)

    D = D_MODEL
    return {
        'x': normal((BATCH, SEQ, D), 1.0),
        'c': normal((BATCH, D), 1.0),
        'ctx': normal((BATCH, CTX_LEN, D), 1.0),
        'c_ctx': normal((D,), 1.0),
        'ada_w': normal((DEPTH, D, ADA_CHUNKS * D), 0.5 * D ** -0.5),
        'ada_b': normal((DEPTH, ADA_CHUNKS * D), 0.02),
        'norm1_g': gain((DEPTH, D)),
        'norm2_g': gain((DEPTH, D)),
        'ev_w_in': normal((N_EVEN, D, EVEN_IN), D ** -0.5),
        'ev_w_out': normal((N_EVEN, EVEN_OUT, D), EVEN_OUT ** -0.5),
        'na_q_g': gain((N_EVEN, HEAD_DIM)),
        'na_k_g': gain((N_EVEN, HEAD_DIM)),
        'na_rpb': normal((N_EVEN, NA_HEADS, 2 * NA_WIN_H - 1, 2 * NA_WIN_W - 1), 0.1),
        'diff_q_g': gain((N_EVEN, HEAD_DIM)),
        'diff_k_g': gain((N_EVEN, HEAD_DIM)),
        'diff_lq1': normal((N_EVEN, HEAD_DIM), 0.1),
        'diff_lk1': normal((N_EVEN, HEAD_DIM), 0.1),
        'diff_lq2': normal((N_EVEN, HEAD_DIM), 0.1),
        'diff_lk2': normal((N_EVEN, HEAD_DIM), 0.1),
        'diff_subln_g': gain((N_EVEN, DIFF_V_DIM)),
        'ffn_w_gate': normal((N_EVEN, D, D_FF), D ** -0.5),
        'ffn_w_up': normal((N_EVEN, D, D_FF), D ** -0.5),
        'ffn_w_down': normal((N_EVEN, D_FF, D), D_FF ** -0.5),
        'od_w_in': normal((N_ODD, D, ODD_IN), D ** -0.5),
        'od_w_out': normal((N_ODD, ODD_OUT, D), ODD_OUT ** -0.5),
        'gqa_q_g': gain((N_ODD, HEAD_DIM)),
        'gqa_k_g': gain((N_ODD, HEAD_DIM)),
        'mla_cq_g': gain((N_ODD, MLA_Q_RANK)),
        'mla_w_uq': normal((N_ODD, MLA_Q_RANK, MLA_HEADS * MLA_QK), MLA_Q_RANK ** -0.5),
        'mla_ckv_g': gain((N_ODD, MLA_KV_RANK)),
        'mla_w_ukv': normal((N_ODD, MLA_KV_RANK, MLA_HEADS * (MLA_NOPE + MLA_V)), MLA_KV_RANK ** -0.5),
        'mla_q_g': gain((N_ODD, MLA_QK)),
        'mla_k_g': gain((N_ODD, MLA_QK)),
        'moe_router': normal((N_ODD, D, N_EXPERTS), D ** -0.5),
        'moe_w1': normal((N_ODD, N_EXPERTS, D, D_FF_EXPERT), D ** -0.5),
        'moe_w3': normal((N_ODD, N_EXPERTS, D, D_FF_EXPERT), D ** -0.5),
        'moe_w2': normal((N_ODD, N_EXPERTS, D_FF_EXPERT, D), D_FF_EXPERT ** -0.5),
    }

def reference(x, c, ctx, c_ctx, ada_w, ada_b, norm1_g, norm2_g,
              ev_w_in, ev_w_out, na_q_g, na_k_g, na_rpb, diff_q_g, diff_k_g,
              diff_lq1, diff_lk1, diff_lq2, diff_lk2, diff_subln_g,
              ffn_w_gate, ffn_w_up, ffn_w_down,
              od_w_in, od_w_out, gqa_q_g, gqa_k_g, mla_cq_g, mla_w_uq, mla_ckv_g, mla_w_ukv,
              mla_q_g, mla_k_g, moe_router, moe_w1, moe_w3, moe_w2):
    xc = ctx
    silu_c = jax.nn.silu(c)
    silu_cc = jax.nn.silu(c_ctx)
    for l in range(DEPTH):
        need_ctx = l < DEPTH - 1
        i = l // 2
        even = l % 2 == 0
        sh1, sc1, g1, sh2, sc2, g2 = jnp.split((silu_c @ ada_w[l] + ada_b[l])[:, None, :], ADA_CHUNKS, axis=-1)
        csh1, csc1, cg1, csh2, csc2, cg2 = jnp.split(silu_cc @ ada_w[l] + ada_b[l], ADA_CHUNKS, axis=-1)
        h = modulate(rms_norm(x, norm1_g[l]), sh1, sc1)
        hc = modulate(rms_norm(xc, norm1_g[l]), csh1, csc1)
        if even:
            y, yc = even_mixer(h, hc, ev_w_in[i], ev_w_out[i], na_q_g[i], na_k_g[i], na_rpb[i],
                               diff_q_g[i], diff_k_g[i], diff_lq1[i], diff_lk1[i], diff_lq2[i], diff_lk2[i],
                               diff_subln_g[i], l, need_ctx)
        else:
            y, yc = odd_mixer(h, hc, od_w_in[i], od_w_out[i], gqa_q_g[i], gqa_k_g[i], mla_cq_g[i], mla_w_uq[i],
                              mla_ckv_g[i], mla_w_ukv[i], mla_q_g[i], mla_k_g[i], need_ctx)

        def channel_mix(t):
            if even:
                return swiglu(t, ffn_w_gate[i], ffn_w_up[i], ffn_w_down[i])
            return moe_swiglu(t, moe_router[i], moe_w1[i], moe_w3[i], moe_w2[i])

        x = x + g1 * y
        x = x + g2 * channel_mix(modulate(rms_norm(x, norm2_g[l]), sh2, sc2))
        if need_ctx:
            xc = xc + cg1 * yc
            xc = xc + cg2 * channel_mix(modulate(rms_norm(xc, norm2_g[l]), csh2, csc2))
    return x


_drawn_inputs = setup_inputs


def setup_inputs(seed=0):
    import zlib

    import numpy as np

    out = dict(_drawn_inputs(seed))
    spreads = {}
    factors = {'norm1_g': 5.393,
     'na_q_g': 8.0,
     'na_k_g': 8.0,
     'na_rpb': 8.0,
     'diff_q_g': 6.394,
     'diff_k_g': 8.0,
     'diff_lq1': 5.249,
     'diff_lk1': 8.0,
     'diff_lq2': 5.367,
     'diff_lk2': 8.0,
     'diff_subln_g': 4.937,
     'gqa_q_g': 8.0,
     'gqa_k_g': 8.0,
     'mla_cq_g': 8.0,
     'mla_ckv_g': 8.0,
     'mla_q_g': 8.0,
     'mla_k_g': 8.0}
    for name, (base, spread) in spreads.items():
        noise = np.random.default_rng([zlib.crc32(name.encode()), seed]).standard_normal(out[name].shape)
        drawn = base * np.exp(spread * noise) if base else spread * noise
        out[name] = jnp.asarray(drawn.astype(out[name].dtype))
    for name, factor in factors.items():
        out[name] = (out[name] * factor).astype(out[name].dtype)
    return out
```

```python
import math
from contextlib import ExitStack

import numpy as np

import concourse.bass as bass
from concourse import mybir

F32 = mybir.dt.float32
I32 = mybir.dt.int32
ALU = mybir.AluOpType
ACT = mybir.ActivationFunctionType
AX = mybir.AxisListType

P = 128
D = 1024
KT = D // P
S_LAT = 256
S_ALL = 512
GRID_W = 64
HD = 64
NA_WIN_W = 16
NA_WIN_H = 8
ROPE_THETA = 10000.0
EPS = 1e-6
NEG = -1e30
D_FF = 2816
FT = D_FF // P
D_FFE = 3584
FTE = D_FFE // P
NE = 8
MLA_QK, MLA_NOPE, MLA_ROPE = 96, 64, 32
RPB_DR = 7
RPB_ROW = (2 * GRID_W - 1) * GRID_W
CAP = 96
ROUNDS = -(-S_LAT // CAP)
LAM_INIT = 0.8 - 0.6 * math.exp(-0.3 * 0)

RING = 4
SLOT = 4096
MRING = 7
MCH = 21
QF = 4

VEC = [("na_q_g", 64), ("na_k_g", 64), ("diff_q_g", 64), ("diff_k_g", 64), ("gqa_q_g", 64),
       ("gqa_k_g", 64), ("mla_cq_g", 256), ("mla_ckv_g", 128), ("mla_q_g", 96), ("mla_k_g", 96),
       ("diff_subln_g", 128), ("diff_lq1", 64), ("diff_lk1", 64), ("diff_lq2", 64), ("diff_lk2", 64)]
VEC_AT = {}
_o = 0
for _n, _w in VEC:
    VEC_AT[_n] = (_o, _w)
    _o += _w
VEC_N = _o

CST = [("ident", 128), ("upper", 128), ("iota", CAP), ("rope64", 256), ("rope32", 128),
       ("mask", 64), ("rank", 8)]
CST_AT = {}
_o = 0
for _n, _w in CST:
    CST_AT[_n] = (_o, _w)
    _o += _w
CST_N = _o


def rope_table(dim, tile):
    pos = np.arange(tile * P, tile * P + P)
    half = dim // 4
    freqs = (ROPE_THETA ** (-np.arange(half, dtype=np.float32) / half)).astype(np.float32)
    cos, sin = [], []
    for p in (pos // GRID_W, pos % GRID_W):
        ang = (p.astype(np.float32)[:, None] * freqs[None, :]).astype(np.float32)
        c, s = np.cos(ang), np.sin(ang)
        cos += [c, c]
        sin += [-s, s]
    return np.concatenate(cos + sin, axis=1).astype(np.float32)


def shape_constants():
    c = np.zeros((P, CST_N), np.float32)

    def put(name, a):
        o, w = CST_AT[name]
        c[:, o:o + w] = a

    i = np.arange(P)
    put("ident", np.eye(P))
    put("upper", (i[:, None] < i[None, :]))
    put("iota", np.broadcast_to(np.arange(CAP), (P, CAP)))
    put("rope64", np.concatenate([rope_table(64, 0), rope_table(64, 1)], axis=1))
    put("rope32", np.concatenate([rope_table(32, 0), rope_table(32, 1)], axis=1))
    col = np.arange(GRID_W)
    c0 = np.clip(col - NA_WIN_W // 2, 0, GRID_W - NA_WIN_W)
    inside = (col[None, :] >= c0[:, None]) & (col[None, :] < c0[:, None] + NA_WIN_W)
    put("mask", np.tile(np.where(inside, 0.0, NEG), (2, 1)))
    put("rank", np.broadcast_to(NE - np.arange(NE), (P, NE)))
    return c


class Chain:

    def __init__(self, eng, sem, reg=None, per=0):
        self.eng, self.sem, self.reg, self.per, self.n = eng, sem, reg, per, 0

    def after(self, ins):
        ins.then_inc(self.sem, 1)
        self.n += 1
        self.eng.wait_ge(self.sem, self.n if self.reg is None else self.reg * self.per + self.n)


def build_kernel(nc, a, out):
    with ExitStack() as ctx:
        def sb(name, shape, dt=F32):
            return ctx.enter_context(nc.sbuf_tensor(name, shape, dt))

        def sem(name):
            return ctx.enter_context(nc.semaphore(name))

        xT = sb("xT", [P, KT, S_ALL])
        hT = sb("hT", [P, KT, S_ALL])
        ring = sb("ring", [P, RING, SLOT])
        work = sb("work", [P, 16384])
        scr = sb("scr", [P, 11, 512])
        cst = sb("cst", [P, CST_N])
        vec = sb("vec", [P, VEC_N])
        bt = sb("bt", [P, 8, 6, GRID_W])
        ones = sb("ones", [P, P])
        cond = sb("cond", [P, 16])
        scond = sb("scond", [P, 16])
        adab = sb("adab", [P, 2, 48])
        ng = sb("ng", [P, 2, 2, KT])
        ada = sb("ada", [P, 2, 48, 2])
        amod = sb("amod", [P, 2, 2, KT, 2])
        ss = sb("ss", [P, 4, 8])
        rt8 = sb("rt8", [P, 4, 8])
        rs8 = sb("rs8", [P, 4, 8])
        krt = sb("krt", [P, 4, 32])
        eps = sb("eps", [P, 1])
        mx = sb("mx", [P, 64])
        nmx = sb("nmx", [P, 64])
        sums = sb("sums", [P, 64])
        rsum = sb("rsum", [P, 64])
        lamt = sb("lamt", [P, 8])
        rtr = sb("rtr", [P, KT, NE])
        nit = sb("nit", [P, 1], I32)
        ps = [ctx.enter_context(nc.psum_tensor(f"ps{b}", [P, 512], F32)) for b in range(8)]

        def cv(name, lo=0, hi=None):
            o, w = CST_AT[name]
            return cst[:, o + lo:o + (w if hi is None else hi)]

        def vv(name):
            o, w = VEC_AT[name]
            return vec[:, o:o + w]

        ident = cv("ident")

        def rope_of(dim, tile):
            o = tile * 2 * dim
            n = "rope64" if dim == 64 else "rope32"
            return cv(n, o, o + dim), cv(n, o + dim, o + 2 * dim)

        def area(o, *dims):
            n = int(np.prod(dims))
            v = work[:, o:o + n]
            if len(dims) == 2:
                v = v.rearrange("p (a b) -> p a b", b=dims[1])
            if len(dims) == 3:
                v = v.rearrange("p (a b c) -> p a b c", b=dims[1], c=dims[2])
            return v

        QT0 = [area(2048 * j, 4, S_ALL) for j in range(4)]
        V0 = area(8192, 4, 1024)
        O0 = area(12288, 4, 1024)
        hid = area(0, FT, S_ALL)
        QcT = area(0, 4, S_LAT)
        KcT = area(1024, 2, S_ALL)
        QdT = area(2048, 8, S_LAT)
        KdT = area(4096, 8, S_ALL)
        Vc = area(8192, 4, 128)
        Vd = area(8704, 4, 512)
        cqT = area(10752, 2, S_LAT)
        ckvT = area(11264, 1, S_ALL)[:, 0, :]
        O1 = area(12288, 2, 1024)
        btf = bt[:, :, :, :].rearrange("p a b c -> p (a b c)")
        htok = btf[:, 0:2 * D].rearrange("p (a b) -> p a b", b=D)
        NI = ROUNDS * NE

        def tail(o, *dims):
            n = int(np.prod(dims))
            v = btf[:, 2 * D + o:2 * D + o + n]
            if len(dims) == 2:
                return v.rearrange("p (a b) -> p a b", b=dims[1])
            return v.rearrange("p (a b c) -> p a b c", b=dims[1], c=dims[2])

        ro = tail(0, 24, 2, NE)
        posr = tail(384, 2, NI)
        gat = tail(384 + 2 * NI, 2, NI)
        chs = tail(384 + 4 * NI, 2, NI)
        kn = tail(384 + 6 * NI, 3, P)
        mslot = [area(SLOT * j, SLOT) for j in range(3)] + [ring[:, s, :] for s in (1, 2, 3, 0)]
        xg = area(12288, KT, CAP)
        hide = area(13056, FTE, CAP)
        yT = hT[:, 0:2, :].rearrange("p a b -> p (a b)")[:, 0:KT * CAP].rearrange("p (a b) -> p a b", b=CAP)
        ytok = hT[:, 2:4, :].rearrange("p a b -> p (a b)")
        pgT = hT[:, 4, 0:S_LAT]
        sel = [hT[:, 5, 0:CAP], hT[:, 5, 128:128 + CAP]]
        gsel = [hT[:, 6, 0:CAP], hT[:, 6, 128:128 + CAP]]

        sq = [scr[:, i, :] for i in range(4)]
        rt, rstd = scr[:, 4, :], scr[:, 5, :]
        tn = [scr[:, 6 + i, :] for i in range(3)]
        ra, rb = scr[:, 9, :], scr[:, 10, :]
        prob = [scr[:, 2 + i, :] for i in range(4)]
        probT = [scr[:, 9 + i, :] for i in range(2)]
        kda = [scr[:, 2 + i, 0:384].rearrange("p (h d) -> p h d", d=MLA_QK) for i in range(2)]

        class Stage:
            at = 0

            def __init__(self, n):
                self.first, self.n = Stage.at, n
                Stage.at += n

        sA0a, sW0, sA0b, sO0, sF0, sD0, sA1, sW1, sU1, sO1 = (
            Stage(n) for n in (4, 6, 8, 2, 11, 8, 12, 3, 1, 2))
        PRE = Stage.at

        def slot_of(g):
            return g % RING

        def slot3(g, w):
            return ring[:, slot_of(g), :].rearrange("p (a b) -> p a b", b=w)

        s_x = sem("x_loaded")
        s_cst = sem("constants_loaded")
        s_bt = sem("bias_loaded")
        s_ones = sem("ones_set")
        slot_full = [sem(f"slot_full{i}") for i in range(RING)]
        ada_used = sem("modulation_chunks_used")
        mslot_full = [sem(f"expert_slot_full{i}") for i in range(MRING)]
        s_scond = sem("silu_cond_ready")
        d_step = sem("dve_step")
        p_step = sem("pool_step")
        a_step = sem("act_step")
        gain_rd = sem("gains_prepared")
        lam_in = sem("lambda_dots_ready")
        lam_ex = sem("lambda_exps_ready")
        norm = {}
        for nm in ("n00", "n01", "n10", "n11"):
            norm[nm] = {k: sem(f"{nm}_{k}") for k in ("square", "summed", "root", "scaled", "ready")}
        proj = {}
        for nm in ("L0", "L1", "UQ"):
            proj[nm] = {k: sem(f"proj{nm}_{k}") for k in
                        ("done", "squared", "reduced", "root", "taken", "normed", "rotated", "turned", "stored")}
        att = {}
        for nm in ("A0", "A1"):
            att[nm] = {k: sem(f"att{nm}_{k}") for k in
                       ("score", "max", "exp", "mixed", "turned", "copied", "pv", "out", "osq", "ored",
                        "oroot", "otok", "oturned", "ostored")}
        outp = {}
        for nm in ("O0", "O1"):
            outp[nm] = {k: sem(f"out{nm}_{k}") for k in ("done", "added")}
        gu_mm = sem("ffn_gate_up_done")
        silu_rd = sem("ffn_silu_ready")
        hid_rd = sem("ffn_hidden_ready")
        dn_mm = sem("ffn_down_done")
        dn_half = sem("ffn_down_first_halves_done")
        dn_add = sem("ffn_down_added")
        tok_t = sem("expert_tokens_turned")
        tok_rd = sem("expert_tokens_ready")
        rt_mm = sem("router_logits_done")
        rt_sel = sem("router_choice_ready")
        rt_ein = sem("router_exp_in")
        rt_ex = sem("router_exp_ready")
        rt_pos = sem("router_positions_done")
        items_rd = sem("item_count_ready")
        m_sel = sem("expert_select_ready")
        m_gat = sem("expert_gathered")
        m_xg = sem("expert_tokens_copied")
        m_pgt = sem("expert_gates_turned")
        m_pg = sem("expert_gates_copied")
        m_g = sem("expert_gate_done")
        m_gu = sem("expert_gate_up_done")
        m_silu = sem("expert_silu_ready")
        m_hid = sem("expert_hidden_ready")
        m_dn = sem("expert_down_chunks_done")
        m_yc = sem("expert_down_copied")
        m_yt = sem("expert_down_turned")
        m_ytc = sem("expert_turned_copied")
        m_sc = sem("expert_scattered")
        m_add = sem("expert_added")
        s_out = sem("output_stored")

        released = {}
        for st, n0 in ((sA0a, 0), (sA0b, 4), (sA1, 12)):
            for j in range(st.n):
                released[st.first + j] = (ada_used, n0 + j + 1)
        for j in range(6):
            released[sW0.first + j] = (proj["L0"]["done"], 4 * j + 4)
        for j, n in enumerate((2, 6, 10)):
            released[sW1.first + j] = (proj["L1"]["done"], n)
        released[sU1.first] = (proj["UQ"]["done"], 12)
        for st, nm in ((sO0, "O0"), (sO1, "O1")):
            for j in range(2):
                released[st.first + j] = (outp[nm]["done"], 4 * j + 4)
        for j in range(sF0.n):
            released[sF0.first + j] = (gu_mm, 2 * j + 2)
        for j in range(sD0.n):
            released[sD0.first + j] = (dn_mm, j + 1) if j % 2 else (dn_half, j // 2 + 1)

        def head_unit(kind, g, t, lhs, w, width, bank, **kw):
            return dict(kind=kind, g=g, t=t, lhs=lhs, w=w, width=width, bank=bank, **kw)

        def v3(ap, b):
            return ap.rearrange("p (a b) -> p a b", b=b)

        units = {"L0": [], "L1": [], "UQ": []}
        nv = 0
        for j in range(6):
            for t in range(4):
                u = len(units["L0"])
                g = sW0.first + j
                un = dict(g=g, lhs=[hT[:, k, t * P:(t + 1) * P] for k in range(KT)],
                          w=[slot3(g, 512)[:, k, :] for k in range(KT)], width=512, bank=u % 4,
                          last=(t == 3), copies=[], groups=[])
                if j in (2, 5):
                    c0 = 0 if j == 2 else 512
                    un["copies"] = [(V0[:, t, c0:c0 + 512], ps[u % 4][:, :])]
                else:
                    q = {0: 0, 1: 1, 3: 2, 4: 3}[j]
                    nm = ("na_q_g", "na_k_g", "diff_q_g", "diff_k_g")[q]
                    tb = tn[nv % 3]
                    un["sq"] = ps[u % 4][:, :]
                    un["groups"] = [dict(src=v3(ps[u % 4][:, :], HD), sq=(0, 512), nh=8, hd=HD, dst=v3(tb, HD),
                                         gain=vv(nm), outs=[v3(tb, HD)],
                                         rope=(rope_of(64, t) + (0, 64)) if (q >= 2 and t < 2) else None)]
                    un["turn"] = [tb[:, c * P:(c + 1) * P] for c in range(4)]
                    un["store"] = (QT0[q][:, :, t * P:(t + 1) * P], P)
                    nv += 1
                units["L0"].append(un)
        nv = 0
        for c, t in [(0, 0), (0, 1)] + [(1, t) for t in range(4)] + [(2, t) for t in range(4)]:
            u = len(units["L1"])
            b = u % 4
            g = sW1.first + c
            tb = tn[nv % 3]
            width = (512, 512 if t < 2 else 256, 160)[c]
            wv = slot3(g, 512) if c < 2 else ring[:, slot_of(g), 0:KT * 160].rearrange("p (a b) -> p a b", b=160)
            un = dict(g=g, lhs=[hT[:, k, t * P:(t + 1) * P] for k in range(KT)],
                      w=[wv[:, k, 0:width] for k in range(KT)], width=width, bank=b,
                      last=(t == (1 if c == 0 else 3)), copies=[], groups=[], sq=ps[b][:, 0:min(width, 512)])
            if c == 0:
                un["groups"] = [dict(src=v3(ps[b][:, :], HD), sq=(0, 512), nh=8, hd=HD, dst=v3(tb, HD),
                                     gain=vv("gqa_q_g"), outs=[v3(tb, HD)], rope=rope_of(64, t) + (0, 64))]
                un["turn"] = [tb[:, i * P:(i + 1) * P] for i in range(4)]
                un["store"] = (QcT[:, :, t * P:(t + 1) * P], P)
            elif c == 1:
                kb = kn[:, nv % 3, :]
                dup = tb[:, 0:256].rearrange("p (v c d) -> p c v d", c=2, d=HD)
                un["copies"] = [(Vc[:, t, :], ps[b][:, 128:256])]
                un["groups"] = [dict(src=v3(ps[b][:, 0:128], HD), sq=(0, 128), nh=2, hd=HD, dst=v3(kb, HD),
                                     gain=vv("gqa_k_g"), outs=[dup[:, 0], dup[:, 1]],
                                     rope=(rope_of(64, t) + (0, 64)) if t < 2 else None)]
                un["turn"] = [tb[:, 0:128], tb[:, 128:256]]
                un["store"] = (KcT[:, :, t * P:(t + 1) * P], P)
                if t < 2:
                    cq = tb[:, 256:512].unsqueeze(1)
                    un["groups"].append(dict(src=ps[b][:, 256:512].unsqueeze(1), sq=(256, 512), nh=1, hd=256,
                                             dst=cq, gain=vv("mla_cq_g"), outs=[cq], rope=None))
                    un["turn"] += [tb[:, 256:384], tb[:, 384:512]]
                    un["store2"] = (cqT[:, :, t * P:(t + 1) * P], 2)
            else:
                ck = tb[:, 0:128].unsqueeze(1)
                un["copies"] = [(krt[:, t, :], ps[b][:, 128:160])]
                un["groups"] = [dict(src=ps[b][:, 0:128].unsqueeze(1), sq=(0, 128), nh=1, hd=128, dst=ck,
                                     gain=vv("mla_ckv_g"), outs=[ck], rope=None)]
                un["turn"] = [tb[:, 0:128]]
                un["store"] = (ckvT[:, t * P:(t + 1) * P].unsqueeze(1), P)
            units["L1"].append(un)
            nv += 1
        nv = 0
        uqw = ring[:, slot_of(sU1.first), 0:1536].rearrange("p (k n) -> p k n", k=2)
        ukvw = ring[:, slot_of(sU1.first), 1536:2560]
        for t in range(2):
            for hh in range(2):
                u = len(units["UQ"])
                b = u % 4
                tb = tn[nv % 3][:, 0:384].rearrange("p (h d) -> p h d", d=MLA_QK)
                units["UQ"].append(dict(
                    g=sU1.first, lhs=[cqT[:, k, t * P:(t + 1) * P] for k in range(2)],
                    w=[uqw[:, k, hh * 384:(hh + 1) * 384] for k in range(2)], width=384, bank=b, last=False,
                    copies=[], sq=ps[b][:, 0:384],
                    groups=[dict(src=ps[b][:, 0:384].rearrange("p (h d) -> p h d", d=MLA_QK), sq=(0, 384), nh=4,
                                 hd=MLA_QK, dst=tb, gain=vv("mla_q_g"), outs=[tb],
                                 rope=rope_of(32, t) + (MLA_NOPE, 32))],
                    turn=[tb[:, i, :] for i in range(4)],
                    store=(QdT[0:MLA_QK, hh * 4:hh * 4 + 4, t * P:(t + 1) * P], MLA_QK)))
                nv += 1
        for t in range(4):
            for hh in range(2):
                u = len(units["UQ"])
                b = u % 4
                tb = tn[nv % 3][:, 0:384].rearrange("p (h d) -> p h d", d=MLA_QK)
                kd = kda[nv % 2]
                pv = ps[b][:, :].rearrange("p (h d) -> p h d", d=128)
                units["UQ"].append(dict(
                    g=sU1.first, lhs=[ckvT[:, t * P:(t + 1) * P]], w=[ukvw[:, hh * 512:(hh + 1) * 512]],
                    width=512, bank=b, last=(t == 3 and hh == 1),
                    copies=[(kd[:, :, 0:MLA_NOPE], pv[:, :, 0:64]),
                            (kd[:, :, MLA_NOPE:], krt[:, t, :].unsqueeze(1).to_broadcast([P, 4, 32])),
                            (Vd[:, t, hh * 256:(hh + 1) * 256].rearrange("p (h d) -> p h d", d=64), pv[:, :, 64:128])],
                    assembled=True,
                    sq=kd.rearrange("p h d -> p (h d)"),
                    groups=[dict(src=kd, sq=(0, 384), nh=4, hd=MLA_QK, dst=tb, gain=vv("mla_k_g"), outs=[tb],
                                 rope=(rope_of(32, t) + (MLA_NOPE, 32)) if t < 2 else None)],
                    turn=[tb[:, i, :] for i in range(4)],
                    store=(KdT[0:MLA_QK, hh * 4:hh * 4 + 4, t * P:(t + 1) * P], MLA_QK)))
                nv += 1
        for us in units.values():
            v = na = 0
            for un in us:
                if un.get("assembled"):
                    na += 1
                    un["nth_assembled"] = na
                un["x"] = next(i for i, o in enumerate(us) if o is un)
                if un["groups"]:
                    un["v"] = v
                    v += 1
        NV = {nm: sum(1 for u in us if u["groups"]) for nm, us in units.items()}
        LAGT = 2

        def att_plan(layer):
            items, pvs, groups = [], [], []
            tiles = range(4) if layer == 0 else range(2)
            for t in tiles:
                nk = 512 if t < 2 else 256
                k0 = 0 if t < 2 else 256
                kts = range(k0 // P, 4)
                for half in range(2):
                    gp = dict(t=t, half=half)
                    if layer == 0 and half == 0:
                        for h in range(8):
                            rows = slice(64 * (h % 2), 64 * (h % 2) + 64)
                            items.append(dict(q=QT0[0][rows, h // 2, t * P:(t + 1) * P],
                                              k=QT0[1][rows, h // 2, k0:512], nk=nk, scale=1.0,
                                              bias=bt[:, h, 2 - 2 * t:6 - 2 * t, :] if t < 2 else None))
                            pvs.append(dict(items=[len(items) - 1], nk=nk, ob=4 + len(pvs) % 2, dv=64,
                                            v=[V0[:, kt, h * 64:h * 64 + 64] for kt in kts],
                                            dst=O0[:, t, h * 64:h * 64 + 64]))
                    elif layer == 0:
                        for h in range(4):
                            for m in range(2):
                                rows = slice(64 * m, 64 * m + 64)
                                items.append(dict(q=QT0[2][rows, h, t * P:(t + 1) * P],
                                                  k=QT0[3][rows, h, k0:512], nk=nk, scale=1.0, bias=None))
                            pvs.append(dict(items=[len(items) - 2, len(items) - 1], nk=nk, ob=4 + len(pvs) % 2,
                                            dv=128, v=[V0[:, kt, 512 + h * 128:512 + h * 128 + 128] for kt in kts],
                                            dst=O0[:, t, 512 + h * 128:512 + h * 128 + 128]))
                    elif half == 0:
                        for h in range(8):
                            rows = slice(64 * (h % 2), 64 * (h % 2) + 64)
                            kv = h // 4
                            items.append(dict(q=QcT[rows, h // 2, t * P:(t + 1) * P], k=KcT[rows, kv, :], nk=nk,
                                              scale=1.0, bias=None))
                            pvs.append(dict(items=[len(items) - 1], nk=nk, ob=4 + len(pvs) % 2, dv=64,
                                            v=[Vc[:, kt, kv * 64:kv * 64 + 64] for kt in kts],
                                            dst=O1[:, t, h * 64:h * 64 + 64]))
                    else:
                        for h in range(8):
                            items.append(dict(q=QdT[0:MLA_QK, h, t * P:(t + 1) * P], k=KdT[0:MLA_QK, h, :], nk=nk,
                                              scale=float(MLA_QK) ** -0.5, bias=None))
                            pvs.append(dict(items=[len(items) - 1], nk=nk, ob=4 + len(pvs) % 2, dv=64,
                                            v=[Vd[:, kt, h * 64:h * 64 + 64] for kt in kts],
                                            dst=O1[:, t, 512 + h * 64:512 + h * 64 + 64]))
                    gp["pv1"] = len(pvs)
                    gp["sub"] = layer == 0 and half == 1
                    gp["otok"] = (O0 if layer == 0 else O1)[:, t, half * 512:(half + 1) * 512]
                    groups.append(gp)
            for j, pv in enumerate(pvs):
                for i in pv["items"]:
                    items[i]["pv"] = j
            for gi, gp in enumerate(groups):
                gp["e"] = gi
                gp["subs_upto"] = sum(1 for q in groups[:gi + 1] if q["sub"])
            return dict(items=items, pvs=pvs, groups=groups)

        plans = {"A0": att_plan(0), "A1": att_plan(1)}
        DONE_AT = 5

        def closes(pl, i):
            return [gp for gp in pl["groups"] if pl["pvs"][gp["pv1"] - 1]["items"][-1] == i - DONE_AT]

        def pv_at(pl, i):
            return [j for j, pv in enumerate(pl["pvs"]) if pv["items"][-1] == i]

        NSTEP = {nm: len(pl["items"]) + DONE_AT + 2 for nm, pl in plans.items()}

        block = ctx.enter_context(nc.Block())

        @block.sync
        def _(sp):
            def load(g, dst, src, wait=True):
                if g >= RING and wait:
                    sp.wait_ge(*released[g - RING])
                sp.dma_start(dst, src).then_inc(slot_full[slot_of(g)], 16)

            def cols(w, c0, n):
                return w[:, c0:c0 + n].rearrange("(k p) n -> p k n", p=P)

            def matrix(st, w, c0=0):
                for j in range(st.n):
                    load(st.first + j, slot3(st.first + j, 512), cols(w, c0 + 512 * j, 512))

            matrix(sA0a, a["ada_w"][0])
            matrix(sW0, a["ev_w_in"])
            matrix(sA0b, a["ada_w"][0], 2048)
            matrix(sO0, a["ev_w_out"])
            for j in range(sF0.n):
                g = sF0.first + j
                load(g, slot3(g, 256)[:, 0:KT, :], cols(a["ffn_w_gate"], 256 * j, 256))
                load(g, slot3(g, 256)[:, KT:2 * KT, :], cols(a["ffn_w_up"], 256 * j, 256), wait=False)
            for j in range(sD0.n):
                g = sD0.first + j
                dst = ring[:, slot_of(g), 0:11 * 256].rearrange("p (f n) -> p f n", n=256)
                rows = slice((j % 2) * 11 * P, (j % 2 + 1) * 11 * P)
                load(g, dst, a["ffn_w_down"][rows, 256 * (j // 2):256 * (j // 2 + 1)].rearrange("(f p) n -> p f n", p=P))
            matrix(sA1, a["ada_w"][1])
            for j in range(3):
                g = sW1.first + j
                n = 512 if j < 2 else 160
                dst = slot3(g, 512) if j < 2 else ring[:, slot_of(g), 0:KT * 160].rearrange("p (a b) -> p a b", b=160)
                load(g, dst, cols(a["od_w_in"], 512 * j, n))
            load(sU1.first, uqw, a["mla_w_uq"].rearrange("(k p) n -> p k n", p=P))
            load(sU1.first, ukvw, a["mla_w_ukv"], wait=False)
            matrix(sO1, a["od_w_out"])

            w13 = [a[n].rearrange("e (k p) (c n) -> e c p k n", p=P, n=QF * P) for n in ("moe_w1", "moe_w3")]
            w2 = a["moe_w2"].rearrange("e (c f p) n -> e c p f n", p=P, f=QF)

            def expert_chunk(e, c):
                m = mslot[c % MRING]
                if c < 14:
                    return m.rearrange("p (a b) -> p a b", b=QF * P), w13[c % 2][e, c // 2]
                return m.rearrange("p (a b) -> p a b", b=D), w2[e, c - 14]

            def expert_load(e, c, sem_, value):
                sp.wait_ge(sem_, value)
                dst, src = expert_chunk(e, c)
                sp.dma_start(dst, src).then_inc(mslot_full[c % MRING], 16)

            def before(c):
                return (m_dn, c - 14) if c >= 14 else ((m_g, m_gu)[c % 2], c // 2)

            for c in (3, 4, 0, 1, 2, 5, 6):
                if c < 3:
                    expert_load(0, c, att["A1"]["pv"], len(plans["A1"]["pvs"]))
                else:
                    expert_load(0, c, *released[PRE - MRING + c])
            for c in range(MRING, MCH):
                sm, k = before(c - MRING)
                expert_load(0, c, sm, k + 1)
            sp.wait_ge(items_rd, 1)
            total = sp.value_load(nit[0:1, 0:1], min_val=NE, max_val=NE * ROUNDS)
            with sp.Fori(1, total) as n:
                e = n % NE
                for c in range(MCH):
                    sm, k = before((c - MRING) % MCH)
                    expert_load(e, c, sm, n * 7 + (k + 1 if c >= MRING else k + 1 - 7))
            sp.wait_ge(m_add, total + 1)
            sp.dma_start(out.rearrange("(k p) n -> p k n", p=P), xT[:, :, 0:S_LAT]).then_inc(s_out, 16)
            sp.wait_ge(s_out, 16)

        @block.gpsimd
        def _(pool):
            ch = Chain(pool, p_step)
            pool.memset(ones[:, :], 1.0).then_inc(s_ones, 1)
            rp = a["rpb"]
            for rr in range(2):
                for h in range(8):
                    off = (h * RPB_DR + 1 - rr) * RPB_ROW + GRID_W - 1
                    pool.dma_start(bt[rr * 64:rr * 64 + 64, h, :, :],
                                   bass.AP(rp.tensor, off, [[2 * GRID_W - 2, 64], [RPB_ROW, 6], [1, 64]])).then_inc(s_bt, 16)
            pool.wait_ge(gain_rd, 1)

            def rotate(nm):
                s = proj[nm]
                for un in units[nm]:
                    if not un["groups"]:
                        continue
                    if un.get("assembled"):
                        pool.wait_ge(s["normed"], un["nth_assembled"])
                    else:
                        pool.wait_ge(s["taken"], un["x"] + 1)
                    for gr in un["groups"]:
                        nh, hd = gr["nh"], gr["hd"]
                        gb = gr["gain"].unsqueeze(1).to_broadcast([P, nh, hd])
                        if gr["rope"] is None:
                            for o in gr["outs"]:
                                ch.after(pool.tensor_tensor(o, gr["dst"], gb, ALU.mult))
                            continue
                        cos, sin, r0, rl = gr["rope"]
                        ch.after(pool.tensor_tensor(gr["dst"], gr["dst"], gb, ALU.mult))
                        q = rl // 4
                        x = gr["dst"][:, :, r0:r0 + rl]
                        va = ra[:, 0:nh * rl].rearrange("p (h d) -> p h d", d=rl)
                        vb = rb[:, 0:nh * rl].rearrange("p (h d) -> p h d", d=rl)
                        pool.tensor_tensor(va, x, cos.unsqueeze(1).to_broadcast([P, nh, rl]), ALU.mult)
                        x4 = x.rearrange("p h (a c q) -> p h a c q", a=2, c=2)
                        b4 = vb.rearrange("p h (a c q) -> p h a c q", a=2, c=2)
                        s4 = sin.rearrange("p (a c q) -> p a c q", a=2, c=2)
                        for c in range(2):
                            for ax in range(2):
                                ins = pool.tensor_tensor(b4[:, :, ax, c, :], x4[:, :, ax, 1 - c, :],
                                                         s4[:, ax, c, :].unsqueeze(1).to_broadcast([P, nh, q]), ALU.mult)
                        ch.after(ins)
                        for o in gr["outs"]:
                            ch.after(pool.tensor_tensor(o[:, :, r0:r0 + rl], va, vb, ALU.add))
                    pool.sem_inc(s["rotated"], 1)

            for nm in ("L0", "L1", "UQ"):
                rotate(nm)

        @block.scalar
        def _(act):
            ch = Chain(act, a_step)
            act.dma_start(cond[:, :], a["cond"]).then_inc(s_cst, 16)
            act.dma_start(adab[:, :, :].rearrange("p a b -> p (a b)"), a["adab"]).then_inc(s_cst, 16)
            act.dma_start(ng[:, :, :, :].rearrange("p a b c -> p (a b c)"), a["ng"]).then_inc(s_cst, 16)
            act.dma_start(cst[:, :], a["cst"]).then_inc(s_cst, 16)
            act.dma_start(vec[:, :], a["vec"].partition_broadcast(P)).then_inc(s_cst, 16)
            act.dma_start(xT[:, :, 0:S_LAT], a["xT"].rearrange("(k p) n -> p k n", p=P)).then_inc(s_x, 16)
            act.dma_start(xT[:, :, S_LAT:S_ALL], a["ctxT"].rearrange("(k p) n -> p k n", p=P)).then_inc(s_x, 16)
            act.dma_start(rtr[:, :, :], a["moe_router"].rearrange("(k p) n -> p k n", p=P)).then_inc(s_cst, 16)
            act.wait_ge(s_cst, 96)
            act.activation(scond[:, :], cond[:, :], ACT.Silu).then_inc(s_scond, 1)
            act.wait_ge(gain_rd, 1)
            act.wait_ge(lam_in, 1)
            act.activation(lamt[:, 2:4], lamt[:, 0:2], ACT.Exp).then_inc(lam_ex, 1)
            act.wait_ge(s_x, 32)

            def norm_act(nm, l, w, nt):
                s = norm[nm]
                for k in range(KT):
                    if k >= 4:
                        act.wait_ge(s["summed"], k - 3)
                    act.activation(sq[k % 4][:, 0:nt], xT[:, k, 0:nt], ACT.Square).then_inc(s["square"], 1)
                act.wait_ge(s["summed"], KT)
                act.activation(rt[:, 0:nt], ps[6][:, 0:nt], ACT.Sqrt, bias=eps[:, 0:1], scale=1.0 / D)\
                   .then_inc(s["root"], 1)
                n = 0
                for c in range(nt // S_LAT):
                    for k in range(KT):
                        n += 1
                        act.wait_ge(s["scaled"], n)
                        hv = hT[:, k, c * S_LAT:(c + 1) * S_LAT]
                        act.activation(hv, hv, ACT.Identity, bias=ada[:, l, 24 * w + k, c:c + 1])\
                           .then_inc(s["ready"], 1)

            def proj_act(nm):
                s = proj[nm]

                def squares(un):
                    v = un["v"]
                    if un.get("assembled"):
                        act.wait_ge(s["taken"], un["x"] + 1)
                    else:
                        act.wait_ge(s["done"], un["x"] + 1)
                    if v >= 2:
                        act.wait_ge(s["reduced"], v - 1)
                    n = un["sq"].shape[1]
                    act.activation(sq[v % 2][:, 0:n], un["sq"], ACT.Square).then_inc(s["squared"], 1)

                def root(un):
                    v = un["v"]
                    act.wait_ge(s["reduced"], v + 1)
                    o = 0
                    for gr in un["groups"]:
                        ins = act.activation(rt8[:, v % 4, o:o + gr["nh"]], ss[:, v % 4, o:o + gr["nh"]], ACT.Sqrt,
                                             bias=eps[:, 0:1], scale=1.0 / gr["hd"])
                        o += gr["nh"]
                    ins.then_inc(s["root"], 1)

                def store(un):
                    v = un["v"]
                    act.wait_ge(s["turned"], v + 1)
                    bank = ps[4 + v % 2]
                    dst, rows = un["store"]
                    n = dst.shape[1]
                    ins = act.activation(dst, bank[0:rows, 0:n * P].rearrange("p (a b) -> p a b", b=P), ACT.Copy)
                    if "store2" in un:
                        d2, n2 = un["store2"]
                        ins = act.activation(d2, bank[:, n * P:(n + n2) * P].rearrange("p (a b) -> p a b", b=P), ACT.Copy)
                    ins.then_inc(s["stored"], 1)

                us = units[nm]
                for x in range(len(us) + 3):
                    if x < len(us) and us[x]["groups"]:
                        squares(us[x])
                        root(us[x])
                    if x >= 3 and us[x - 3]["groups"]:
                        store(us[x - 3])

            def att_act(nm):
                s, pl = att[nm], plans[nm]
                nst = 0
                for i in range(NSTEP[nm]):
                    if i < len(pl["items"]):
                        it = pl["items"][i]
                        act.wait_ge(s["max"], i + 1)
                        if i >= 4:
                            act.wait_ge(s["turned"], pl["items"][i - 4]["pv"] + 1)
                        act.activation(prob[i % 4][:, 0:it["nk"]], ps[i % 2][:, 0:it["nk"]], ACT.Exp,
                                       bias=nmx[:, i % 64:i % 64 + 1], scale=it["scale"],
                                       accum_out=sums[:, i % 64:i % 64 + 1]).then_inc(s["exp"], 1)
                    for j in pv_at(pl, i - 2):
                        nk = pl["pvs"][j]["nk"]
                        act.wait_ge(s["turned"], j + 1)
                        if j >= 2:
                            act.wait_ge(s["pv"], j - 1)
                        act.activation(probT[j % 2][:, 0:nk], ps[2 + j % 2][:, 0:nk], ACT.Copy).then_inc(s["copied"], 1)
                    for gp in closes(pl, i):
                        if gp["sub"]:
                            act.wait_ge(s["out"], gp["pv1"])
                            act.activation(sq[gp["e"] % 2], gp["otok"], ACT.Square).then_inc(s["osq"], 1)
                            act.wait_ge(s["ored"], gp["subs_upto"])
                            act.activation(rt8[:, 0, 0:4], ss[:, 0, 0:4], ACT.Sqrt, bias=eps[:, 0:1], scale=1.0 / P)\
                               .then_inc(s["oroot"], 1)
                    for gp in closes(pl, i - 1):
                        e = gp["e"]
                        act.wait_ge(s["oturned"], e + 1)
                        act.activation(hT[:, 4 * gp["half"]:4 * gp["half"] + 4, gp["t"] * P:(gp["t"] + 1) * P],
                                       ps[6 + e % 2][:, :].rearrange("p (a b) -> p a b", b=P), ACT.Copy)\
                           .then_inc(s["ostored"], 1)

            norm_act("n00", 0, 0, S_ALL)
            proj_act("L0")
            att_act("A0")
            act.wait_ge(outp["O0"]["added"], KT)
            norm_act("n01", 0, 1, S_ALL)
            with act.Fori(0, 5) as i:
                for j in range(4):
                    act.wait_ge(gu_mm, i * 4 + (j + 1))
                    act.activation(sq[j], ps[2 * j][:, :], ACT.Silu).then_inc(silu_rd, 1)
            for j in range(2):
                act.wait_ge(gu_mm, 20 + j + 1)
                act.activation(sq[j], ps[2 * j][:, :], ACT.Silu).then_inc(silu_rd, 1)
            act.wait_ge(dn_add, KT + 4)
            norm_act("n10", 1, 0, S_ALL)
            proj_act("L1")
            proj_act("UQ")
            att_act("A1")
            act.wait_ge(outp["O1"]["added"], KT)
            norm_act("n11", 1, 1, S_LAT)
            for t in range(2):
                for hh in range(2):
                    act.wait_ge(tok_t, 2 * t + hh + 1)
                    act.activation(htok[:, t, hh * 512:(hh + 1) * 512], ps[2 * t + hh][:, :], ACT.Copy).then_inc(tok_rd, 1)
            act.wait_ge(rt_ein, 1)
            act.activation(ro[:, 8, 0, 0:2], ro[:, 7, 0, 0:2], ACT.Exp).then_inc(rt_ex, 1)
            act.wait_ge(items_rd, 1)
            total = act.value_load(nit[0:1, 0:1], min_val=NE, max_val=NE * ROUNDS)
            with act.Fori(0, total) as n:
                for hh in range(2):
                    act.wait_ge(m_gat, n * 2 + (hh + 1))
                    act.activation(xg[:, 4 * hh:4 * hh + 4, :], v3(ps[hh][:, 0:4 * CAP], CAP), ACT.Copy).then_inc(m_xg, 1)
                for j in range(7):
                    act.wait_ge(m_gu, n * 7 + (j + 1))
                    act.activation(sq[j % 4][:, 0:QF * CAP], ps[4 + 2 * (j % 2)][:, 0:QF * CAP], ACT.Silu)\
                       .then_inc(m_silu, 1)
                act.wait_ge(m_dn, n * 7 + 7)
                act.activation(yT[:, 0:4, :], v3(ps[2][:, 0:4 * CAP], CAP), ACT.Copy).then_inc(m_yc, 1)
                act.activation(yT[:, 4:8, :], v3(ps[3][:, 0:4 * CAP], CAP), ACT.Copy).then_inc(m_yc, 1)
                for hh in range(2):
                    act.wait_ge(m_yt, n * 2 + (hh + 1))
                    act.activation(ytok[0:CAP, hh * 512:(hh + 1) * 512], ps[hh][0:CAP, :], ACT.Copy).then_inc(m_ytc, 1)

        @block.vector
        def _(dve):
            ch = Chain(dve, d_step)
            dve.memset(eps[:, :], EPS)
            dve.wait_ge(s_cst, 96)
            for n in ("na_q_g", "diff_q_g", "gqa_q_g"):
                dve.tensor_scalar(vv(n), vv(n), HD ** -0.5, None, ALU.mult)
            dve.tensor_scalar(vv("diff_subln_g"), vv("diff_subln_g"), 1.0 - LAM_INIT, None, ALU.mult).then_inc(gain_rd, 1)
            ch.after(dve.tensor_tensor(sq[0][:, 0:64], vv("diff_lq1"), vv("diff_lk1"), ALU.mult))
            ch.after(dve.tensor_tensor(sq[0][:, 64:128], vv("diff_lq2"), vv("diff_lk2"), ALU.mult))
            dve.tensor_reduce(lamt[:, 0:2], v3(sq[0][:, 0:128], 64), AX.X, ALU.add).then_inc(lam_in, 1)
            dve.wait_ge(s_bt, 16 * 16)
            btv = bt[:, :, :, :].rearrange("p h u c -> p (h u) c")
            ch.after(dve.tensor_tensor(btv, btv, cv("mask").unsqueeze(1).to_broadcast([P, 48, GRID_W]), ALU.add))
            dve.wait_ge(lam_ex, 1)
            ch.after(dve.tensor_tensor(lamt[:, 4:5], lamt[:, 3:4], lamt[:, 2:3], ALU.subtract))
            ch.after(dve.tensor_scalar(lamt[:, 5:6], lamt[:, 4:5], -LAM_INIT, None, ALU.add))

            def ada_take(n, l, m0, m1):
                dve.wait_ge(ada_used, n)
                c0 = 96 * l
                ch.after(dve.tensor_tensor(ada[:, l, m0:m1, :],
                                           ps[7][:, c0 + 2 * m0:c0 + 2 * m1].rearrange("p (m c) -> p m c", c=2),
                                           adab[:, l, m0:m1].unsqueeze(2).to_broadcast([P, m1 - m0, 2]), ALU.add))

            def mod(l, w):
                ch.after(dve.scalar_tensor_tensor(out=amod[:, l, w, :, :], in0=ada[:, l, 24 * w + 8:24 * w + 16, :],
                                                  scalar=1.0, in1=ng[:, w, l, :].unsqueeze(2).to_broadcast([P, KT, 2]),
                                                  op0=ALU.add, op1=ALU.mult))

            def norm_dve(nm, l, w, nt):
                s = norm[nm]
                dve.wait_ge(s["root"], 1)
                ch.after(dve.reciprocal(rstd[:, 0:nt], rt[:, 0:nt]))
                for c in range(nt // S_LAT):
                    for k in range(KT):
                        tc = slice(c * S_LAT, (c + 1) * S_LAT)
                        dve.scalar_tensor_tensor(out=hT[:, k, tc], in0=xT[:, k, tc], scalar=amod[:, l, w, k, c:c + 1],
                                                 in1=rstd[:, tc], op0=ALU.mult, op1=ALU.mult).then_inc(s["scaled"], 1)

            def proj_dve(nm):
                s, us = proj[nm], units[nm]

                def first(x, un):
                    if un["copies"]:
                        if un["groups"] and not un.get("assembled"):
                            dve.wait_ge(s["squared"], un["v"] + 1)
                        else:
                            dve.wait_ge(s["done"], x + 1)
                        for d, sr in un["copies"]:
                            ins = dve.tensor_copy(d, sr)
                        if un.get("assembled") or not un["groups"]:
                            ins.then_inc(s["taken"], 1)
                    if un["groups"]:
                        v = un["v"]
                        dve.wait_ge(s["squared"], v + 1)
                        o = 0
                        for gr in un["groups"]:
                            lo, hi = gr["sq"]
                            ins = dve.tensor_reduce(ss[:, v % 4, o:o + gr["nh"]],
                                                    sq[v % 2][:, lo:hi].rearrange("p (h d) -> p h d", d=gr["hd"]),
                                                    AX.X, ALU.add)
                            o += gr["nh"]
                        ins.then_inc(s["reduced"], 1)

                def second(un):
                    v = un["v"]
                    dve.wait_ge(s["root"], v + 1)
                    nh = sum(gr["nh"] for gr in un["groups"])
                    ch.after(dve.reciprocal(rs8[:, v % 4, 0:nh], rt8[:, v % 4, 0:nh]))
                    if v >= 3:
                        dve.wait_ge(s["turned"], v - 2)
                    o = 0
                    for gr in un["groups"]:
                        ins = dve.tensor_tensor(gr["dst"], gr["src"],
                                                rs8[:, v % 4, o:o + gr["nh"]].unsqueeze(2)
                                                .to_broadcast([P, gr["nh"], gr["hd"]]), ALU.mult)
                        o += gr["nh"]
                    ins.then_inc(s["normed" if un.get("assembled") else "taken"], 1)

                pend = None
                for x, un in enumerate(us):
                    if pend is not None:
                        second(pend)
                        pend = None
                    first(x, un)
                    if un["groups"]:
                        pend = un
                if pend is not None:
                    second(pend)

            def att_dve(nm):
                s, pl = att[nm], plans[nm]
                nsub = 0
                for i in range(NSTEP[nm]):
                    if i < len(pl["items"]):
                        it = pl["items"][i]
                        c = i % 64
                        bank = ps[i % 2]
                        dve.wait_ge(s["score"], i + 1)
                        if it["bias"] is not None:
                            b3 = bank[:, 0:S_LAT].rearrange("p (r c) -> p r c", c=GRID_W)
                            ch.after(dve.tensor_tensor(b3, b3, it["bias"], ALU.add))
                        ch.after(dve.reduce_max(mx[:, c:c + 1], bank[:, 0:it["nk"]], AX.X))
                        dve.tensor_scalar(nmx[:, c:c + 1], mx[:, c:c + 1], -it["scale"], None, ALU.mult)\
                           .then_inc(s["max"], 1)
                    if 1 <= i <= len(pl["items"]):
                        q = i - 1
                        c = q % 64
                        dve.wait_ge(s["exp"], q + 1)
                        ch.after(dve.reciprocal(rsum[:, c:c + 1], sums[:, c:c + 1]))
                        for j in pv_at(pl, q):
                            pv = pl["pvs"][j]
                            if len(pv["items"]) == 2:
                                c0 = pv["items"][0] % 64
                                p0 = prob[pv["items"][0] % 4][:, 0:pv["nk"]]
                                p1 = prob[q % 4][:, 0:pv["nk"]]
                                dve.tensor_scalar(p0, p0, rsum[:, c0:c0 + 1], None, ALU.mult)
                                ch.after(dve.tensor_tensor(rsum[:, c:c + 1], rsum[:, c:c + 1], lamt[:, 5:6], ALU.mult))
                                dve.scalar_tensor_tensor(out=p1, in0=p1, scalar=rsum[:, c:c + 1], in1=p0,
                                                         op0=ALU.mult, op1=ALU.add).then_inc(s["mixed"], 1)
                    for j in pv_at(pl, i - 4):
                        pv = pl["pvs"][j]
                        o = ps[pv["ob"]][:, 0:pv["dv"]]
                        dve.wait_ge(s["pv"], j + 1)
                        if len(pv["items"]) == 2:
                            dve.tensor_copy(pv["dst"], o).then_inc(s["out"], 1)
                        else:
                            c = pv["items"][0] % 64
                            dve.tensor_scalar(pv["dst"], o, rsum[:, c:c + 1], None, ALU.mult).then_inc(s["out"], 1)
                    for gp in closes(pl, i):
                        if gp["sub"]:
                            nsub += 1
                            dve.wait_ge(s["osq"], nsub)
                            dve.tensor_reduce(ss[:, 0, 0:4], v3(sq[gp["e"] % 2], P), AX.X, ALU.add).then_inc(s["ored"], 1)
                            dve.wait_ge(s["oroot"], nsub)
                            ch.after(dve.reciprocal(rs8[:, 0, 0:4], rt8[:, 0, 0:4]))
                            o3 = v3(gp["otok"], P)
                            ch.after(dve.tensor_tensor(o3, o3,
                                                       rs8[:, 0, 0:4].unsqueeze(2).to_broadcast([P, 4, P]), ALU.mult))
                            dve.tensor_tensor(o3, o3, vv("diff_subln_g").unsqueeze(1).to_broadcast([P, 4, P]),
                                              ALU.mult).then_inc(s["otok"], 1)

            def out_dve(nm, l, nc_):
                s = outp[nm]
                for d in range(KT):
                    dve.wait_ge(s["done"], d + 1)
                    for c in range(nc_):
                        tc = slice(c * S_LAT, (c + 1) * S_LAT)
                        ins = dve.scalar_tensor_tensor(out=xT[:, d, tc], in0=ps[d % 4][:, tc],
                                                       scalar=ada[:, l, 16 + d, c:c + 1], in1=xT[:, d, tc],
                                                       op0=ALU.mult, op1=ALU.add)
                    ins.then_inc(s["added"], 1)

            ada_take(4, 0, 0, 16)
            mod(0, 0)
            norm_dve("n00", 0, 0, S_ALL)
            proj_dve("L0")
            ada_take(12, 0, 16, 48)
            mod(0, 1)
            att_dve("A0")
            out_dve("O0", 0, 2)
            norm_dve("n01", 0, 1, S_ALL)
            dve.sem_inc(hid_rd, 4)
            with dve.Fori(0, 5) as i:
                for j in range(4):
                    dve.wait_ge(silu_rd, i * 4 + (j + 1))
                    hv = hid.rearrange("p f n -> p (f n)")[:, bass.ds(i * (4 * S_ALL) + j * S_ALL, S_ALL)]
                    dve.tensor_tensor(hv, sq[j], ps[2 * j + 1][:, :], ALU.mult).then_inc(hid_rd, 1)
            for j in range(2):
                dve.wait_ge(silu_rd, 20 + j + 1)
                dve.tensor_tensor(hid[:, 20 + j, :], sq[j], ps[2 * j + 1][:, :], ALU.mult).then_inc(hid_rd, 1)
            dve.sem_inc(dn_add, 4)
            with dve.Fori(0, 2) as i:
                for j in range(4):
                    dve.wait_ge(dn_mm, i * 4 + (j + 1))
                    for c in range(2):
                        xv = xT[:, :, :].rearrange("p k n -> p (k n)")[:, bass.ds(i * (4 * S_ALL) + (j * S_ALL + c * S_LAT), S_LAT)]
                        gv = ada[:, 0, :, :].rearrange("p m c -> p (m c)")[:, bass.ds(i * 8 + (2 * (40 + j) + c), 1)]
                        ins = dve.scalar_tensor_tensor(out=xv, in0=ps[j][:, c * S_LAT:(c + 1) * S_LAT], scalar=gv,
                                                       in1=xv, op0=ALU.mult, op1=ALU.add)
                    ins.then_inc(dn_add, 1)
            ada_take(24, 1, 0, 48)
            mod(1, 0)
            mod(1, 1)
            norm_dve("n10", 1, 0, S_ALL)
            proj_dve("L1")
            proj_dve("UQ")
            att_dve("A1")
            out_dve("O1", 1, 1)
            norm_dve("n11", 1, 1, S_LAT)

            def R(i):
                return ro[:, i, :, :]

            def B(ap):
                return ap.unsqueeze(2).to_broadcast([P, 2, NE])

            col = [ro[:, 16 + i, 0, 0:2] for i in range(8)]
            rank = cv("rank").unsqueeze(1).to_broadcast([P, 2, NE])
            dve.wait_ge(rt_mm, 1)
            ch.after(dve.tensor_copy(R(0), ps[5][:, 0:2 * NE].rearrange("p (t e) -> p t e", e=NE)))

            def best(src, eq, one, m):
                ch.after(dve.tensor_reduce(m, src, AX.X, ALU.max))
                ch.after(dve.tensor_tensor(eq, src, B(m), ALU.is_equal))
                ch.after(dve.tensor_tensor(eq, eq, rank, ALU.mult))
                ch.after(dve.tensor_reduce(col[7], eq, AX.X, ALU.max))
                ch.after(dve.tensor_tensor(one, eq, B(col[7]), ALU.is_equal))

            best(R(0), R(1), R(2), col[0])
            ch.after(dve.scalar_tensor_tensor(out=R(3), in0=R(2), scalar=-3e38, in1=R(0), op0=ALU.mult, op1=ALU.add))
            best(R(3), R(1), R(4), col[1])
            dve.tensor_tensor(R(5), R(2), R(4), ALU.add).then_inc(rt_sel, 1)
            dve.tensor_tensor(ro[:, 7, 0, 0:2], col[1], col[0], ALU.subtract).then_inc(rt_ein, 1)
            dve.wait_ge(rt_ex, 1)
            ch.after(dve.tensor_scalar(col[2], ro[:, 8, 0, 0:2], 1.0, None, ALU.add))
            ch.after(dve.reciprocal(col[3], col[2]))
            ch.after(dve.tensor_tensor(col[4], col[3], ro[:, 8, 0, 0:2], ALU.mult))
            ch.after(dve.tensor_tensor(R(9), R(2), B(col[3]), ALU.mult))
            ch.after(dve.tensor_tensor(R(10), R(4), B(col[4]), ALU.mult))
            ch.after(dve.tensor_tensor(R(11), R(9), R(10), ALU.add))
            dve.wait_ge(rt_pos, 1)
            for r in range(ROUNDS):
                rs = slice(r * NE, (r + 1) * NE)
                dve.tensor_scalar(posr[:, :, rs], ps[4][:, 0:2 * NE].rearrange("p (t e) -> p t e", e=NE),
                                  -float(r * CAP), None, ALU.add)
                dve.tensor_copy(gat[:, :, rs], R(11))
                dve.tensor_copy(chs[:, :, rs], R(5))
            ch.after(dve.reduce_max(col[5][:, 0:1], ps[4][:, 2 * NE:3 * NE], AX.X))
            ch.after(dve.tensor_scalar(col[5][:, 1:2], col[5][:, 0:1], float(CAP), float(NE), ALU.is_gt, ALU.mult))
            ch.after(dve.tensor_scalar(col[6][:, 0:1], col[5][:, 0:1], 2.0 * CAP, float(NE), ALU.is_gt, ALU.mult))
            ch.after(dve.tensor_tensor(col[6][:, 1:2], col[6][:, 0:1], col[5][:, 1:2], ALU.add))
            dve.tensor_scalar(nit[:, 0:1], col[6][:, 1:2], float(NE), None, ALU.add).then_inc(items_rd, 1)
            dve.wait_ge(items_rd, 1)
            total = dve.value_load(nit[0:1, 0:1], min_val=NE, max_val=NE * ROUNDS)
            pf = posr[:, :, :].rearrange("p t n -> p (t n)")
            gf = gat[:, :, :].rearrange("p t n -> p (t n)")
            cf = chs[:, :, :].rearrange("p t n -> p (t n)")
            dve.sem_inc(m_add, 1)
            with dve.Fori(0, total) as n:
                for t in range(2):
                    pc = pf[:, bass.ds(n + t * NI, 1)]
                    dve.tensor_scalar(sel[t], cv("iota"), pc, cf[:, bass.ds(n + t * NI, 1)], ALU.is_equal, ALU.mult)
                    ins = dve.tensor_scalar(gsel[t], cv("iota"), pc, gf[:, bass.ds(n + t * NI, 1)], ALU.is_equal, ALU.mult)
                ins.then_inc(m_sel, 1)
                dve.wait_ge(m_pgt, n + 1)
                dve.tensor_copy(pgT[0:CAP, :], ps[2][0:CAP, 0:S_LAT]).then_inc(m_pg, 1)
                for j in range(7):
                    dve.wait_ge(m_silu, n * 7 + (j + 1))
                    dve.tensor_tensor(hide[:, QF * j:QF * j + QF, :], v3(sq[j % 4][:, 0:QF * CAP], CAP),
                                      v3(ps[5 + 2 * (j % 2)][:, 0:QF * CAP], CAP), ALU.mult).then_inc(m_hid, 1)
                for d in range(KT):
                    if d % 2 == 0:
                        dve.wait_ge(m_sc, n * 4 + (d // 2 + 1))
                    ins = dve.scalar_tensor_tensor(out=xT[:, d, 0:S_LAT],
                                                   in0=ps[4 + d // 2][:, (d % 2) * S_LAT:(d % 2 + 1) * S_LAT],
                                                   scalar=ada[:, 1, 40 + d, 0:1], in1=xT[:, d, 0:S_LAT],
                                                   op0=ALU.mult, op1=ALU.add)
                ins.then_inc(m_add, 1)

        @block.tensor
        def _(pe):
            def arrived(g, i=None, per=1, times=1):
                pe.wait_ge(slot_full[slot_of(g)], 16 * loads_upto(g) if i is None else i * (16 * times) + 16 * loads_upto(g))

            def dmas(g):
                return 2 if (sF0.first <= g < sF0.first + sF0.n or g == sU1.first) else 1

            def loads_upto(g):
                return sum(dmas(q) for q in range(slot_of(g), g + 1, RING))

            def norm_pe(nm, nt):
                s = norm[nm]
                for k in range(KT):
                    pe.wait_ge(s["square"], k + 1)
                    pe.matmul(ps[6][:, 0:nt], ones[:, :], sq[k % 4][:, 0:nt], start=(k == 0), stop=(k == KT - 1))\
                      .then_inc(s["summed"], 1)

            def ada_chunk(g, l, m, i=None):
                arrived(g, i)
                w = slot3(g, 512)
                for q in range(4):
                    c = 96 * l + 2 * (m + q)
                    o = ps[7][:, c:c + 2] if i is None else ps[7][:, bass.ds(i * 32 + c, 2)]
                    for k in range(KT):
                        ins = pe.matmul(o, w[:, k, q * P:(q + 1) * P], scond[:, 2 * k:2 * k + 2],
                                        start=(k == 0), stop=(k == KT - 1))
                ins.then_inc(ada_used, 1)

            def ada_loop(st, l, m0):
                with pe.Fori(0, st.n // 4) as i:
                    for j in range(4):
                        ada_chunk(st.first + j, l, m0 + 4 * j, i)

            def proj_pe(nm):
                s, us = proj[nm], units[nm]

                def turn(un):
                    v = un["v"]
                    pe.wait_ge(s["rotated"], v + 1)
                    if v >= 2:
                        pe.wait_ge(s["stored"], v - 1)
                    for c, src in enumerate(un["turn"]):
                        w = src.shape[1]
                        ins = pe.transpose(ps[4 + v % 2][0:w, c * P:(c + 1) * P], src, ident)
                    ins.then_inc(s["turned"], 1)

                for x in range(len(us) + LAGT):
                    if x < len(us):
                        un = us[x]
                        if x == 0 or us[x - 1]["g"] != un["g"]:
                            arrived(un["g"])
                        if x >= 4:
                            pe.wait_ge(s["taken"], x - 3)
                        for k in range(len(un["lhs"])):
                            ins = pe.matmul(ps[un["bank"]][:, 0:un["width"]], un["lhs"][k], un["w"][k],
                                            start=(k == 0), stop=(k == len(un["lhs"]) - 1))
                        ins.then_inc(s["done"], 1)
                    if x >= LAGT and us[x - LAGT]["groups"]:
                        turn(us[x - LAGT])

            def att_pe(nm, nproj):
                s, pl = att[nm], plans[nm]
                for i in range(NSTEP[nm]):
                    if i < len(pl["items"]):
                        it = pl["items"][i]
                        if i >= 2:
                            pe.wait_ge(s["exp"], i - 1)
                        pe.matmul(ps[i % 2][:, 0:it["nk"]], it["q"], it["k"], start=True, stop=True)\
                          .then_inc(s["score"], 1)
                    for j in pv_at(pl, i - 3):
                        pv = pl["pvs"][j]
                        pe.wait_ge(s["copied"], j + 1)
                        if j >= 2:
                            pe.wait_ge(s["out"], j - 1)
                        nkt = pv["nk"] // P
                        for c in range(nkt):
                            ins = pe.matmul(ps[pv["ob"]][:, 0:pv["dv"]],
                                            probT[j % 2][:, c * P:(c + 1) * P], pv["v"][c],
                                            start=(c == 0), stop=(c == nkt - 1))
                        ins.then_inc(s["pv"], 1)
                    for j in pv_at(pl, i - 2):
                        pv = pl["pvs"][j]
                        if len(pv["items"]) == 2:
                            pe.wait_ge(s["mixed"], sum(1 for q in pl["pvs"][:j + 1] if len(q["items"]) == 2))
                        else:
                            pe.wait_ge(s["exp"], pv["items"][0] + 1)
                        if j >= 2:
                            pe.wait_ge(s["copied"], j - 1)
                        src = prob[pv["items"][-1] % 4]
                        for c in range(pv["nk"] // P):
                            ins = pe.transpose(ps[2 + j % 2][:, c * P:(c + 1) * P], src[:, c * P:(c + 1) * P], ident)
                        ins.then_inc(s["turned"], 1)
                    for gp in closes(pl, i - 1):
                        e = gp["e"]
                        if gp["sub"]:
                            pe.wait_ge(s["otok"], gp["subs_upto"])
                        else:
                            pe.wait_ge(s["out"], gp["pv1"])
                        if e >= 2:
                            pe.wait_ge(s["ostored"], e - 1)
                        for c in range(4):
                            ins = pe.transpose(ps[6 + e % 2][:, c * P:(c + 1) * P], gp["otok"][:, c * P:(c + 1) * P], ident)
                        ins.then_inc(s["oturned"], 1)

            def out_pe(nm, an, st, nt):
                s = outp[nm]
                pe.wait_ge(att[an]["ostored"], len(plans[an]["groups"]))
                for d in range(KT):
                    g = st.first + d // 4
                    if d % 4 == 0:
                        arrived(g)
                    if d >= 4:
                        pe.wait_ge(s["added"], d - 3)
                    w = slot3(g, 512)
                    for k in range(KT):
                        ins = pe.matmul(ps[d % 4][:, 0:nt], w[:, k, (d % 4) * P:(d % 4 + 1) * P], hT[:, k, 0:nt],
                                        start=(k == 0), stop=(k == KT - 1))
                    ins.then_inc(s["done"], 1)

            pe.wait_ge(s_ones, 1)
            norm_pe("n00", S_ALL)
            pe.wait_ge(s_scond, 1)
            for j in range(4):
                ada_chunk(sA0a.first + j, 0, 4 * j)
            pe.wait_ge(norm["n00"]["ready"], 2 * KT)
            pe.wait_ge(s_cst, 96)
            proj_pe("L0")
            ada_loop(sA0b, 0, 16)
            pe.wait_ge(proj["L0"]["stored"], NV["L0"])
            pe.wait_ge(proj["L0"]["taken"], len(units["L0"]))
            att_pe("A0", "L0")
            out_pe("O0", "A0", sO0, S_ALL)
            norm_pe("n01", S_ALL)
            pe.wait_ge(norm["n01"]["ready"], 2 * KT)

            def gate_up(g, j, i=None):
                arrived(g, i, times=2)
                w = slot3(g, 256)
                for q in range(2):
                    f = 2 * j + q
                    b = 2 * (f % 4)
                    pe.wait_ge(hid_rd, f + 1 if i is None else i * 8 + (f + 1))
                    for part in range(2):
                        for k in range(KT):
                            ins = pe.matmul(ps[b + part][:, :], w[:, part * KT + k, q * P:(q + 1) * P], hT[:, k, :],
                                            start=(k == 0), stop=(k == KT - 1))
                    ins.then_inc(gu_mm, 1)

            with pe.Fori(0, 2) as i:
                for j in range(4):
                    gate_up(sF0.first + j, j, i)
            for j in range(8, 11):
                gate_up(sF0.first + j, j)
            pe.wait_ge(hid_rd, FT + 4)
            with pe.Fori(0, 2) as i:
                for j in range(4):
                    g = sD0.first + j
                    arrived(g, i)
                    w = ring[:, slot_of(g), 0:11 * 256].rearrange("p (f n) -> p f n", n=256)
                    for q in range(2):
                        d = 2 * (j // 2) + q
                        if j % 2 == 0:
                            pe.wait_ge(dn_add, i * 4 + (d + 1))
                        for f in range(11):
                            ins = pe.matmul(ps[d][:, :], w[:, f, q * P:(q + 1) * P], hid[:, 11 * (j % 2) + f, :],
                                            start=(j % 2 == 0 and f == 0), stop=(j % 2 == 1 and f == 10))
                        if j % 2 == 1:
                            ins.then_inc(dn_mm, 1)
                    if j % 2 == 0:
                        ins.then_inc(dn_half, 1)

            ada_loop(sA1, 1, 0)
            norm_pe("n10", S_ALL)
            pe.wait_ge(norm["n10"]["ready"], 2 * KT)
            proj_pe("L1")
            pe.wait_ge(proj["L1"]["stored"], NV["L1"])
            pe.wait_ge(proj["L1"]["taken"], len(units["L1"]))
            proj_pe("UQ")
            pe.wait_ge(proj["UQ"]["stored"], NV["UQ"])
            pe.wait_ge(proj["UQ"]["taken"], len(units["UQ"]))
            att_pe("A1", "UQ")
            out_pe("O1", "A1", sO1, S_LAT)
            norm_pe("n11", S_LAT)
            pe.wait_ge(norm["n11"]["ready"], KT)
            for t in range(2):
                for k in range(KT):
                    pe.matmul(ps[5][:, t * NE:(t + 1) * NE], hT[:, k, t * P:(t + 1) * P], rtr[:, k, :],
                              start=(k == 0), stop=(k == KT - 1)) if not (t == 1 and k == KT - 1) else \
                        pe.matmul(ps[5][:, t * NE:(t + 1) * NE], hT[:, k, t * P:(t + 1) * P], rtr[:, k, :],
                                  start=False, stop=True).then_inc(rt_mm, 1)
            for t in range(2):
                for hh in range(2):
                    for q in range(4):
                        ins = pe.transpose(ps[2 * t + hh][:, q * P:(q + 1) * P],
                                           hT[:, 4 * hh + q, t * P:(t + 1) * P], ident)
                    ins.then_inc(tok_t, 1)
            pe.wait_ge(rt_sel, 1)
            up = cv("upper")
            ch0, ch1 = ro[:, 5, 0, :], ro[:, 5, 1, :]
            pe.matmul(ps[4][:, 0:NE], up, ch0, start=True, stop=True)
            pe.matmul(ps[4][:, NE:2 * NE], ones[:, :], ch0, start=True, stop=False)
            pe.matmul(ps[4][:, NE:2 * NE], up, ch1, start=False, stop=True)
            pe.matmul(ps[4][:, 2 * NE:3 * NE], ones[:, :], ch0, start=True, stop=False)
            pe.matmul(ps[4][:, 2 * NE:3 * NE], ones[:, :], ch1, start=False, stop=True).then_inc(rt_pos, 1)
            pe.wait_ge(tok_rd, 4)
            pe.wait_ge(items_rd, 1)
            total = pe.value_load(nit[0:1, 0:1], min_val=NE, max_val=NE * ROUNDS)
            with pe.Fori(0, total) as n:
                pe.wait_ge(m_sel, n + 1)
                for hh in range(2):
                    for q in range(4):
                        d = 4 * hh + q
                        for t in range(2):
                            ins = pe.matmul(ps[hh][:, q * CAP:(q + 1) * CAP], htok[:, t, d * P:(d + 1) * P], sel[t],
                                            start=(t == 0), stop=(t == 1))
                    ins.then_inc(m_gat, 1)
                for t in range(2):
                    ins = pe.transpose(ps[2][0:CAP, t * P:(t + 1) * P], gsel[t], ident)
                ins.then_inc(m_pgt, 1)
                pe.wait_ge(m_add, n + 1)
                pe.wait_ge(m_xg, n * 2 + 2)
                for j in range(7):
                    if j >= 2:
                        pe.wait_ge(m_hid, n * 7 + (j - 1))
                    for part in range(2):
                        c = 2 * j + part
                        pe.wait_ge(mslot_full[c % MRING], n * 48 + 16 * (c // MRING + 1))
                        w = v3(mslot[c % MRING], QF * P)
                        for q in range(QF):
                            for k in range(KT):
                                ins = pe.matmul(ps[4 + 2 * (j % 2) + part][:, q * CAP:(q + 1) * CAP],
                                                w[:, k, q * P:(q + 1) * P], xg[:, k, :],
                                                start=(k == 0), stop=(k == KT - 1))
                        ins.then_inc((m_g, m_gu)[part], 1)
                pe.wait_ge(m_pg, n + 1)
                for j in range(7):
                    c = 14 + j
                    pe.wait_ge(m_hid, n * 7 + (j + 1))
                    pe.wait_ge(mslot_full[c % MRING], n * 48 + 16 * (c // MRING + 1))
                    w = v3(mslot[c % MRING], D)
                    for q in range(QF):
                        f = QF * j + q
                        for d in range(KT):
                            ins = pe.matmul(ps[2 + d // 4][:, (d % 4) * CAP:(d % 4 + 1) * CAP],
                                            w[:, q, d * P:(d + 1) * P], hide[:, f, :],
                                            start=(f == 0 and d % 4 == 0), stop=(f == FTE - 1),
                                            skip_group_check=True)
                    ins.then_inc(m_dn, 1)
                for hh in range(2):
                    pe.wait_ge(m_yc, n * 2 + (hh + 1))
                    for q in range(4):
                        ins = pe.transpose(ps[hh][0:CAP, q * P:(q + 1) * P], yT[:, 4 * hh + q, :], ident)
                    ins.then_inc(m_yt, 1)
                for d in range(KT):
                    if d % 4 == 0:
                        pe.wait_ge(m_ytc, n * 2 + (d // 4 + 1))
                    ins = pe.matmul(ps[4 + d // 2][:, (d % 2) * S_LAT:(d % 2 + 1) * S_LAT],
                                    ytok[0:CAP, d * P:(d + 1) * P], pgT[0:CAP, :], start=True, stop=True)
                    if d % 2 == 1:
                        ins.then_inc(m_sc, 1)


def kernel(**inputs):
    import concourse.bacc as _bacc
    from concourse.bass_utils import run_bass_kernel_spmd as _run

    x = {k: np.asarray(v) for k, v in inputs.items()}

    def tiles(v):
        v = v.reshape(v.shape[:-1] + (v.shape[-1] // P, P))
        return np.moveaxis(v, -1, 0)

    rpb = np.zeros((8, RPB_DR, 2 * GRID_W - 1), np.float32)
    lo = GRID_W - NA_WIN_W
    rpb[:, :, lo:lo + 2 * NA_WIN_W - 1] = x["na_rpb"][0][:, NA_WIN_H - 4:NA_WIN_H + 3]
    rpb = np.tile(rpb, (1, 1, GRID_W))
    arrays = {
        "xT": x["x"][0].T, "ctxT": x["ctx"][0].T,
        "cond": tiles(np.stack([x["c"][0], x["c_ctx"]])).transpose(0, 2, 1).reshape(P, 16),
        "adab": tiles(x["ada_b"]).reshape(P, 96),
        "ng": tiles(np.stack([x["norm1_g"], x["norm2_g"]])).reshape(P, 32),
        "vec": np.concatenate([x[n].reshape(-1) for n, _ in VEC]),
        "cst": shape_constants(), "rpb": rpb,
        "ada_w": x["ada_w"], "moe_router": x["moe_router"][0],
    }
    for n in ("ev_w_in", "ev_w_out", "ffn_w_gate", "ffn_w_up", "ffn_w_down", "od_w_in", "od_w_out",
              "mla_w_uq", "mla_w_ukv", "moe_w1", "moe_w3", "moe_w2"):
        arrays[n] = x[n][0]
    nc = _bacc.Bacc("TRN2", target_bir_lowering=False, num_devices=1)
    feed, aps = {}, {}
    for n, v in arrays.items():
        v = np.ascontiguousarray(v)
        feed[f"in_{n}"] = v
        aps[n] = nc.dram_tensor(f"in_{n}", v.shape, F32, kind="ExternalInput").ap()
    o = nc.dram_tensor("out_T", (D, S_LAT), F32, kind="ExternalOutput").ap()
    build_kernel(nc, aps, o)
    r = _run(nc, [feed], core_ids=[0])
    return np.ascontiguousarray(r.results[0]["out_T"].T)[None]
```

```python
import math
from contextlib import ExitStack

import numpy as np

import concourse.bass as bass
from concourse import mybir

F32 = mybir.dt.float32
F32R = mybir.dt.float32r
I32 = mybir.dt.int32
ALU = mybir.AluOpType
ACT = mybir.ActivationFunctionType
AX = mybir.AxisListType

P = 128
D = 1024
KT = D // P
S_LAT = 256
S_ALL = 512
GRID_W = 64
HD = 64
NA_WIN_W = 16
NA_WIN_H = 8
ROPE_THETA = 10000.0
EPS = 1e-6
NEG = -1e30
D_FF = 2816
FT = D_FF // P
D_FFE = 3584
FTE = D_FFE // P
NE = 8
MLA_QK, MLA_NOPE, MLA_ROPE = 96, 64, 32
RPB_DR = 7
RPB_ROW = (2 * GRID_W - 1) * GRID_W
CAP = 128
ROUNDS = -(-S_LAT // CAP)
LAM_INIT = 0.8 - 0.6 * math.exp(-0.3 * 0)

RING = 4
SLOT = 4096
MRING = 3
UNIT = SLOT // 2
NU = 42
URING = 3
MCH = 21
QF = 4

VEC = [("na_q_g", 64), ("na_k_g", 64), ("diff_q_g", 64), ("diff_k_g", 64), ("gqa_q_g", 64),
       ("gqa_k_g", 64), ("mla_cq_g", 256), ("mla_ckv_g", 128), ("mla_q_g", 96), ("mla_k_g", 96),
       ("diff_subln_g", 128), ("diff_lq1", 64), ("diff_lk1", 64), ("diff_lq2", 64), ("diff_lk2", 64)]
VEC_AT = {}
_o = 0
for _n, _w in VEC:
    VEC_AT[_n] = (_o, _w)
    _o += _w
VEC_N = _o

CST = [("ident", 128), ("upper", 128), ("iota", CAP), ("rope64", 256), ("rope32", 128),
       ("mask", 64), ("rank", 8)]
CST_AT = {}
_o = 0
for _n, _w in CST:
    CST_AT[_n] = (_o, _w)
    _o += _w
CST_N = _o


def rope_table(dim, tile):
    pos = np.arange(tile * P, tile * P + P)
    half = dim // 4
    freqs = (ROPE_THETA ** (-np.arange(half, dtype=np.float32) / half)).astype(np.float32)
    cos, sin = [], []
    for p in (pos // GRID_W, pos % GRID_W):
        ang = (p.astype(np.float32)[:, None] * freqs[None, :]).astype(np.float32)
        c, s = np.cos(ang), np.sin(ang)
        cos += [c, c]
        sin += [-s, s]
    return np.concatenate(cos + sin, axis=1).astype(np.float32)


def shape_constants():
    c = np.zeros((P, CST_N), np.float32)

    def put(name, a):
        o, w = CST_AT[name]
        c[:, o:o + w] = a

    i = np.arange(P)
    put("ident", np.eye(P))
    put("upper", (i[:, None] < i[None, :]))
    put("iota", np.broadcast_to(np.arange(CAP), (P, CAP)))
    put("rope64", np.concatenate([rope_table(64, 0), rope_table(64, 1)], axis=1))
    put("rope32", np.concatenate([rope_table(32, 0), rope_table(32, 1)], axis=1))
    col = np.arange(GRID_W)
    c0 = np.clip(col - NA_WIN_W // 2, 0, GRID_W - NA_WIN_W)
    inside = (col[None, :] >= c0[:, None]) & (col[None, :] < c0[:, None] + NA_WIN_W)
    put("mask", np.tile(np.where(inside, 0.0, NEG), (2, 1)))
    put("rank", np.broadcast_to(NE - np.arange(NE), (P, NE)))
    return c


class Chain:

    def __init__(self, eng, sem, reg=None, per=0):
        self.eng, self.sem, self.reg, self.per, self.n = eng, sem, reg, per, 0

    def after(self, ins):
        ins.then_inc(self.sem, 1)
        self.n += 1
        self.eng.wait_ge(self.sem, self.n if self.reg is None else self.reg * self.per + self.n)


def build_kernel(nc, a, out):
    with ExitStack() as ctx:
        def sb(name, shape, dt=F32):
            return ctx.enter_context(nc.sbuf_tensor(name, shape, dt))

        def sem(name):
            return ctx.enter_context(nc.semaphore(name))

        xT = sb("xT", [P, KT, S_ALL])
        cst = sb("cst", [P, CST_N])
        vec = sb("vec", [P, VEC_N])
        bt = sb("bt", [P, 8, 6, GRID_W])
        ones = sb("ones", [P, P])
        cond = sb("cond", [P, 16])
        scond = sb("scond", [P, 16])
        adab = sb("adab", [P, 2, 48])
        ng = sb("ng", [P, 2, 2, KT])
        ada = sb("ada", [P, 2, 48, 2])
        amod = sb("amod", [P, 2, 2, KT, 2])
        ss = sb("ss", [P, 4, 8])
        rt8 = sb("rt8", [P, 4, 8])
        rs8 = sb("rs8", [P, 4, 8])
        krt = sb("krt", [P, 4, 32])
        eps = sb("eps", [P, 1])
        mx = sb("mx", [P, 64])
        nmx = sb("nmx", [P, 64])
        sums = sb("sums", [P, 64])
        rsum = sb("rsum", [P, 64])
        lamt = sb("lamt", [P, 8])
        rtr = sb("rtr", [P, KT, NE])
        nit = sb("nit", [P, 1], I32)
        ring012 = sb("ring", [P, RING - 1, SLOT])
        with ExitStack() as early:
            ring3 = early.enter_context(nc.sbuf_tensor("ring3", [P, SLOT], F32))
            work = early.enter_context(nc.sbuf_tensor("work", [P, 16384], F32))
            hT = early.enter_context(nc.sbuf_tensor("hT", [P, KT, S_ALL], F32))
            scr = early.enter_context(nc.sbuf_tensor("scr", [P, 11, 512], F32))
        whi = sb("whi", [P, URING, UNIT], F32R)
        wlo = sb("wlo", [P, URING, UNIT], F32R)
        hidr = sb("hidr", [P, 2, FTE, CAP], F32R)
        xgr = sb("xgr", [P, 2, KT, CAP], F32R)
        ytok = sb("ytok", [P, D])
        pgT = sb("pgT", [P, S_LAT])
        hidtok = sb("hidtok", [P, 2, QF * P])
        sg = sb("sg", [P, 2, QF * P])
        sel = sb("sel", [P, 2, CAP])
        gsel = sb("gsel", [P, 2, CAP])
        ps = [ctx.enter_context(nc.psum_tensor(f"ps{b}", [P, 512], F32)) for b in range(8)]

        def cv(name, lo=0, hi=None):
            o, w = CST_AT[name]
            return cst[:, o + lo:o + (w if hi is None else hi)]

        def vv(name):
            o, w = VEC_AT[name]
            return vec[:, o:o + w]

        ident = cv("ident")

        def rope_of(dim, tile):
            o = tile * 2 * dim
            n = "rope64" if dim == 64 else "rope32"
            return cv(n, o, o + dim), cv(n, o + dim, o + 2 * dim)

        def area(o, *dims):
            n = int(np.prod(dims))
            v = work[:, o:o + n]
            if len(dims) == 2:
                v = v.rearrange("p (a b) -> p a b", b=dims[1])
            if len(dims) == 3:
                v = v.rearrange("p (a b c) -> p a b c", b=dims[1], c=dims[2])
            return v

        QT0 = [area(2048 * j, 4, S_ALL) for j in range(4)]
        V0 = area(8192, 4, 1024)
        O0 = area(12288, 4, 1024)
        hid = area(0, FT, S_ALL)
        QcT = area(0, 4, S_LAT)
        KcT = area(1024, 2, S_ALL)
        QdT = area(2048, 8, S_LAT)
        KdT = area(4096, 8, S_ALL)
        Vc = area(8192, 4, 128)
        Vd = area(8704, 4, 512)
        cqT = area(10752, 2, S_LAT)
        ckvT = area(11264, 1, S_ALL)[:, 0, :]
        O1 = area(12288, 2, 1024)
        btf = bt[:, :, :, :].rearrange("p a b c -> p (a b c)")
        htok = btf[:, 0:2 * D].rearrange("p (a b) -> p a b", b=D)
        NI = ROUNDS * NE + 1

        def tail(o, *dims):
            n = int(np.prod(dims))
            v = btf[:, 2 * D + o:2 * D + o + n]
            if len(dims) == 2:
                return v.rearrange("p (a b) -> p a b", b=dims[1])
            return v.rearrange("p (a b c) -> p a b c", b=dims[1], c=dims[2])

        ro = tail(0, 24, 2, NE)
        posr = tail(384, 2, NI)
        gat = tail(384 + 2 * NI, 2, NI)
        chs = tail(384 + 4 * NI, 2, NI)
        kn = tail(384 + 6 * NI, 3, P)
        mslot = [ring012[:, i, :] for i in (1, 2, 0)]

        sq = [scr[:, i, :] for i in range(4)]
        rt, rstd = scr[:, 4, :], scr[:, 5, :]
        tn = [scr[:, 6 + i, :] for i in range(3)]
        adar = scr[:, 6:8, :]
        ra, rb = scr[:, 9, :], scr[:, 10, :]
        prob = [scr[:, 2 + i, :] for i in range(4)]
        probT = [scr[:, 9 + i, :] for i in range(2)]
        kda = [scr[:, 2 + i, 0:384].rearrange("p (h d) -> p h d", d=MLA_QK) for i in range(2)]

        class Stage:
            at = 0

            def __init__(self, n):
                self.first, self.n = Stage.at, n
                Stage.at += n

        sA0a, sW0, sA0b, sO0, sF0, sD0, sA1, sW1, sU1, sO1 = (
            Stage(n) for n in (4, 6, 8, 2, 11, 8, 12, 3, 1, 2))
        PRE = Stage.at

        def slot_of(g):
            return g % RING

        def rslot(g):
            return ring3[:, :] if slot_of(g) == RING - 1 else ring012[:, slot_of(g), :]

        def slot3(g, w):
            return rslot(g).rearrange("p (a b) -> p a b", b=w)

        s_x = sem("x_loaded")
        s_cst = sem("constants_loaded")
        s_bt = sem("bias_loaded")
        s_ones = sem("ones_set")
        slot_full = [sem(f"slot_full{i}") for i in range(RING)]
        ada_used = sem("modulation_chunks_used")
        ada_row = sem("modulation_rows_copied")
        ada_tr = sem("modulation_rows_turned")
        ada_rd = sem("modulation_turns_taken")
        mslot_full = [sem(f"expert_slot_full{i}") for i in range(MRING)]
        s_scond = sem("silu_cond_ready")
        d_step = sem("dve_step")
        p_step = sem("pool_step")
        a_step = sem("act_step")
        gain_rd = sem("gains_prepared")
        lam_in = sem("lambda_dots_ready")
        lam_ex = sem("lambda_exps_ready")
        norm = {}
        for nm in ("n00", "n01", "n10", "n11"):
            norm[nm] = {k: sem(f"{nm}_{k}") for k in ("square", "summed", "root", "scaled", "ready")}
        proj = {}
        for nm in ("L0", "L1", "UQ"):
            proj[nm] = {k: sem(f"proj{nm}_{k}") for k in
                        ("done", "squared", "reduced", "root", "taken", "normed", "rotated", "turned", "stored")}
        att = {}
        for nm in ("A0", "A1"):
            att[nm] = {k: sem(f"att{nm}_{k}") for k in
                       ("score", "max", "exp", "mixed", "turned", "copied", "pv", "out", "osq", "ored",
                        "oroot", "otok", "oturned", "ostored")}
        outp = {}
        for nm in ("O0", "O1"):
            outp[nm] = {k: sem(f"out{nm}_{k}") for k in ("done", "added")}
        gu_mm = sem("ffn_gate_up_done")
        silu_rd = sem("ffn_silu_ready")
        hid_rd = sem("ffn_hidden_ready")
        dn_mm = sem("ffn_down_done")
        dn_half = sem("ffn_down_first_halves_done")
        dn_add = sem("ffn_down_added")
        tok_t = sem("expert_tokens_turned")
        tok_rd = sem("expert_tokens_ready")
        rt_mm = sem("router_logits_done")
        rt_sel = sem("router_choice_ready")
        rt_ein = sem("router_exp_in")
        rt_ex = sem("router_exp_ready")
        rt_pos = sem("router_positions_done")
        items_rd = sem("item_count_ready")
        m_init = sem("expert_buffers_cleared")
        m_sel = sem("expert_select_ready")
        m_gat = sem("expert_gathered")
        m_xh = sem("expert_tokens_high_ready")
        m_xl = sem("expert_tokens_low_ready")
        m_gsel = sem("expert_gates_ready")
        m_pgt = sem("expert_gates_turned")
        m_pg = sem("expert_gates_copied")
        m_hi = sem("unit_high_ready")
        m_lo = sem("unit_low_ready")
        m_pe = sem("unit_used")
        m_silu = sem("expert_silu_ready")
        m_mul = sem("expert_hidden_ready")
        m_t = sem("expert_hidden_turned")
        m_hh = sem("expert_hidden_high_ready")
        m_hl = sem("expert_hidden_low_ready")
        m_ya = sem("expert_sum_copied_by_act")
        m_yb = sem("expert_sum_copied_by_dve")
        m_sc = sem("expert_scattered")
        m_add = sem("expert_added")
        s_out = sem("output_stored")

        released = {}
        for st, n0 in ((sA0a, 0), (sA0b, 4), (sA1, 12)):
            for j in range(st.n):
                released[st.first + j] = (ada_used, n0 + j + 1)
        for j in range(6):
            released[sW0.first + j] = (proj["L0"]["done"], 4 * j + 4)
        for j, n in enumerate((2, 6, 10)):
            released[sW1.first + j] = (proj["L1"]["done"], n)
        released[sU1.first] = (proj["UQ"]["done"], 12)
        for st, nm in ((sO0, "O0"), (sO1, "O1")):
            for j in range(2):
                released[st.first + j] = (outp[nm]["done"], 4 * j + 4)
        for j in range(sF0.n):
            released[sF0.first + j] = (gu_mm, 2 * j + 2)
        for j in range(sD0.n):
            released[sD0.first + j] = (dn_mm, j + 1) if j % 2 else (dn_half, j // 2 + 1)

        def head_unit(kind, g, t, lhs, w, width, bank, **kw):
            return dict(kind=kind, g=g, t=t, lhs=lhs, w=w, width=width, bank=bank, **kw)

        def v3(ap, b):
            return ap.rearrange("p (a b) -> p a b", b=b)

        units = {"L0": [], "L1": [], "UQ": []}
        nv = 0
        for j in range(6):
            for t in range(4):
                u = len(units["L0"])
                g = sW0.first + j
                un = dict(g=g, lhs=[hT[:, k, t * P:(t + 1) * P] for k in range(KT)],
                          w=[slot3(g, 512)[:, k, :] for k in range(KT)], width=512, bank=u % 4,
                          last=(t == 3), copies=[], groups=[])
                if j in (2, 5):
                    c0 = 0 if j == 2 else 512
                    un["copies"] = [(V0[:, t, c0:c0 + 512], ps[u % 4][:, :])]
                else:
                    q = {0: 0, 1: 1, 3: 2, 4: 3}[j]
                    nm = ("na_q_g", "na_k_g", "diff_q_g", "diff_k_g")[q]
                    tb = tn[nv % 3]
                    un["sq"] = ps[u % 4][:, :]
                    un["groups"] = [dict(src=v3(ps[u % 4][:, :], HD), sq=(0, 512), nh=8, hd=HD, dst=v3(tb, HD),
                                         gain=vv(nm), outs=[v3(tb, HD)],
                                         rope=(rope_of(64, t) + (0, 64)) if (q >= 2 and t < 2) else None)]
                    un["turn"] = [tb[:, c * P:(c + 1) * P] for c in range(4)]
                    un["store"] = (QT0[q][:, :, t * P:(t + 1) * P], P)
                    nv += 1
                units["L0"].append(un)
        nv = 0
        for c, t in [(0, 0), (0, 1)] + [(1, t) for t in range(4)] + [(2, t) for t in range(4)]:
            u = len(units["L1"])
            b = u % 4
            g = sW1.first + c
            tb = tn[nv % 3]
            width = (512, 512 if t < 2 else 256, 160)[c]
            wv = slot3(g, 512) if c < 2 else rslot(g)[:, 0:KT * 160].rearrange("p (a b) -> p a b", b=160)
            un = dict(g=g, lhs=[hT[:, k, t * P:(t + 1) * P] for k in range(KT)],
                      w=[wv[:, k, 0:width] for k in range(KT)], width=width, bank=b,
                      last=(t == (1 if c == 0 else 3)), copies=[], groups=[], sq=ps[b][:, 0:min(width, 512)])
            if c == 0:
                un["groups"] = [dict(src=v3(ps[b][:, :], HD), sq=(0, 512), nh=8, hd=HD, dst=v3(tb, HD),
                                     gain=vv("gqa_q_g"), outs=[v3(tb, HD)], rope=rope_of(64, t) + (0, 64))]
                un["turn"] = [tb[:, i * P:(i + 1) * P] for i in range(4)]
                un["store"] = (QcT[:, :, t * P:(t + 1) * P], P)
            elif c == 1:
                kb = kn[:, nv % 3, :]
                dup = tb[:, 0:256].rearrange("p (v c d) -> p c v d", c=2, d=HD)
                un["copies"] = [(Vc[:, t, :], ps[b][:, 128:256])]
                un["groups"] = [dict(src=v3(ps[b][:, 0:128], HD), sq=(0, 128), nh=2, hd=HD, dst=v3(kb, HD),
                                     gain=vv("gqa_k_g"), outs=[dup[:, 0], dup[:, 1]],
                                     rope=(rope_of(64, t) + (0, 64)) if t < 2 else None)]
                un["turn"] = [tb[:, 0:128], tb[:, 128:256]]
                un["store"] = (KcT[:, :, t * P:(t + 1) * P], P)
                if t < 2:
                    cq = tb[:, 256:512].unsqueeze(1)
                    un["groups"].append(dict(src=ps[b][:, 256:512].unsqueeze(1), sq=(256, 512), nh=1, hd=256,
                                             dst=cq, gain=vv("mla_cq_g"), outs=[cq], rope=None))
                    un["turn"] += [tb[:, 256:384], tb[:, 384:512]]
                    un["store2"] = (cqT[:, :, t * P:(t + 1) * P], 2)
            else:
                ck = tb[:, 0:128].unsqueeze(1)
                un["copies"] = [(krt[:, t, :], ps[b][:, 128:160])]
                un["groups"] = [dict(src=ps[b][:, 0:128].unsqueeze(1), sq=(0, 128), nh=1, hd=128, dst=ck,
                                     gain=vv("mla_ckv_g"), outs=[ck], rope=None)]
                un["turn"] = [tb[:, 0:128]]
                un["store"] = (ckvT[:, t * P:(t + 1) * P].unsqueeze(1), P)
            units["L1"].append(un)
            nv += 1
        nv = 0
        uqw = rslot(sU1.first)[:, 0:1536].rearrange("p (k n) -> p k n", k=2)
        ukvw = rslot(sU1.first)[:, 1536:2560]
        for t in range(2):
            for hh in range(2):
                u = len(units["UQ"])
                b = u % 4
                tb = tn[nv % 3][:, 0:384].rearrange("p (h d) -> p h d", d=MLA_QK)
                units["UQ"].append(dict(
                    g=sU1.first, lhs=[cqT[:, k, t * P:(t + 1) * P] for k in range(2)],
                    w=[uqw[:, k, hh * 384:(hh + 1) * 384] for k in range(2)], width=384, bank=b, last=False,
                    copies=[], sq=ps[b][:, 0:384],
                    groups=[dict(src=ps[b][:, 0:384].rearrange("p (h d) -> p h d", d=MLA_QK), sq=(0, 384), nh=4,
                                 hd=MLA_QK, dst=tb, gain=vv("mla_q_g"), outs=[tb],
                                 rope=rope_of(32, t) + (MLA_NOPE, 32))],
                    turn=[tb[:, i, :] for i in range(4)],
                    store=(QdT[0:MLA_QK, hh * 4:hh * 4 + 4, t * P:(t + 1) * P], MLA_QK)))
                nv += 1
        for t in range(4):
            for hh in range(2):
                u = len(units["UQ"])
                b = u % 4
                tb = tn[nv % 3][:, 0:384].rearrange("p (h d) -> p h d", d=MLA_QK)
                kd = kda[nv % 2]
                pv = ps[b][:, :].rearrange("p (h d) -> p h d", d=128)
                units["UQ"].append(dict(
                    g=sU1.first, lhs=[ckvT[:, t * P:(t + 1) * P]], w=[ukvw[:, hh * 512:(hh + 1) * 512]],
                    width=512, bank=b, last=(t == 3 and hh == 1),
                    copies=[(kd[:, :, 0:MLA_NOPE], pv[:, :, 0:64]),
                            (kd[:, :, MLA_NOPE:], krt[:, t, :].unsqueeze(1).to_broadcast([P, 4, 32])),
                            (Vd[:, t, hh * 256:(hh + 1) * 256].rearrange("p (h d) -> p h d", d=64), pv[:, :, 64:128])],
                    assembled=True,
                    sq=kd.rearrange("p h d -> p (h d)"),
                    groups=[dict(src=kd, sq=(0, 384), nh=4, hd=MLA_QK, dst=tb, gain=vv("mla_k_g"), outs=[tb],
                                 rope=(rope_of(32, t) + (MLA_NOPE, 32)) if t < 2 else None)],
                    turn=[tb[:, i, :] for i in range(4)],
                    store=(KdT[0:MLA_QK, hh * 4:hh * 4 + 4, t * P:(t + 1) * P], MLA_QK)))
                nv += 1
        for us in units.values():
            v = na = 0
            for un in us:
                if un.get("assembled"):
                    na += 1
                    un["nth_assembled"] = na
                un["x"] = next(i for i, o in enumerate(us) if o is un)
                if un["groups"]:
                    un["v"] = v
                    v += 1
        NV = {nm: sum(1 for u in us if u["groups"]) for nm, us in units.items()}
        LAGT = 2

        def att_plan(layer):
            items, pvs, groups = [], [], []
            tiles = range(4) if layer == 0 else range(2)
            for t in tiles:
                nk = 512 if t < 2 else 256
                k0 = 0 if t < 2 else 256
                kts = range(k0 // P, 4)
                for half in range(2):
                    gp = dict(t=t, half=half)
                    if layer == 0 and half == 0:
                        for h in range(8):
                            rows = slice(64 * (h % 2), 64 * (h % 2) + 64)
                            items.append(dict(q=QT0[0][rows, h // 2, t * P:(t + 1) * P],
                                              k=QT0[1][rows, h // 2, k0:512], nk=nk, scale=1.0,
                                              bias=bt[:, h, 2 - 2 * t:6 - 2 * t, :] if t < 2 else None))
                            pvs.append(dict(items=[len(items) - 1], nk=nk, ob=4 + len(pvs) % 2, dv=64,
                                            v=[V0[:, kt, h * 64:h * 64 + 64] for kt in kts],
                                            dst=O0[:, t, h * 64:h * 64 + 64]))
                    elif layer == 0:
                        for h in range(4):
                            for m in range(2):
                                rows = slice(64 * m, 64 * m + 64)
                                items.append(dict(q=QT0[2][rows, h, t * P:(t + 1) * P],
                                                  k=QT0[3][rows, h, k0:512], nk=nk, scale=1.0, bias=None))
                            pvs.append(dict(items=[len(items) - 2, len(items) - 1], nk=nk, ob=4 + len(pvs) % 2,
                                            dv=128, v=[V0[:, kt, 512 + h * 128:512 + h * 128 + 128] for kt in kts],
                                            dst=O0[:, t, 512 + h * 128:512 + h * 128 + 128]))
                    elif half == 0:
                        for h in range(8):
                            rows = slice(64 * (h % 2), 64 * (h % 2) + 64)
                            kv = h // 4
                            items.append(dict(q=QcT[rows, h // 2, t * P:(t + 1) * P], k=KcT[rows, kv, :], nk=nk,
                                              scale=1.0, bias=None))
                            pvs.append(dict(items=[len(items) - 1], nk=nk, ob=4 + len(pvs) % 2, dv=64,
                                            v=[Vc[:, kt, kv * 64:kv * 64 + 64] for kt in kts],
                                            dst=O1[:, t, h * 64:h * 64 + 64]))
                    else:
                        for h in range(8):
                            items.append(dict(q=QdT[0:MLA_QK, h, t * P:(t + 1) * P], k=KdT[0:MLA_QK, h, :], nk=nk,
                                              scale=float(MLA_QK) ** -0.5, bias=None))
                            pvs.append(dict(items=[len(items) - 1], nk=nk, ob=4 + len(pvs) % 2, dv=64,
                                            v=[Vd[:, kt, h * 64:h * 64 + 64] for kt in kts],
                                            dst=O1[:, t, 512 + h * 64:512 + h * 64 + 64]))
                    gp["pv1"] = len(pvs)
                    gp["sub"] = layer == 0 and half == 1
                    gp["otok"] = (O0 if layer == 0 else O1)[:, t, half * 512:(half + 1) * 512]
                    groups.append(gp)
            for j, pv in enumerate(pvs):
                for i in pv["items"]:
                    items[i]["pv"] = j
            for gi, gp in enumerate(groups):
                gp["e"] = gi
                gp["subs_upto"] = sum(1 for q in groups[:gi + 1] if q["sub"])
            return dict(items=items, pvs=pvs, groups=groups)

        plans = {"A0": att_plan(0), "A1": att_plan(1)}
        DONE_AT = 5

        def closes(pl, i):
            return [gp for gp in pl["groups"] if pl["pvs"][gp["pv1"] - 1]["items"][-1] == i - DONE_AT]

        def pv_at(pl, i):
            return [j for j, pv in enumerate(pl["pvs"]) if pv["items"][-1] == i]

        NSTEP = {nm: len(pl["items"]) + DONE_AT + 2 for nm, pl in plans.items()}

        block = ctx.enter_context(nc.Block())

        @block.sync
        def _(sp):
            def load(g, dst, src, wait=True):
                if g >= RING and wait:
                    sp.wait_ge(*released[g - RING])
                sp.dma_start(dst, src).then_inc(slot_full[slot_of(g)], 16)

            def cols(w, c0, n):
                return w[:, c0:c0 + n].rearrange("(k p) n -> p k n", p=P)

            def matrix(st, w, c0=0):
                for j in range(st.n):
                    load(st.first + j, slot3(st.first + j, 512), cols(w, c0 + 512 * j, 512))

            matrix(sA0a, a["ada_w"][0])
            matrix(sW0, a["ev_w_in"])
            matrix(sA0b, a["ada_w"][0], 2048)
            matrix(sO0, a["ev_w_out"])
            for j in range(sF0.n):
                g = sF0.first + j
                load(g, slot3(g, 256)[:, 0:KT, :], cols(a["ffn_w_gate"], 256 * j, 256))
                load(g, slot3(g, 256)[:, KT:2 * KT, :], cols(a["ffn_w_up"], 256 * j, 256), wait=False)
            for j in range(sD0.n):
                g = sD0.first + j
                dst = rslot(g)[:, 0:11 * 256].rearrange("p (f n) -> p f n", n=256)
                rows = slice((j % 2) * 11 * P, (j % 2 + 1) * 11 * P)
                load(g, dst, a["ffn_w_down"][rows, 256 * (j // 2):256 * (j // 2 + 1)].rearrange("(f p) n -> p f n", p=P))
            matrix(sA1, a["ada_w"][1])
            for j in range(3):
                g = sW1.first + j
                n = 512 if j < 2 else 160
                dst = slot3(g, 512) if j < 2 else rslot(g)[:, 0:KT * 160].rearrange("p (a b) -> p a b", b=160)
                load(g, dst, cols(a["od_w_in"], 512 * j, n))
            load(sU1.first, uqw, a["mla_w_uq"].rearrange("(k p) n -> p k n", p=P))
            load(sU1.first, ukvw, a["mla_w_ukv"], wait=False)
            matrix(sO1, a["od_w_out"])

            w13 = [a[n].rearrange("e (k p) (c n) -> e c p k n", p=P, n=QF * P) for n in ("moe_w1", "moe_w3")]
            w2 = a["moe_w2"].rearrange("e (c f p) n -> e c p f n", p=P, f=QF)

            def expert_chunk(e, c):
                m = mslot[c % MRING]
                if c < 14:
                    return m.rearrange("p (a b) -> p a b", b=QF * P), w13[c % 2][e, c // 2]
                return m.rearrange("p (a b) -> p a b", b=D), w2[e, c - 14]

            def expert_load(e, c, sem_, value):
                sp.wait_ge(sem_, value)
                dst, src = expert_chunk(e, c)
                sp.dma_start(dst, src).then_inc(mslot_full[c % MRING], 16)

            for c in range(MCH):
                if c < MRING:
                    expert_load(0, c, *released[PRE - 1 - (3, 2, 0)[c]])
                else:
                    expert_load(0, c, m_lo, 2 * (c - MRING) + 2)
            sp.wait_ge(items_rd, 1)
            total = sp.value_load(nit[0:1, 0:1], min_val=NE, max_val=NE * ROUNDS)
            with sp.Fori(1, total) as n:
                e = n % NE
                for c in range(MCH):
                    expert_load(e, c, m_lo, n * NU + 2 * (c - MRING) + 2)
            sp.wait_ge(m_add, total + 1)
            sp.dma_start(out.rearrange("(k p) n -> p k n", p=P), xT[:, :, 0:S_LAT]).then_inc(s_out, 16)
            sp.wait_ge(s_out, 16)

        @block.gpsimd
        def _(pool):
            ch = Chain(pool, p_step)
            pool.memset(ones[:, :], 1.0).then_inc(s_ones, 1)
            rp = a["rpb"]
            for rr in range(2):
                for h in range(8):
                    off = (h * RPB_DR + 1 - rr) * RPB_ROW + GRID_W - 1
                    pool.dma_start(bt[rr * 64:rr * 64 + 64, h, :, :],
                                   bass.AP(rp.tensor, off, [[2 * GRID_W - 2, 64], [RPB_ROW, 6], [1, 64]])).then_inc(s_bt, 16)
            pool.wait_ge(gain_rd, 1)

            def rotate(nm):
                s = proj[nm]
                for un in units[nm]:
                    if not un["groups"]:
                        continue
                    if un.get("assembled"):
                        pool.wait_ge(s["normed"], un["nth_assembled"])
                    else:
                        pool.wait_ge(s["taken"], un["x"] + 1)
                    for gr in un["groups"]:
                        nh, hd = gr["nh"], gr["hd"]
                        gb = gr["gain"].unsqueeze(1).to_broadcast([P, nh, hd])
                        if gr["rope"] is None:
                            for o in gr["outs"]:
                                ch.after(pool.tensor_tensor(o, gr["dst"], gb, ALU.mult))
                            continue
                        cos, sin, r0, rl = gr["rope"]
                        ch.after(pool.tensor_tensor(gr["dst"], gr["dst"], gb, ALU.mult))
                        q = rl // 4
                        x = gr["dst"][:, :, r0:r0 + rl]
                        va = ra[:, 0:nh * rl].rearrange("p (h d) -> p h d", d=rl)
                        vb = rb[:, 0:nh * rl].rearrange("p (h d) -> p h d", d=rl)
                        pool.tensor_tensor(va, x, cos.unsqueeze(1).to_broadcast([P, nh, rl]), ALU.mult)
                        x4 = x.rearrange("p h (a c q) -> p h a c q", a=2, c=2)
                        b4 = vb.rearrange("p h (a c q) -> p h a c q", a=2, c=2)
                        s4 = sin.rearrange("p (a c q) -> p a c q", a=2, c=2)
                        for c in range(2):
                            for ax in range(2):
                                ins = pool.tensor_tensor(b4[:, :, ax, c, :], x4[:, :, ax, 1 - c, :],
                                                         s4[:, ax, c, :].unsqueeze(1).to_broadcast([P, nh, q]), ALU.mult)
                        ch.after(ins)
                        for o in gr["outs"]:
                            ch.after(pool.tensor_tensor(o[:, :, r0:r0 + rl], va, vb, ALU.add))
                    pool.sem_inc(s["rotated"], 1)

            for nm in ("L0", "L1", "UQ"):
                rotate(nm)

        @block.scalar
        def _(act):
            ch = Chain(act, a_step)
            act.dma_start(cond[:, :], a["cond"]).then_inc(s_cst, 16)
            act.dma_start(adab[:, :, :].rearrange("p a b -> p (a b)"), a["adab"]).then_inc(s_cst, 16)
            act.dma_start(ng[:, :, :, :].rearrange("p a b c -> p (a b c)"), a["ng"]).then_inc(s_cst, 16)
            act.dma_start(cst[:, :], a["cst"]).then_inc(s_cst, 16)
            act.dma_start(vec[:, :], a["vec"].partition_broadcast(P)).then_inc(s_cst, 16)
            act.dma_start(xT[:, :, 0:S_LAT], a["xT"].rearrange("(k p) n -> p k n", p=P)).then_inc(s_x, 16)
            act.dma_start(xT[:, :, S_LAT:S_ALL], a["ctxT"].rearrange("(k p) n -> p k n", p=P)).then_inc(s_x, 16)
            act.dma_start(rtr[:, :, :], a["moe_router"].rearrange("(k p) n -> p k n", p=P)).then_inc(s_cst, 16)
            act.wait_ge(s_cst, 96)
            act.activation(scond[:, :], cond[:, :], ACT.Silu).then_inc(s_scond, 1)
            act.wait_ge(gain_rd, 1)
            act.wait_ge(lam_in, 1)
            act.activation(lamt[:, 2:4], lamt[:, 0:2], ACT.Exp).then_inc(lam_ex, 1)
            act.wait_ge(s_x, 32)

            def squares(nm, nt, k0, k1):
                s = norm[nm]
                for k in range(k0, k1):
                    if k >= 4:
                        act.wait_ge(s["summed"], k - 3)
                    act.activation(sq[k % 4][:, 0:nt], xT[:, k, 0:nt], ACT.Square).then_inc(s["square"], 1)

            def root(nm, nt):
                s = norm[nm]
                act.wait_ge(s["summed"], KT)
                act.activation(rt[:, 0:nt], ps[6][:, 0:nt], ACT.Sqrt, bias=eps[:, 0:1], scale=1.0 / D)\
                   .then_inc(s["root"], 1)

            def shift(nm, l, w, nt):
                s = norm[nm]
                n = 0
                for c in range(nt // S_LAT):
                    for k in range(KT):
                        n += 1
                        act.wait_ge(s["scaled"], n)
                        hv = hT[:, k, c * S_LAT:(c + 1) * S_LAT]
                        act.activation(hv, hv, ACT.Identity, bias=ada[:, l, 24 * w + k, c:c + 1])\
                           .then_inc(s["ready"], 1)

            def ada_act(turns, n0):
                with act.Fori(0, turns) as i:
                    for j in range(4):
                        act.wait_ge(ada_used, i * 4 + (n0 + j + 1))
                        act.activation(adar[0:2, j % 2, :], ps[j % 2][0:2, :], ACT.Copy).then_inc(ada_row, 1)

            def proj_act(nm):
                s = proj[nm]

                def squares(un):
                    v = un["v"]
                    if un.get("assembled"):
                        act.wait_ge(s["taken"], un["x"] + 1)
                    else:
                        act.wait_ge(s["done"], un["x"] + 1)
                    if v >= 2:
                        act.wait_ge(s["reduced"], v - 1)
                    n = un["sq"].shape[1]
                    act.activation(sq[v % 2][:, 0:n], un["sq"], ACT.Square).then_inc(s["squared"], 1)

                def root(un):
                    v = un["v"]
                    act.wait_ge(s["reduced"], v + 1)
                    o = 0
                    for gr in un["groups"]:
                        ins = act.activation(rt8[:, v % 4, o:o + gr["nh"]], ss[:, v % 4, o:o + gr["nh"]], ACT.Sqrt,
                                             bias=eps[:, 0:1], scale=1.0 / gr["hd"])
                        o += gr["nh"]
                    ins.then_inc(s["root"], 1)

                def store(un):
                    v = un["v"]
                    act.wait_ge(s["turned"], v + 1)
                    bank = ps[4 + v % 2]
                    dst, rows = un["store"]
                    n = dst.shape[1]
                    ins = act.activation(dst, bank[0:rows, 0:n * P].rearrange("p (a b) -> p a b", b=P), ACT.Copy)
                    if "store2" in un:
                        d2, n2 = un["store2"]
                        ins = act.activation(d2, bank[:, n * P:(n + n2) * P].rearrange("p (a b) -> p a b", b=P), ACT.Copy)
                    ins.then_inc(s["stored"], 1)

                us = units[nm]
                for x in range(len(us) + 3):
                    if x < len(us) and us[x]["groups"]:
                        squares(us[x])
                        root(us[x])
                    if x >= 3 and us[x - 3]["groups"]:
                        store(us[x - 3])

            def att_act(nm):
                s, pl = att[nm], plans[nm]
                nst = 0
                for i in range(NSTEP[nm]):
                    if i < len(pl["items"]):
                        it = pl["items"][i]
                        act.wait_ge(s["max"], i + 1)
                        if i >= 4:
                            act.wait_ge(s["turned"], pl["items"][i - 4]["pv"] + 1)
                        act.activation(prob[i % 4][:, 0:it["nk"]], ps[i % 2][:, 0:it["nk"]], ACT.Exp,
                                       bias=nmx[:, i % 64:i % 64 + 1], scale=it["scale"],
                                       accum_out=sums[:, i % 64:i % 64 + 1]).then_inc(s["exp"], 1)
                    for j in pv_at(pl, i - 2):
                        nk = pl["pvs"][j]["nk"]
                        act.wait_ge(s["turned"], j + 1)
                        if j >= 2:
                            act.wait_ge(s["pv"], j - 1)
                        act.activation(probT[j % 2][:, 0:nk], ps[2 + j % 2][:, 0:nk], ACT.Copy).then_inc(s["copied"], 1)
                    for gp in closes(pl, i):
                        if gp["sub"]:
                            act.wait_ge(s["out"], gp["pv1"])
                            act.activation(sq[gp["e"] % 2], gp["otok"], ACT.Square).then_inc(s["osq"], 1)
                            act.wait_ge(s["ored"], gp["subs_upto"])
                            act.activation(rt8[:, 0, 0:4], ss[:, 0, 0:4], ACT.Sqrt, bias=eps[:, 0:1], scale=1.0 / P)\
                               .then_inc(s["oroot"], 1)
                    for gp in closes(pl, i - 1):
                        e = gp["e"]
                        act.wait_ge(s["oturned"], e + 1)
                        act.activation(hT[:, 4 * gp["half"]:4 * gp["half"] + 4, gp["t"] * P:(gp["t"] + 1) * P],
                                       ps[6 + e % 2][:, :].rearrange("p (a b) -> p a b", b=P), ACT.Copy)\
                           .then_inc(s["ostored"], 1)

            squares("n00", S_ALL, 0, KT)
            root("n00", S_ALL)
            ada_act(1, 0)
            shift("n00", 0, 0, S_ALL)
            proj_act("L0")
            ada_act(2, 4)
            att_act("A0")
            act.wait_ge(outp["O0"]["added"], KT)
            squares("n01", S_ALL, 0, KT)
            root("n01", S_ALL)
            shift("n01", 0, 1, S_ALL)
            with act.Fori(0, 5) as i:
                for j in range(4):
                    act.wait_ge(gu_mm, i * 4 + (j + 1))
                    act.activation(sq[j], ps[2 * j][:, :], ACT.Silu).then_inc(silu_rd, 1)
            for j in range(2):
                act.wait_ge(gu_mm, 20 + j + 1)
                act.activation(sq[j], ps[2 * j][:, :], ACT.Silu).then_inc(silu_rd, 1)
            act.wait_ge(dn_add, KT + 4)
            squares("n10", S_ALL, 0, 4)
            ada_act(3, 12)
            squares("n10", S_ALL, 4, KT)
            root("n10", S_ALL)
            shift("n10", 1, 0, S_ALL)
            proj_act("L1")
            proj_act("UQ")
            att_act("A1")
            act.wait_ge(outp["O1"]["added"], KT)
            squares("n11", S_LAT, 0, KT)
            root("n11", S_LAT)
            shift("n11", 1, 1, S_LAT)
            for t in range(2):
                for hh in range(2):
                    act.wait_ge(tok_t, 2 * t + hh + 1)
                    act.activation(htok[:, t, hh * 512:(hh + 1) * 512], ps[2 * t + hh][:, :], ACT.Copy).then_inc(tok_rd, 1)
            act.wait_ge(rt_ein, 1)
            act.activation(ro[:, 8, 0, 0:2], ro[:, 7, 0, 0:2], ACT.Exp).then_inc(rt_ex, 1)
            act.wait_ge(items_rd, 1)
            total = act.value_load(nit[0:1, 0:1], min_val=NE, max_val=NE * ROUNDS)
            act.wait_ge(m_init, 1)

            def tokens_high(n):
                for hh in range(2):
                    act.wait_ge(m_gat, hh + 1 if n is None else n * 2 + (hh + 1))
                    act.activation(xgr[:, 0, 4 * hh:4 * hh + 4, :], v3(ps[4 + hh][:, :], CAP), ACT.Copy)\
                       .then_inc(m_xh, 1)

            def sum_copy(n):
                act.wait_ge(m_pe, n * NU + URING)
                act.activation(ytok[:, 0:512], ps[0][:, :], ACT.Copy).then_inc(m_ya, 1)

            tokens_high(None)
            with act.Fori(0, total) as n:
                for h in range(NU):
                    if h == 3:
                        sum_copy(n)
                    j = (h - 6) // 4
                    if h % 4 == 2 and 0 <= j < 7:
                        act.wait_ge(m_pe, n * NU + (4 * j + 4 + URING))
                        act.activation(sg[:, j % 2, :], ps[4 + 2 * (j % 2)][:, :], ACT.Silu).then_inc(m_silu, 1)
                    j = (h - 10) // 4
                    if h % 4 == 2 and 0 <= j < 7:
                        act.wait_ge(m_t, n * 7 + (j + 1))
                        act.activation(hidr[:, 0, QF * j:QF * j + QF, :], v3(ps[2 + j % 2][:, :], CAP), ACT.Copy)\
                           .then_inc(m_hh, 1)
                    if h == 37:
                        tokens_high(n + 1)
                    if h % 2 == 0:
                        c = h // 2
                        act.wait_ge(mslot_full[c % MRING], n * 112 + 16 * (c // MRING + 1))
                    act.wait_ge(m_pe, n * NU + (h + 1))
                    act.activation(whi[:, h % URING, :], mslot[(h // 2) % MRING][:, (h % 2) * UNIT:(h % 2 + 1) * UNIT],
                                   ACT.Copy).then_inc(m_hi, 1)
            sum_copy(total)

        @block.vector
        def _(dve):
            ch = Chain(dve, d_step)
            dve.sem_inc(ada_rd, 1)
            dve.memset(eps[:, :], EPS)
            dve.wait_ge(s_cst, 96)
            for n in ("na_q_g", "diff_q_g", "gqa_q_g"):
                dve.tensor_scalar(vv(n), vv(n), HD ** -0.5, None, ALU.mult)
            dve.tensor_scalar(vv("diff_subln_g"), vv("diff_subln_g"), 1.0 - LAM_INIT, None, ALU.mult).then_inc(gain_rd, 1)
            ch.after(dve.tensor_tensor(sq[0][:, 0:64], vv("diff_lq1"), vv("diff_lk1"), ALU.mult))
            ch.after(dve.tensor_tensor(sq[0][:, 64:128], vv("diff_lq2"), vv("diff_lk2"), ALU.mult))
            dve.tensor_reduce(lamt[:, 0:2], v3(sq[0][:, 0:128], 64), AX.X, ALU.add).then_inc(lam_in, 1)
            dve.wait_ge(s_bt, 16 * 16)
            btv = bt[:, :, :, :].rearrange("p h u c -> p (h u) c")
            ch.after(dve.tensor_tensor(btv, btv, cv("mask").unsqueeze(1).to_broadcast([P, 48, GRID_W]), ALU.add))
            dve.wait_ge(lam_ex, 1)
            ch.after(dve.tensor_tensor(lamt[:, 4:5], lamt[:, 3:4], lamt[:, 2:3], ALU.subtract))
            ch.after(dve.tensor_scalar(lamt[:, 5:6], lamt[:, 4:5], -LAM_INIT, None, ALU.add))

            adaf = ada[:, :, :, :].rearrange("p l m c -> p (l m c)")
            adabf = adab[:, :, :].rearrange("p l m -> p (l m)")

            def ada_take(turns, n0, l, m0):
                with dve.Fori(0, turns) as i:
                    dve.wait_ge(ada_tr, i * 4 + (n0 + 4))
                    dve.tensor_tensor(adaf[:, bass.ds(i * 32 + (96 * l + 2 * m0), 32)].rearrange("p (m c) -> p m c", c=2),
                                      ps[7][:, 0:32].rearrange("p (m c) -> p m c", c=2),
                                      adabf[:, bass.ds(i * 16 + (48 * l + m0), 16)].unsqueeze(2).to_broadcast([P, 16, 2]),
                                      ALU.add).then_inc(ada_rd, 1)
                dve.wait_ge(ada_rd, n0 // 4 + turns + 1)

            def mod(l, w):
                ch.after(dve.scalar_tensor_tensor(out=amod[:, l, w, :, :], in0=ada[:, l, 24 * w + 8:24 * w + 16, :],
                                                  scalar=1.0, in1=ng[:, w, l, :].unsqueeze(2).to_broadcast([P, KT, 2]),
                                                  op0=ALU.add, op1=ALU.mult))

            def norm_dve(nm, l, w, nt):
                s = norm[nm]
                dve.wait_ge(s["root"], 1)
                ch.after(dve.reciprocal(rstd[:, 0:nt], rt[:, 0:nt]))
                for c in range(nt // S_LAT):
                    for k in range(KT):
                        tc = slice(c * S_LAT, (c + 1) * S_LAT)
                        dve.scalar_tensor_tensor(out=hT[:, k, tc], in0=xT[:, k, tc], scalar=amod[:, l, w, k, c:c + 1],
                                                 in1=rstd[:, tc], op0=ALU.mult, op1=ALU.mult).then_inc(s["scaled"], 1)

            def proj_dve(nm):
                s, us = proj[nm], units[nm]

                def first(x, un):
                    if un["copies"]:
                        if un["groups"] and not un.get("assembled"):
                            dve.wait_ge(s["squared"], un["v"] + 1)
                        else:
                            dve.wait_ge(s["done"], x + 1)
                        for d, sr in un["copies"]:
                            ins = dve.tensor_copy(d, sr)
                        if un.get("assembled") or not un["groups"]:
                            ins.then_inc(s["taken"], 1)
                    if un["groups"]:
                        v = un["v"]
                        dve.wait_ge(s["squared"], v + 1)
                        o = 0
                        for gr in un["groups"]:
                            lo, hi = gr["sq"]
                            ins = dve.tensor_reduce(ss[:, v % 4, o:o + gr["nh"]],
                                                    sq[v % 2][:, lo:hi].rearrange("p (h d) -> p h d", d=gr["hd"]),
                                                    AX.X, ALU.add)
                            o += gr["nh"]
                        ins.then_inc(s["reduced"], 1)

                def second(un):
                    v = un["v"]
                    dve.wait_ge(s["root"], v + 1)
                    nh = sum(gr["nh"] for gr in un["groups"])
                    ch.after(dve.reciprocal(rs8[:, v % 4, 0:nh], rt8[:, v % 4, 0:nh]))
                    if v >= 3:
                        dve.wait_ge(s["turned"], v - 2)
                    o = 0
                    for gr in un["groups"]:
                        ins = dve.tensor_tensor(gr["dst"], gr["src"],
                                                rs8[:, v % 4, o:o + gr["nh"]].unsqueeze(2)
                                                .to_broadcast([P, gr["nh"], gr["hd"]]), ALU.mult)
                        o += gr["nh"]
                    ins.then_inc(s["normed" if un.get("assembled") else "taken"], 1)

                pend = None
                for x, un in enumerate(us):
                    if pend is not None:
                        second(pend)
                        pend = None
                    first(x, un)
                    if un["groups"]:
                        pend = un
                if pend is not None:
                    second(pend)

            def att_dve(nm):
                s, pl = att[nm], plans[nm]
                nsub = 0
                for i in range(NSTEP[nm]):
                    if i < len(pl["items"]):
                        it = pl["items"][i]
                        c = i % 64
                        bank = ps[i % 2]
                        dve.wait_ge(s["score"], i + 1)
                        if it["bias"] is not None:
                            b3 = bank[:, 0:S_LAT].rearrange("p (r c) -> p r c", c=GRID_W)
                            ch.after(dve.tensor_tensor(b3, b3, it["bias"], ALU.add))
                        ch.after(dve.reduce_max(mx[:, c:c + 1], bank[:, 0:it["nk"]], AX.X))
                        dve.tensor_scalar(nmx[:, c:c + 1], mx[:, c:c + 1], -it["scale"], None, ALU.mult)\
                           .then_inc(s["max"], 1)
                    if 1 <= i <= len(pl["items"]):
                        q = i - 1
                        c = q % 64
                        dve.wait_ge(s["exp"], q + 1)
                        ch.after(dve.reciprocal(rsum[:, c:c + 1], sums[:, c:c + 1]))
                        for j in pv_at(pl, q):
                            pv = pl["pvs"][j]
                            if len(pv["items"]) == 2:
                                c0 = pv["items"][0] % 64
                                p0 = prob[pv["items"][0] % 4][:, 0:pv["nk"]]
                                p1 = prob[q % 4][:, 0:pv["nk"]]
                                dve.tensor_scalar(p0, p0, rsum[:, c0:c0 + 1], None, ALU.mult)
                                ch.after(dve.tensor_tensor(rsum[:, c:c + 1], rsum[:, c:c + 1], lamt[:, 5:6], ALU.mult))
                                dve.scalar_tensor_tensor(out=p1, in0=p1, scalar=rsum[:, c:c + 1], in1=p0,
                                                         op0=ALU.mult, op1=ALU.add).then_inc(s["mixed"], 1)
                    for j in pv_at(pl, i - 4):
                        pv = pl["pvs"][j]
                        o = ps[pv["ob"]][:, 0:pv["dv"]]
                        dve.wait_ge(s["pv"], j + 1)
                        if len(pv["items"]) == 2:
                            dve.tensor_copy(pv["dst"], o).then_inc(s["out"], 1)
                        else:
                            c = pv["items"][0] % 64
                            dve.tensor_scalar(pv["dst"], o, rsum[:, c:c + 1], None, ALU.mult).then_inc(s["out"], 1)
                    for gp in closes(pl, i):
                        if gp["sub"]:
                            nsub += 1
                            dve.wait_ge(s["osq"], nsub)
                            dve.tensor_reduce(ss[:, 0, 0:4], v3(sq[gp["e"] % 2], P), AX.X, ALU.add).then_inc(s["ored"], 1)
                            dve.wait_ge(s["oroot"], nsub)
                            ch.after(dve.reciprocal(rs8[:, 0, 0:4], rt8[:, 0, 0:4]))
                            o3 = v3(gp["otok"], P)
                            ch.after(dve.tensor_tensor(o3, o3,
                                                       rs8[:, 0, 0:4].unsqueeze(2).to_broadcast([P, 4, P]), ALU.mult))
                            dve.tensor_tensor(o3, o3, vv("diff_subln_g").unsqueeze(1).to_broadcast([P, 4, P]),
                                              ALU.mult).then_inc(s["otok"], 1)

            def out_dve(nm, l, nc_):
                s = outp[nm]
                for d in range(KT):
                    dve.wait_ge(s["done"], d + 1)
                    for c in range(nc_):
                        tc = slice(c * S_LAT, (c + 1) * S_LAT)
                        ins = dve.scalar_tensor_tensor(out=xT[:, d, tc], in0=ps[d % 4][:, tc],
                                                       scalar=ada[:, l, 16 + d, c:c + 1], in1=xT[:, d, tc],
                                                       op0=ALU.mult, op1=ALU.add)
                    ins.then_inc(s["added"], 1)

            ada_take(1, 0, 0, 0)
            mod(0, 0)
            norm_dve("n00", 0, 0, S_ALL)
            proj_dve("L0")
            ada_take(2, 4, 0, 16)
            mod(0, 1)
            att_dve("A0")
            out_dve("O0", 0, 2)
            norm_dve("n01", 0, 1, S_ALL)
            dve.sem_inc(hid_rd, 4)
            with dve.Fori(0, 5) as i:
                for j in range(4):
                    dve.wait_ge(silu_rd, i * 4 + (j + 1))
                    hv = hid.rearrange("p f n -> p (f n)")[:, bass.ds(i * (4 * S_ALL) + j * S_ALL, S_ALL)]
                    dve.tensor_tensor(hv, sq[j], ps[2 * j + 1][:, :], ALU.mult).then_inc(hid_rd, 1)
            for j in range(2):
                dve.wait_ge(silu_rd, 20 + j + 1)
                dve.tensor_tensor(hid[:, 20 + j, :], sq[j], ps[2 * j + 1][:, :], ALU.mult).then_inc(hid_rd, 1)
            dve.sem_inc(dn_add, 4)
            with dve.Fori(0, 2) as i:
                for j in range(4):
                    dve.wait_ge(dn_mm, i * 4 + (j + 1))
                    for c in range(2):
                        xv = xT[:, :, :].rearrange("p k n -> p (k n)")[:, bass.ds(i * (4 * S_ALL) + (j * S_ALL + c * S_LAT), S_LAT)]
                        gv = ada[:, 0, :, :].rearrange("p m c -> p (m c)")[:, bass.ds(i * 8 + (2 * (40 + j) + c), 1)]
                        ins = dve.scalar_tensor_tensor(out=xv, in0=ps[j][:, c * S_LAT:(c + 1) * S_LAT], scalar=gv,
                                                       in1=xv, op0=ALU.mult, op1=ALU.add)
                    ins.then_inc(dn_add, 1)
            ada_take(3, 12, 1, 0)
            mod(1, 0)
            mod(1, 1)
            norm_dve("n10", 1, 0, S_ALL)
            proj_dve("L1")
            proj_dve("UQ")
            att_dve("A1")
            out_dve("O1", 1, 1)
            norm_dve("n11", 1, 1, S_LAT)

            def R(i):
                return ro[:, i, :, :]

            def B(ap):
                return ap.unsqueeze(2).to_broadcast([P, 2, NE])

            col = [ro[:, 16 + i, 0, 0:2] for i in range(8)]
            rank = cv("rank").unsqueeze(1).to_broadcast([P, 2, NE])
            dve.wait_ge(rt_mm, 1)
            ch.after(dve.tensor_copy(R(0), ps[5][:, 0:2 * NE].rearrange("p (t e) -> p t e", e=NE)))

            def best(src, eq, one, m):
                ch.after(dve.tensor_reduce(m, src, AX.X, ALU.max))
                ch.after(dve.tensor_tensor(eq, src, B(m), ALU.is_equal))
                ch.after(dve.tensor_tensor(eq, eq, rank, ALU.mult))
                ch.after(dve.tensor_reduce(col[7], eq, AX.X, ALU.max))
                ch.after(dve.tensor_tensor(one, eq, B(col[7]), ALU.is_equal))

            best(R(0), R(1), R(2), col[0])
            ch.after(dve.scalar_tensor_tensor(out=R(3), in0=R(2), scalar=-3e38, in1=R(0), op0=ALU.mult, op1=ALU.add))
            best(R(3), R(1), R(4), col[1])
            dve.tensor_tensor(R(5), R(2), R(4), ALU.add).then_inc(rt_sel, 1)
            dve.tensor_tensor(ro[:, 7, 0, 0:2], col[1], col[0], ALU.subtract).then_inc(rt_ein, 1)
            dve.wait_ge(rt_ex, 1)
            ch.after(dve.tensor_scalar(col[2], ro[:, 8, 0, 0:2], 1.0, None, ALU.add))
            ch.after(dve.reciprocal(col[3], col[2]))
            ch.after(dve.tensor_tensor(col[4], col[3], ro[:, 8, 0, 0:2], ALU.mult))
            ch.after(dve.tensor_tensor(R(9), R(2), B(col[3]), ALU.mult))
            ch.after(dve.tensor_tensor(R(10), R(4), B(col[4]), ALU.mult))
            ch.after(dve.tensor_tensor(R(11), R(9), R(10), ALU.add))
            dve.wait_ge(rt_pos, 1)
            dve.memset(posr[:, :, NI - 1:NI], 0.0)
            dve.memset(gat[:, :, NI - 1:NI], 0.0)
            dve.memset(chs[:, :, NI - 1:NI], 0.0)
            for r in range(ROUNDS):
                rs = slice(r * NE, (r + 1) * NE)
                dve.tensor_scalar(posr[:, :, rs], ps[4][:, 0:2 * NE].rearrange("p (t e) -> p t e", e=NE),
                                  -float(r * CAP), None, ALU.add)
                dve.tensor_copy(gat[:, :, rs], R(11))
                dve.tensor_copy(chs[:, :, rs], R(5))
            ch.after(dve.reduce_max(col[5][:, 0:1], ps[4][:, 2 * NE:3 * NE], AX.X))
            ch.after(dve.tensor_scalar(col[5][:, 1:2], col[5][:, 0:1], float(CAP), float(NE), ALU.is_gt, ALU.mult))
            assert ROUNDS == 2
            dve.tensor_scalar(nit[:, 0:1], col[5][:, 1:2], float(NE), None, ALU.add).then_inc(items_rd, 1)
            dve.wait_ge(items_rd, 1)
            total = dve.value_load(nit[0:1, 0:1], min_val=NE, max_val=NE * ROUNDS)
            pf = posr[:, :, :].rearrange("p t n -> p (t n)")
            gf = gat[:, :, :].rearrange("p t n -> p (t n)")
            cf = chs[:, :, :].rearrange("p t n -> p (t n)")
            dve.memset(ps[0][:, :], 0.0)
            dve.memset(ps[1][:, :], 0.0)
            dve.memset(pgT[:, :], 0.0).then_inc(m_init, 1)
            dve.sem_inc(m_mul, 2)

            def choose(dst, m, table):
                for t in range(2):
                    pc = pf[:, t * NI:t * NI + 1] if m is None else pf[:, bass.ds(m + t * NI, 1)]
                    tc = table[:, t * NI:t * NI + 1] if m is None else table[:, bass.ds(m + t * NI, 1)]
                    ins = dve.tensor_scalar(dst[:, t, :], cv("iota"), pc, tc, ALU.is_equal, ALU.mult)
                return ins

            def tokens_low(n):
                for hh in range(2):
                    dve.wait_ge(m_xh, hh + 1 if n is None else n * 2 + (hh + 1))
                    dve.tensor_tensor(xgr[:, 1, 4 * hh:4 * hh + 4, :], v3(ps[4 + hh][:, :], CAP),
                                      xgr[:, 0, 4 * hh:4 * hh + 4, :].bitcast(F32), ALU.subtract).then_inc(m_xl, 1)

            def sum_copy(n):
                dve.wait_ge(m_pe, n * NU + URING)
                dve.tensor_copy(ytok[:, 512:1024], ps[1][:, :]).then_inc(m_yb, 1)

            def add(n, i):
                dve.wait_ge(m_sc, n * 4 + (i + 1))
                for q in range(2):
                    d = 2 * i + q
                    ins = dve.scalar_tensor_tensor(out=xT[:, d, 0:S_LAT], in0=ps[i][:, q * S_LAT:(q + 1) * S_LAT],
                                                   scalar=ada[:, 1, 40 + d, 0:1], in1=xT[:, d, 0:S_LAT],
                                                   op0=ALU.mult, op1=ALU.add)
                if i == 3:
                    ins.then_inc(m_add, 1)

            choose(sel, None, cf).then_inc(m_sel, 1)
            tokens_low(None)
            with dve.Fori(0, total) as n:
                for h in range(NU):
                    if h == 3:
                        sum_copy(n)
                    if 5 <= h < 9:
                        add(n, h - 5)
                    j = (h - 6) // 4
                    if h % 4 == 2 and 0 <= j < 7:
                        dve.wait_ge(m_silu, n * 7 + (j + 1))
                        dve.tensor_tensor(hidtok[:, j % 2, :], sg[:, j % 2, :], ps[5 + 2 * (j % 2)][:, :], ALU.mult)\
                           .then_inc(m_mul, 1)
                    j = (h - 10) // 4
                    if h % 4 == 2 and 0 <= j < 7:
                        dve.wait_ge(m_hh, n * 7 + (j + 1))
                        hs = slice(QF * j, QF * j + QF)
                        dve.tensor_tensor(hidr[:, 1, hs, :], v3(ps[2 + j % 2][:, :], CAP),
                                          hidr[:, 0, hs, :].bitcast(F32), ALU.subtract).then_inc(m_hl, 1)
                    if h == 9:
                        choose(gsel, n, gf).then_inc(m_gsel, 1)
                    if h == 17:
                        dve.wait_ge(m_pgt, n + 1)
                        dve.tensor_copy(pgT[:, :], ps[0][:, 0:S_LAT]).then_inc(m_pg, 1)
                    if h == 29:
                        choose(sel, n + 1, cf).then_inc(m_sel, 1)
                    if h == 37:
                        tokens_low(n + 1)
                    dve.wait_ge(m_hi, n * NU + (h + 1))
                    dve.tensor_tensor(wlo[:, h % URING, :], mslot[(h // 2) % MRING][:, (h % 2) * UNIT:(h % 2 + 1) * UNIT],
                                      whi[:, h % URING, :].bitcast(F32), ALU.subtract).then_inc(m_lo, 1)
            sum_copy(total)
            for i in range(4):
                add(total, i)

        @block.tensor
        def _(pe):
            def arrived(g, i=None, per=1, times=1):
                pe.wait_ge(slot_full[slot_of(g)], 16 * loads_upto(g) if i is None else i * (16 * times) + 16 * loads_upto(g))

            def dmas(g):
                return 2 if (sF0.first <= g < sF0.first + sF0.n or g == sU1.first) else 1

            def loads_upto(g):
                return sum(dmas(q) for q in range(slot_of(g), g + 1, RING))

            def norm_pe(nm, nt):
                s = norm[nm]
                for k in range(KT):
                    pe.wait_ge(s["square"], k + 1)
                    pe.matmul(ps[6][:, 0:nt], ones[:, :], sq[k % 4][:, 0:nt], start=(k == 0), stop=(k == KT - 1))\
                      .then_inc(s["summed"], 1)

            def ada_stage(st, n0):
                def turn(j):
                    pe.wait_ge(ada_row, n0 + j + 1)
                    if j % 4 == 0:
                        pe.wait_ge(ada_rd, (n0 + j) // 4 + 1)
                    for q in range(4):
                        c = 2 * (4 * (j % 4) + q)
                        ins = pe.transpose(ps[7][:, c:c + 2], adar[0:2, j % 2, q * P:(q + 1) * P], ident[0:2, 0:2])
                    ins.then_inc(ada_tr, 1)

                for j in range(st.n):
                    arrived(st.first + j)
                    w = slot3(st.first + j, 512)
                    for k in range(KT):
                        ins = pe.matmul(ps[j % 2][0:2, :], scond[:, 2 * k:2 * k + 2], w[:, k, :],
                                        start=(k == 0), stop=(k == KT - 1))
                    ins.then_inc(ada_used, 1)
                    if j:
                        turn(j - 1)
                turn(st.n - 1)

            def proj_pe(nm):
                s, us = proj[nm], units[nm]

                def turn(un):
                    v = un["v"]
                    pe.wait_ge(s["rotated"], v + 1)
                    if v >= 2:
                        pe.wait_ge(s["stored"], v - 1)
                    for c, src in enumerate(un["turn"]):
                        w = src.shape[1]
                        ins = pe.transpose(ps[4 + v % 2][0:w, c * P:(c + 1) * P], src, ident)
                    ins.then_inc(s["turned"], 1)

                for x in range(len(us) + LAGT):
                    if x < len(us):
                        un = us[x]
                        if x == 0 or us[x - 1]["g"] != un["g"]:
                            arrived(un["g"])
                        if x >= 4:
                            pe.wait_ge(s["taken"], x - 3)
                        for k in range(len(un["lhs"])):
                            ins = pe.matmul(ps[un["bank"]][:, 0:un["width"]], un["lhs"][k], un["w"][k],
                                            start=(k == 0), stop=(k == len(un["lhs"]) - 1))
                        ins.then_inc(s["done"], 1)
                    if x >= LAGT and us[x - LAGT]["groups"]:
                        turn(us[x - LAGT])

            def att_pe(nm, nproj):
                s, pl = att[nm], plans[nm]
                for i in range(NSTEP[nm]):
                    if i < len(pl["items"]):
                        it = pl["items"][i]
                        if i >= 2:
                            pe.wait_ge(s["exp"], i - 1)
                        pe.matmul(ps[i % 2][:, 0:it["nk"]], it["q"], it["k"], start=True, stop=True)\
                          .then_inc(s["score"], 1)
                    for j in pv_at(pl, i - 3):
                        pv = pl["pvs"][j]
                        pe.wait_ge(s["copied"], j + 1)
                        if j >= 2:
                            pe.wait_ge(s["out"], j - 1)
                        nkt = pv["nk"] // P
                        for c in range(nkt):
                            ins = pe.matmul(ps[pv["ob"]][:, 0:pv["dv"]],
                                            probT[j % 2][:, c * P:(c + 1) * P], pv["v"][c],
                                            start=(c == 0), stop=(c == nkt - 1))
                        ins.then_inc(s["pv"], 1)
                    for j in pv_at(pl, i - 2):
                        pv = pl["pvs"][j]
                        if len(pv["items"]) == 2:
                            pe.wait_ge(s["mixed"], sum(1 for q in pl["pvs"][:j + 1] if len(q["items"]) == 2))
                        else:
                            pe.wait_ge(s["exp"], pv["items"][0] + 1)
                        if j >= 2:
                            pe.wait_ge(s["copied"], j - 1)
                        src = prob[pv["items"][-1] % 4]
                        for c in range(pv["nk"] // P):
                            ins = pe.transpose(ps[2 + j % 2][:, c * P:(c + 1) * P], src[:, c * P:(c + 1) * P], ident)
                        ins.then_inc(s["turned"], 1)
                    for gp in closes(pl, i - 1):
                        e = gp["e"]
                        if gp["sub"]:
                            pe.wait_ge(s["otok"], gp["subs_upto"])
                        else:
                            pe.wait_ge(s["out"], gp["pv1"])
                        if e >= 2:
                            pe.wait_ge(s["ostored"], e - 1)
                        for c in range(4):
                            ins = pe.transpose(ps[6 + e % 2][:, c * P:(c + 1) * P], gp["otok"][:, c * P:(c + 1) * P], ident)
                        ins.then_inc(s["oturned"], 1)

            def out_pe(nm, an, st, nt):
                s = outp[nm]
                pe.wait_ge(att[an]["ostored"], len(plans[an]["groups"]))
                for d in range(KT):
                    g = st.first + d // 4
                    if d % 4 == 0:
                        arrived(g)
                    if d >= 4:
                        pe.wait_ge(s["added"], d - 3)
                    w = slot3(g, 512)
                    for k in range(KT):
                        ins = pe.matmul(ps[d % 4][:, 0:nt], w[:, k, (d % 4) * P:(d % 4 + 1) * P], hT[:, k, 0:nt],
                                        start=(k == 0), stop=(k == KT - 1))
                    ins.then_inc(s["done"], 1)

            pe.wait_ge(s_ones, 1)
            norm_pe("n00", S_ALL)
            pe.wait_ge(s_scond, 1)
            ada_stage(sA0a, 0)
            pe.wait_ge(norm["n00"]["ready"], 2 * KT)
            pe.wait_ge(s_cst, 96)
            proj_pe("L0")
            pe.wait_ge(proj["L0"]["stored"], NV["L0"])
            pe.wait_ge(proj["L0"]["taken"], len(units["L0"]))
            ada_stage(sA0b, 4)
            pe.wait_ge(proj["L0"]["stored"], NV["L0"])
            pe.wait_ge(proj["L0"]["taken"], len(units["L0"]))
            att_pe("A0", "L0")
            out_pe("O0", "A0", sO0, S_ALL)
            norm_pe("n01", S_ALL)
            pe.wait_ge(norm["n01"]["ready"], 2 * KT)

            def gate_up(g, j, i=None):
                arrived(g, i, times=2)
                w = slot3(g, 256)
                for q in range(2):
                    f = 2 * j + q
                    b = 2 * (f % 4)
                    pe.wait_ge(hid_rd, f + 1 if i is None else i * 8 + (f + 1))
                    for part in range(2):
                        for k in range(KT):
                            ins = pe.matmul(ps[b + part][:, :], w[:, part * KT + k, q * P:(q + 1) * P], hT[:, k, :],
                                            start=(k == 0), stop=(k == KT - 1))
                    ins.then_inc(gu_mm, 1)

            with pe.Fori(0, 2) as i:
                for j in range(4):
                    gate_up(sF0.first + j, j, i)
            for j in range(8, 11):
                gate_up(sF0.first + j, j)
            pe.wait_ge(hid_rd, FT + 4)
            with pe.Fori(0, 2) as i:
                for j in range(4):
                    g = sD0.first + j
                    arrived(g, i)
                    w = rslot(g)[:, 0:11 * 256].rearrange("p (f n) -> p f n", n=256)
                    for q in range(2):
                        d = 2 * (j // 2) + q
                        if j % 2 == 0:
                            pe.wait_ge(dn_add, i * 4 + (d + 1))
                        for f in range(11):
                            ins = pe.matmul(ps[d][:, :], w[:, f, q * P:(q + 1) * P], hid[:, 11 * (j % 2) + f, :],
                                            start=(j % 2 == 0 and f == 0), stop=(j % 2 == 1 and f == 10))
                        if j % 2 == 1:
                            ins.then_inc(dn_mm, 1)
                    if j % 2 == 0:
                        ins.then_inc(dn_half, 1)

            pe.wait_ge(dn_add, KT + 4)
            ada_stage(sA1, 12)
            norm_pe("n10", S_ALL)
            pe.wait_ge(norm["n10"]["ready"], 2 * KT)
            proj_pe("L1")
            pe.wait_ge(proj["L1"]["stored"], NV["L1"])
            pe.wait_ge(proj["L1"]["taken"], len(units["L1"]))
            proj_pe("UQ")
            pe.wait_ge(proj["UQ"]["stored"], NV["UQ"])
            pe.wait_ge(proj["UQ"]["taken"], len(units["UQ"]))
            att_pe("A1", "UQ")
            out_pe("O1", "A1", sO1, S_LAT)
            norm_pe("n11", S_LAT)
            pe.wait_ge(norm["n11"]["ready"], KT)
            for t in range(2):
                for k in range(KT):
                    pe.matmul(ps[5][:, t * NE:(t + 1) * NE], hT[:, k, t * P:(t + 1) * P], rtr[:, k, :],
                              start=(k == 0), stop=(k == KT - 1)) if not (t == 1 and k == KT - 1) else \
                        pe.matmul(ps[5][:, t * NE:(t + 1) * NE], hT[:, k, t * P:(t + 1) * P], rtr[:, k, :],
                                  start=False, stop=True).then_inc(rt_mm, 1)
            for t in range(2):
                for hh in range(2):
                    for q in range(4):
                        ins = pe.transpose(ps[2 * t + hh][:, q * P:(q + 1) * P],
                                           hT[:, 4 * hh + q, t * P:(t + 1) * P], ident)
                    ins.then_inc(tok_t, 1)
            pe.wait_ge(rt_sel, 1)
            up = cv("upper")
            ch0, ch1 = ro[:, 5, 0, :], ro[:, 5, 1, :]
            pe.matmul(ps[4][:, 0:NE], up, ch0, start=True, stop=True)
            pe.matmul(ps[4][:, NE:2 * NE], ones[:, :], ch0, start=True, stop=False)
            pe.matmul(ps[4][:, NE:2 * NE], up, ch1, start=False, stop=True)
            pe.matmul(ps[4][:, 2 * NE:3 * NE], ones[:, :], ch0, start=True, stop=False)
            pe.matmul(ps[4][:, 2 * NE:3 * NE], ones[:, :], ch1, start=False, stop=True).then_inc(rt_pos, 1)
            pe.wait_ge(tok_rd, 4)
            pe.wait_ge(items_rd, 1)
            total = pe.value_load(nit[0:1, 0:1], min_val=NE, max_val=NE * ROUNDS)
            pe.sem_inc(m_pe, URING)

            def gather(n):
                pe.wait_ge(m_sel, 1 if n is None else n + 1)
                for hh in range(2):
                    for q in range(4):
                        d = 4 * hh + q
                        for t in range(2):
                            ins = pe.matmul(ps[4 + hh][:, q * CAP:(q + 1) * CAP], htok[:, t, d * P:(d + 1) * P],
                                            sel[:, t, :], start=(t == 0), stop=(t == 1))
                    ins.then_inc(m_gat, 1)

            def scatter(n):
                for d in range(KT):
                    if d == 0:
                        pe.wait_ge(m_ya, n + 1)
                        pe.wait_ge(m_yb, n + 1)
                    ins = pe.matmul(ps[d // 2][:, (d % 2) * S_LAT:(d % 2 + 1) * S_LAT],
                                    ytok[:, d * P:(d + 1) * P], pgT[:, :], start=True, stop=True)
                    if d % 2 == 1:
                        ins.then_inc(m_sc, 1)

            gather(None)
            pe.wait_ge(m_init, 1)
            with pe.Fori(0, total) as n:
                for h in range(NU):
                    c, half = h // 2, h % 2
                    hi, lo = whi[:, h % URING, :], wlo[:, h % URING, :]
                    if h == 0:
                        pe.wait_ge(m_xl, n * 2 + 2)
                    pe.wait_ge(m_lo, n * NU + (h + 1))
                    if c < 14:
                        j, part = c // 2, c % 2
                        if part == 0 and half == 0 and j != 1:
                            pe.wait_ge(m_mul, n * 7 + (2 if j == 0 else j + 1))
                        bank = ps[4 + 2 * (j % 2) + part]
                        for k in range(4):
                            kk = 4 * half + k
                            ws = slice(k * 512, (k + 1) * 512)
                            pe.matmul(bank[:, :], xgr[:, 0, kk, :], hi[:, ws], start=(kk == 0), stop=False)
                            pe.matmul(bank[:, :], xgr[:, 0, kk, :], lo[:, ws], start=False, stop=False)
                            ins = pe.matmul(bank[:, :], xgr[:, 1, kk, :], hi[:, ws], start=False, stop=(kk == KT - 1))
                        ins.then_inc(m_pe, 1)
                    else:
                        j = c - 14
                        if h == 28:
                            pe.wait_ge(m_pg, n + 1)
                        if half == 0:
                            pe.wait_ge(m_hl, n * 7 + (j + 1))
                        for q in range(2):
                            f = QF * j + 2 * half + q
                            for z in range(2):
                                ws = slice(q * D + z * 512, q * D + z * 512 + 512)
                                pe.matmul(ps[z][:, :], hidr[:, 0, f, :], hi[:, ws], start=(f == 0), stop=False)
                                pe.matmul(ps[z][:, :], hidr[:, 0, f, :], lo[:, ws], start=False, stop=False)
                                ins = pe.matmul(ps[z][:, :], hidr[:, 1, f, :], hi[:, ws], start=False,
                                                stop=(f == FTE - 1))
                        ins.then_inc(m_pe, 1)
                    if h == 1:
                        scatter(n)
                    if h == 12:
                        pe.wait_ge(m_gsel, n + 1)
                        pe.wait_ge(m_add, n + 1)
                        for t in range(2):
                            ins = pe.transpose(ps[0][:, t * P:(t + 1) * P], gsel[:, t, :], ident)
                        ins.then_inc(m_pgt, 1)
                    j = (h - 6) // 4
                    if h % 4 == 2 and 0 <= j < 7:
                        pe.wait_ge(m_mul, n * 7 + (j + 3))
                        if j < 2:
                            pe.wait_ge(m_add, n + 1)
                        else:
                            pe.wait_ge(m_hl, n * 7 + (j - 1))
                        for q in range(QF):
                            ins = pe.transpose(ps[2 + j % 2][:, q * P:(q + 1) * P], hidtok[:, j % 2, q * P:(q + 1) * P],
                                               ident)
                        ins.then_inc(m_t, 1)
                    if h == 32:
                        pe.wait_ge(m_mul, n * 7 + 9)
                        gather(n + 1)
            scatter(total)


def kernel(**inputs):
    import concourse.bacc as _bacc
    from concourse.bass_utils import run_bass_kernel_spmd as _run

    x = {k: np.asarray(v) for k, v in inputs.items()}

    def tiles(v):
        v = v.reshape(v.shape[:-1] + (v.shape[-1] // P, P))
        return np.moveaxis(v, -1, 0)

    rpb = np.zeros((8, RPB_DR, 2 * GRID_W - 1), np.float32)
    lo = GRID_W - NA_WIN_W
    rpb[:, :, lo:lo + 2 * NA_WIN_W - 1] = x["na_rpb"][0][:, NA_WIN_H - 4:NA_WIN_H + 3]
    rpb = np.tile(rpb, (1, 1, GRID_W))
    arrays = {
        "xT": x["x"][0].T, "ctxT": x["ctx"][0].T,
        "cond": tiles(np.stack([x["c"][0], x["c_ctx"]])).transpose(0, 2, 1).reshape(P, 16),
        "adab": tiles(x["ada_b"]).reshape(P, 96),
        "ng": tiles(np.stack([x["norm1_g"], x["norm2_g"]])).reshape(P, 32),
        "vec": np.concatenate([x[n].reshape(-1) for n, _ in VEC]),
        "cst": shape_constants(), "rpb": rpb,
        "ada_w": x["ada_w"], "moe_router": x["moe_router"][0],
    }
    for n in ("ev_w_in", "ev_w_out", "ffn_w_gate", "ffn_w_up", "ffn_w_down", "od_w_in", "od_w_out",
              "mla_w_uq", "mla_w_ukv", "moe_w1", "moe_w3", "moe_w2"):
        arrays[n] = x[n][0]
    nc = _bacc.Bacc("TRN2", target_bir_lowering=False, num_devices=1)
    feed, aps = {}, {}
    for n, v in arrays.items():
        v = np.ascontiguousarray(v)
        feed[f"in_{n}"] = v
        aps[n] = nc.dram_tensor(f"in_{n}", v.shape, F32, kind="ExternalInput").ap()
    o = nc.dram_tensor("out_T", (D, S_LAT), F32, kind="ExternalOutput").ap()
    build_kernel(nc, aps, o)
    r = _run(nc, [feed], core_ids=[0])
    return np.ascontiguousarray(r.results[0]["out_T"].T)[None]
```

```python
import math
from contextlib import ExitStack

import numpy as np

import concourse.bass as bass
from concourse import mybir

F32 = mybir.dt.float32
F32R = mybir.dt.float32r
I32 = mybir.dt.int32
ALU = mybir.AluOpType
ACT = mybir.ActivationFunctionType
AX = mybir.AxisListType

P = 128
D = 1024
KT = D // P
S_LAT = 256
S_ALL = 512
GRID_W = 64
HD = 64
NA_WIN_W = 16
NA_WIN_H = 8
ROPE_THETA = 10000.0
EPS = 1e-6
NEG = -1e30
D_FF = 2816
FT = D_FF // P
D_FFE = 3584
FTE = D_FFE // P
NE = 8
MLA_QK, MLA_NOPE, MLA_ROPE = 96, 64, 32
RPB_DR = 7
RPB_ROW = (2 * GRID_W - 1) * GRID_W
CAP = 128
ROUNDS = -(-S_LAT // CAP)
LAM_INIT = 0.8 - 0.6 * math.exp(-0.3 * 0)

RING = 4
SLOT = 4096
MRING = 3
UNIT = SLOT // 2
NU = 42
URING = 3
MCH = 21
HALF_T = (12, 10)
NUF = 4 * (FT // 2) + 4 * 8
UF = 2
FU = 1024
QF = 4

VEC = [("na_q_g", 64), ("na_k_g", 64), ("diff_q_g", 64), ("diff_k_g", 64), ("gqa_q_g", 64),
       ("gqa_k_g", 64), ("mla_cq_g", 256), ("mla_ckv_g", 128), ("mla_q_g", 96), ("mla_k_g", 96),
       ("diff_subln_g", 128), ("diff_lq1", 64), ("diff_lk1", 64), ("diff_lq2", 64), ("diff_lk2", 64)]
VEC_AT = {}
_o = 0
for _n, _w in VEC:
    VEC_AT[_n] = (_o, _w)
    _o += _w
VEC_N = _o

CST = [("ident", 128), ("upper", 128), ("iota", CAP), ("rope64", 256), ("rope32", 128),
       ("mask", 64), ("rank", 8)]
CST_AT = {}
_o = 0
for _n, _w in CST:
    CST_AT[_n] = (_o, _w)
    _o += _w
CST_N = _o


def rope_table(dim, tile):
    pos = np.arange(tile * P, tile * P + P)
    half = dim // 4
    freqs = (ROPE_THETA ** (-np.arange(half, dtype=np.float32) / half)).astype(np.float32)
    cos, sin = [], []
    for p in (pos // GRID_W, pos % GRID_W):
        ang = (p.astype(np.float32)[:, None] * freqs[None, :]).astype(np.float32)
        c, s = np.cos(ang), np.sin(ang)
        cos += [c, c]
        sin += [-s, s]
    return np.concatenate(cos + sin, axis=1).astype(np.float32)


def shape_constants():
    c = np.zeros((P, CST_N), np.float32)

    def put(name, a):
        o, w = CST_AT[name]
        c[:, o:o + w] = a

    i = np.arange(P)
    put("ident", np.eye(P))
    put("upper", (i[:, None] < i[None, :]))
    put("iota", np.broadcast_to(np.arange(CAP), (P, CAP)))
    put("rope64", np.concatenate([rope_table(64, 0), rope_table(64, 1)], axis=1))
    put("rope32", np.concatenate([rope_table(32, 0), rope_table(32, 1)], axis=1))
    col = np.arange(GRID_W)
    c0 = np.clip(col - NA_WIN_W // 2, 0, GRID_W - NA_WIN_W)
    inside = (col[None, :] >= c0[:, None]) & (col[None, :] < c0[:, None] + NA_WIN_W)
    put("mask", np.tile(np.where(inside, 0.0, NEG), (2, 1)))
    put("rank", np.broadcast_to(NE - np.arange(NE), (P, NE)))
    return c


class Chain:

    def __init__(self, eng, sem, reg=None, per=0):
        self.eng, self.sem, self.reg, self.per, self.n = eng, sem, reg, per, 0

    def after(self, ins):
        ins.then_inc(self.sem, 1)
        self.n += 1
        self.eng.wait_ge(self.sem, self.n if self.reg is None else self.reg * self.per + self.n)


def build_kernel(nc, a, out):
    with ExitStack() as ctx:
        def sb(name, shape, dt=F32):
            return ctx.enter_context(nc.sbuf_tensor(name, shape, dt))

        def sem(name):
            return ctx.enter_context(nc.semaphore(name))

        xT = sb("xT", [P, KT, S_ALL])
        cst = sb("cst", [P, CST_N])
        vec = sb("vec", [P, VEC_N])
        ones = sb("ones", [P, P])
        cond = sb("cond", [P, 16])
        scond = sb("scond", [P, 16])
        adab = sb("adab", [P, 2, 48])
        ng = sb("ng", [P, 2, 2, KT])
        ada = sb("ada", [P, 2, 48, 2])
        amod = sb("amod", [P, 2, 2, KT, 2])
        ss = sb("ss", [P, 4, 8])
        rt8 = sb("rt8", [P, 4, 8])
        rs8 = sb("rs8", [P, 4, 8])
        krt = sb("krt", [P, 4, 32])
        eps = sb("eps", [P, 1])
        mx = sb("mx", [P, 64])
        nmx = sb("nmx", [P, 64])
        sums = sb("sums", [P, 64])
        rsum = sb("rsum", [P, 64])
        lamt = sb("lamt", [P, 8])
        rtr = sb("rtr", [P, KT, NE])
        nit = sb("nit", [P, 1], I32)
        ring012 = sb("ring", [P, RING - 1, SLOT])
        with ExitStack() as scope:
            bt = scope.enter_context(nc.sbuf_tensor("bt", [P, 8, 6, GRID_W], F32))
        with ExitStack() as scope:
            fsa = scope.enter_context(nc.sbuf_tensor("fsa", [P, 3, FU], F32R))
        etab = sb("etab", [P, 3 * FU])
        with ExitStack() as early:
            ring3 = early.enter_context(nc.sbuf_tensor("ring3", [P, SLOT], F32))
            work = early.enter_context(nc.sbuf_tensor("work", [P, 16384], F32))
            hT = early.enter_context(nc.sbuf_tensor("hT", [P, KT, S_ALL], F32))
            scr = early.enter_context(nc.sbuf_tensor("scr", [P, 11, 512], F32))
        with ExitStack() as dense:
            dense.enter_context(nc.sbuf_tensor("ring3_kept", [P, SLOT], F32))
            hTl = dense.enter_context(nc.sbuf_tensor("hTl", [P, KT, S_ALL], F32R))
            hidh = dense.enter_context(nc.sbuf_tensor("hidh", [P, HALF_T[0], S_ALL], F32R))
            hidl = dense.enter_context(nc.sbuf_tensor("hidl", [P, HALF_T[0], S_ALL], F32R))
            hTh = dense.enter_context(nc.sbuf_tensor("hTh", [P, KT, S_ALL], F32R))
            dense.enter_context(nc.sbuf_tensor("scr_kept", [P, 6, 512], F32))
            fsb = dense.enter_context(nc.sbuf_tensor("fsb", [P, FU], F32R))
        assert 16384 == (KT + 2 * HALF_T[0]) * S_ALL
        whi = sb("whi", [P, URING, UNIT], F32R)
        wlo = sb("wlo", [P, URING, UNIT], F32R)
        hidr = sb("hidr", [P, 2, FTE, CAP], F32R)
        xgr = sb("xgr", [P, 2, KT, CAP], F32R)
        ytok = sb("ytok", [P, D])
        pgT = sb("pgT", [P, S_LAT])
        hidtok = sb("hidtok", [P, 2, QF * P])
        sg = sb("sg", [P, 2, QF * P])
        sel = sb("sel", [P, 2, CAP])
        gsel = sb("gsel", [P, 2, CAP])
        ps = [ctx.enter_context(nc.psum_tensor(f"ps{b}", [P, 512], F32)) for b in range(8)]

        def cv(name, lo=0, hi=None):
            o, w = CST_AT[name]
            return cst[:, o + lo:o + (w if hi is None else hi)]

        def vv(name):
            o, w = VEC_AT[name]
            return vec[:, o:o + w]

        ident = cv("ident")

        def rope_of(dim, tile):
            o = tile * 2 * dim
            n = "rope64" if dim == 64 else "rope32"
            return cv(n, o, o + dim), cv(n, o + dim, o + 2 * dim)

        def area(o, *dims):
            n = int(np.prod(dims))
            v = work[:, o:o + n]
            if len(dims) == 2:
                v = v.rearrange("p (a b) -> p a b", b=dims[1])
            if len(dims) == 3:
                v = v.rearrange("p (a b c) -> p a b c", b=dims[1], c=dims[2])
            return v

        QT0 = [area(2048 * j, 4, S_ALL) for j in range(4)]
        V0 = area(8192, 4, 1024)
        O0 = area(12288, 4, 1024)
        hraw = area(4096, KT, S_ALL)
        QcT = area(0, 4, S_LAT)
        KcT = area(1024, 2, S_ALL)
        QdT = area(2048, 8, S_LAT)
        KdT = area(4096, 8, S_ALL)
        Vc = area(8192, 4, 128)
        Vd = area(8704, 4, 512)
        cqT = area(10752, 2, S_LAT)
        ckvT = area(11264, 1, S_ALL)[:, 0, :]
        O1 = area(12288, 2, 1024)
        btf = etab[:, :]
        htok = btf[:, 0:2 * D].rearrange("p (a b) -> p a b", b=D)
        NI = ROUNDS * NE + 1

        def tail(o, *dims):
            n = int(np.prod(dims))
            v = btf[:, 2 * D + o:2 * D + o + n]
            if len(dims) == 2:
                return v.rearrange("p (a b) -> p a b", b=dims[1])
            return v.rearrange("p (a b c) -> p a b c", b=dims[1], c=dims[2])

        ro = tail(0, 24, 2, NE)
        posr = tail(384, 2, NI)
        gat = tail(384 + 2 * NI, 2, NI)
        chs = tail(384 + 4 * NI, 2, NI)
        kn = tail(384 + 6 * NI, 3, P)
        mslot = [ring012[:, i, :] for i in (1, 2, 0)]

        sq = [scr[:, i, :] for i in range(4)]
        rt, rstd = scr[:, 4, :], scr[:, 5, :]
        tn = [scr[:, 6 + i, :] for i in range(3)]
        acc = scr[:, 2:6, :]
        adar = scr[:, 6:8, :]
        ra, rb = scr[:, 9, :], scr[:, 10, :]
        prob = [scr[:, 2 + i, :] for i in range(4)]
        hbuf = [scr[:, 8 + i, :] for i in range(2)]
        uhi, ulo = [fsa[:, 0, :], fsa[:, 1, :]], [fsa[:, 2, :], fsb[:, :]]
        probT = [scr[:, 9 + i, :] for i in range(2)]
        kda = [scr[:, 2 + i, 0:384].rearrange("p (h d) -> p h d", d=MLA_QK) for i in range(2)]

        order = [("A0a", j) for j in range(4)]
        order += [("W0", 0), ("A0b", 0), ("A0b", 1), ("W0", 1), ("A0b", 2), ("W0", 2), ("A0b", 3), ("A0b", 4),
                  ("W0", 3), ("A0b", 5), ("W0", 4), ("A0b", 6), ("A0b", 7), ("W0", 5), ("O0", 0), ("O0", 1)]
        for j in range(FT // 2):
            order += [("F0", j), ("A1", j)]
            if j == 5:
                order += [("D0", q) for q in range(4)]
        order += [("A1", FT // 2)] + [("D0", j) for j in range(4, 8)]
        order += [("W1", 0), ("W1", 1), ("W1", 2), ("U1", 0), ("O1", 0), ("O1", 1)]
        at = {nj: g for g, nj in enumerate(order)}
        PRE = len(order)

        def slot_of(g):
            return g % RING

        def rslot(g):
            return ring3[:, :] if slot_of(g) == RING - 1 else ring012[:, slot_of(g), :]

        def slot3(g, w):
            return rslot(g).rearrange("p (a b) -> p a b", b=w)

        def loads_upto(g):
            return sum(2 if order[q][0] in ("F0", "U1") else 1 for q in range(slot_of(g), g + 1, RING))

        s_x = sem("x_loaded")
        s_cond = sem("conditioning_loaded")
        s_cst = sem("constants_loaded")
        eps_set = sem("eps_set")
        s_bt = sem("bias_loaded")
        s_ones = sem("ones_set")
        slot_full = [sem(f"slot_full{i}") for i in range(RING)]
        ada_used = sem("modulation_chunks_used")
        ada_row = sem("modulation_rows_copied")
        ada_tr = sem("modulation_rows_turned")
        ada_rd = sem("modulation_turns_taken")
        acc_st = sem("modulation_partial_steps")
        acc_rd = sem("modulation_partials_ready")
        sum_rd = sem("modulation_sums_done")
        take_rd = sem("modulation_sums_taken")
        mslot_full = [sem(f"expert_slot_full{i}") for i in range(MRING)]
        s_scond = sem("silu_cond_ready")
        d_step = sem("dve_step")
        p_step = sem("pool_step")
        a_step = sem("act_step")
        gain_rd = sem("gains_prepared")
        lam_in = sem("lambda_dots_ready")
        lam_ex = sem("lambda_exps_ready")
        norm = {}
        for nm in ("n00", "n01", "n10", "n11"):
            norm[nm] = {k: sem(f"{nm}_{k}") for k in ("square", "summed", "root", "scaled", "ready")}
        n01_low = sem("n01_low_parts_ready")
        proj = {}
        for nm in ("L0", "L1", "UQ"):
            proj[nm] = {k: sem(f"proj{nm}_{k}") for k in
                        ("done", "squared", "reduced", "root", "taken", "normed", "rotated", "turned", "stored")}
        att = {}
        for nm in ("A0", "A1"):
            att[nm] = {k: sem(f"att{nm}_{k}") for k in
                       ("score", "max", "exp", "mixed", "turned", "copied", "pv", "out", "osq", "ored",
                        "oroot", "otok", "oturned", "ostored")}
        outp = {}
        for nm in ("O0", "O1"):
            outp[nm] = {k: sem(f"out{nm}_{k}") for k in ("done", "added")}
        f_hi = sem("ffn_unit_high_ready")
        f_lo = sem("ffn_unit_low_ready")
        f_used = sem("ffn_unit_used")
        silu_rd = sem("ffn_silu_ready")
        mul_rd = sem("ffn_hidden_multiplied")
        f_hh = sem("ffn_hidden_high_ready")
        f_hl = sem("ffn_hidden_low_ready")
        dn_add = sem("ffn_down_added")
        tok_t = sem("expert_tokens_turned")
        tok_rd = sem("expert_tokens_ready")
        rt_mm = sem("router_logits_done")
        rt_sel = sem("router_choice_ready")
        rt_ein = sem("router_exp_in")
        rt_ex = sem("router_exp_ready")
        rt_pos = sem("router_positions_done")
        items_rd = sem("item_count_ready")
        m_init = sem("expert_buffers_cleared")
        m_sel = sem("expert_select_ready")
        m_gat = sem("expert_gathered")
        m_xh = sem("expert_tokens_high_ready")
        m_xl = sem("expert_tokens_low_ready")
        m_gsel = sem("expert_gates_ready")
        m_pgt = sem("expert_gates_turned")
        m_pg = sem("expert_gates_copied")
        m_hi = sem("unit_high_ready")
        m_lo = sem("unit_low_ready")
        m_pe = sem("unit_used")
        m_silu = sem("expert_silu_ready")
        m_mul = sem("expert_hidden_ready")
        m_t = sem("expert_hidden_turned")
        m_hh = sem("expert_hidden_high_ready")
        m_hl = sem("expert_hidden_low_ready")
        m_ya = sem("expert_sum_copied_by_act")
        m_yb = sem("expert_sum_copied_by_dve")
        m_sc = sem("expert_scattered")
        m_add = sem("expert_added")
        s_out = sem("output_stored")

        def first_unit(nm, j):
            if nm == "F0":
                return 4 * j + (16 if j >= 6 else 0)
            return 24 + 4 * j + (20 if j >= 4 else 0)

        unit_src = []
        gate_at, up_at, down_at = {}, {}, {}
        for nm, js in (("F0", range(0, 6)), ("D0", range(0, 4)), ("F0", range(6, 11)), ("D0", range(4, 8))):
            for j in js:
                assert first_unit(nm, j) == len(unit_src)
                for q in range(2):
                    for z in range(2):
                        cs = slice(q * P, (q + 1) * P)
                        if nm == "F0":
                            w = slot3(at[nm, j], 256)[:, KT * z:KT * (z + 1), cs]
                            (gate_at, up_at)[z][len(unit_src)] = 2 * j + q
                        else:
                            n = HALF_T[j // 4] // 2
                            w = slot3(at[nm, j], 256)[:, n * z:n * (z + 1), cs]
                            if z == 1:
                                down_at[len(unit_src)] = 2 * j + q
                        unit_src.append((at[nm, j], w))
        assert len(unit_src) == NUF

        def kept(f):
            return f if f < HALF_T[0] else f - HALF_T[0]

        def unit_parts(u):
            n = unit_src[u][1].shape[1] * P
            return tuple(b[u % UF][:, 0:n].rearrange("p (k n) -> p k n", n=P) for b in (uhi, ulo))

        released = {}
        for j in range(4):
            released[at["A0a", j]] = (ada_used, j + 1)
        for j in range(8):
            released[at["A0b", j]] = (acc_rd, j + 1)
        for j in range(12):
            released[at["A1", j]] = (acc_rd, 8 + j + 1)
        for j in range(6):
            released[at["W0", j]] = (proj["L0"]["done"], 4 * j + 4)
        for j, n in enumerate((2, 6, 10)):
            released[at["W1", j]] = (proj["L1"]["done"], n)
        released[at["U1", 0]] = (proj["UQ"]["done"], 12)
        for nm in ("O0", "O1"):
            for j in range(2):
                released[at[nm, j]] = (outp[nm]["done"], 4 * j + 4)
        for j in range(11):
            released[at["F0", j]] = (f_lo, first_unit("F0", j) + 4)
        for j in range(8):
            released[at["D0", j]] = (f_lo, first_unit("D0", j) + 4)

        def head_unit(kind, g, t, lhs, w, width, bank, **kw):
            return dict(kind=kind, g=g, t=t, lhs=lhs, w=w, width=width, bank=bank, **kw)

        def v3(ap, b):
            return ap.rearrange("p (a b) -> p a b", b=b)

        units = {"L0": [], "L1": [], "UQ": []}
        nv = 0
        for j in range(6):
            for t in range(4):
                u = len(units["L0"])
                g = at["W0", j]
                un = dict(g=g, t=t, lhs=[hT[:, k, t * P:(t + 1) * P] for k in range(KT)],
                          w=[slot3(g, 512)[:, k, :] for k in range(KT)], width=512, bank=u % 4,
                          last=(t == 3), copies=[], groups=[])
                if j in (2, 5):
                    c0 = 0 if j == 2 else 512
                    un["copies"] = [(V0[:, t, c0:c0 + 512], ps[u % 4][:, :])]
                else:
                    q = {0: 0, 1: 1, 3: 2, 4: 3}[j]
                    nm = ("na_q_g", "na_k_g", "diff_q_g", "diff_k_g")[q]
                    tb = tn[nv % 3]
                    un["sq"] = ps[u % 4][:, :]
                    un["groups"] = [dict(src=v3(ps[u % 4][:, :], HD), sq=(0, 512), nh=8, hd=HD, dst=v3(tb, HD),
                                         gain=vv(nm), outs=[v3(tb, HD)],
                                         rope=(rope_of(64, t) + (0, 64)) if (q >= 2 and t < 2) else None)]
                    un["turn"] = [tb[:, c * P:(c + 1) * P] for c in range(4)]
                    un["store"] = (QT0[q][:, :, t * P:(t + 1) * P], P)
                    nv += 1
                units["L0"].append(un)
        nv = 0
        for c, t in [(0, 0), (0, 1)] + [(1, t) for t in range(4)] + [(2, t) for t in range(4)]:
            u = len(units["L1"])
            b = u % 4
            g = at["W1", c]
            tb = tn[nv % 3]
            width = (512, 512 if t < 2 else 256, 160)[c]
            wv = slot3(g, 512) if c < 2 else rslot(g)[:, 0:KT * 160].rearrange("p (a b) -> p a b", b=160)
            un = dict(g=g, t=t, lhs=[hT[:, k, t * P:(t + 1) * P] for k in range(KT)],
                      w=[wv[:, k, 0:width] for k in range(KT)], width=width, bank=b,
                      last=(t == (1 if c == 0 else 3)), copies=[], groups=[], sq=ps[b][:, 0:min(width, 512)])
            if c == 0:
                un["groups"] = [dict(src=v3(ps[b][:, :], HD), sq=(0, 512), nh=8, hd=HD, dst=v3(tb, HD),
                                     gain=vv("gqa_q_g"), outs=[v3(tb, HD)], rope=rope_of(64, t) + (0, 64))]
                un["turn"] = [tb[:, i * P:(i + 1) * P] for i in range(4)]
                un["store"] = (QcT[:, :, t * P:(t + 1) * P], P)
            elif c == 1:
                kb = kn[:, nv % 3, :]
                dup = tb[:, 0:256].rearrange("p (v c d) -> p c v d", c=2, d=HD)
                un["copies"] = [(Vc[:, t, :], ps[b][:, 128:256])]
                un["groups"] = [dict(src=v3(ps[b][:, 0:128], HD), sq=(0, 128), nh=2, hd=HD, dst=v3(kb, HD),
                                     gain=vv("gqa_k_g"), outs=[dup[:, 0], dup[:, 1]],
                                     rope=(rope_of(64, t) + (0, 64)) if t < 2 else None)]
                un["turn"] = [tb[:, 0:128], tb[:, 128:256]]
                un["store"] = (KcT[:, :, t * P:(t + 1) * P], P)
                if t < 2:
                    cq = tb[:, 256:512].unsqueeze(1)
                    un["groups"].append(dict(src=ps[b][:, 256:512].unsqueeze(1), sq=(256, 512), nh=1, hd=256,
                                             dst=cq, gain=vv("mla_cq_g"), outs=[cq], rope=None))
                    un["turn"] += [tb[:, 256:384], tb[:, 384:512]]
                    un["store2"] = (cqT[:, :, t * P:(t + 1) * P], 2)
            else:
                ck = tb[:, 0:128].unsqueeze(1)
                un["copies"] = [(krt[:, t, :], ps[b][:, 128:160])]
                un["groups"] = [dict(src=ps[b][:, 0:128].unsqueeze(1), sq=(0, 128), nh=1, hd=128, dst=ck,
                                     gain=vv("mla_ckv_g"), outs=[ck], rope=None)]
                un["turn"] = [tb[:, 0:128]]
                un["store"] = (ckvT[:, t * P:(t + 1) * P].unsqueeze(1), P)
            units["L1"].append(un)
            nv += 1
        nv = 0
        uqw = rslot(at["U1", 0])[:, 0:1536].rearrange("p (k n) -> p k n", k=2)
        ukvw = rslot(at["U1", 0])[:, 1536:2560]
        for t in range(2):
            for hh in range(2):
                u = len(units["UQ"])
                b = u % 4
                tb = tn[nv % 3][:, 0:384].rearrange("p (h d) -> p h d", d=MLA_QK)
                units["UQ"].append(dict(
                    g=at["U1", 0], lhs=[cqT[:, k, t * P:(t + 1) * P] for k in range(2)],
                    w=[uqw[:, k, hh * 384:(hh + 1) * 384] for k in range(2)], width=384, bank=b, last=False,
                    copies=[], sq=ps[b][:, 0:384],
                    groups=[dict(src=ps[b][:, 0:384].rearrange("p (h d) -> p h d", d=MLA_QK), sq=(0, 384), nh=4,
                                 hd=MLA_QK, dst=tb, gain=vv("mla_q_g"), outs=[tb],
                                 rope=rope_of(32, t) + (MLA_NOPE, 32))],
                    turn=[tb[:, i, :] for i in range(4)],
                    store=(QdT[0:MLA_QK, hh * 4:hh * 4 + 4, t * P:(t + 1) * P], MLA_QK)))
                nv += 1
        for t in range(4):
            for hh in range(2):
                u = len(units["UQ"])
                b = u % 4
                tb = tn[nv % 3][:, 0:384].rearrange("p (h d) -> p h d", d=MLA_QK)
                kd = kda[nv % 2]
                pv = ps[b][:, :].rearrange("p (h d) -> p h d", d=128)
                units["UQ"].append(dict(
                    g=at["U1", 0], lhs=[ckvT[:, t * P:(t + 1) * P]], w=[ukvw[:, hh * 512:(hh + 1) * 512]],
                    width=512, bank=b, last=(t == 3 and hh == 1),
                    copies=[(kd[:, :, 0:MLA_NOPE], pv[:, :, 0:64]),
                            (kd[:, :, MLA_NOPE:], krt[:, t, :].unsqueeze(1).to_broadcast([P, 4, 32])),
                            (Vd[:, t, hh * 256:(hh + 1) * 256].rearrange("p (h d) -> p h d", d=64), pv[:, :, 64:128])],
                    assembled=True,
                    sq=kd.rearrange("p h d -> p (h d)"),
                    groups=[dict(src=kd, sq=(0, 384), nh=4, hd=MLA_QK, dst=tb, gain=vv("mla_k_g"), outs=[tb],
                                 rope=(rope_of(32, t) + (MLA_NOPE, 32)) if t < 2 else None)],
                    turn=[tb[:, i, :] for i in range(4)],
                    store=(KdT[0:MLA_QK, hh * 4:hh * 4 + 4, t * P:(t + 1) * P], MLA_QK)))
                nv += 1
        for us in units.values():
            v = na = 0
            for un in us:
                if un.get("assembled"):
                    na += 1
                    un["nth_assembled"] = na
                un["x"] = next(i for i, o in enumerate(us) if o is un)
                if un["groups"]:
                    un["v"] = v
                    v += 1
        NV = {nm: sum(1 for u in us if u["groups"]) for nm, us in units.items()}
        LAGT = 2

        def att_plan(layer):
            items, pvs, groups = [], [], []
            tiles = range(4) if layer == 0 else range(2)
            for t in tiles:
                nk = 512 if t < 2 else 256
                k0 = 0 if t < 2 else 256
                kts = range(k0 // P, 4)
                for half in range(2):
                    gp = dict(t=t, half=half)
                    if layer == 0 and half == 0:
                        for h in range(8):
                            rows = slice(64 * (h % 2), 64 * (h % 2) + 64)
                            items.append(dict(q=QT0[0][rows, h // 2, t * P:(t + 1) * P],
                                              k=QT0[1][rows, h // 2, k0:512], nk=nk, scale=1.0,
                                              bias=bt[:, h, 2 - 2 * t:6 - 2 * t, :] if t < 2 else None))
                            pvs.append(dict(items=[len(items) - 1], nk=nk, ob=4 + len(pvs) % 2, dv=64,
                                            v=[V0[:, kt, h * 64:h * 64 + 64] for kt in kts],
                                            dst=O0[:, t, h * 64:h * 64 + 64]))
                    elif layer == 0:
                        for h in range(4):
                            for m in range(2):
                                rows = slice(64 * m, 64 * m + 64)
                                items.append(dict(q=QT0[2][rows, h, t * P:(t + 1) * P],
                                                  k=QT0[3][rows, h, k0:512], nk=nk, scale=1.0, bias=None))
                            pvs.append(dict(items=[len(items) - 2, len(items) - 1], nk=nk, ob=4 + len(pvs) % 2,
                                            dv=128, v=[V0[:, kt, 512 + h * 128:512 + h * 128 + 128] for kt in kts],
                                            dst=O0[:, t, 512 + h * 128:512 + h * 128 + 128]))
                    elif half == 0:
                        for h in range(8):
                            rows = slice(64 * (h % 2), 64 * (h % 2) + 64)
                            kv = h // 4
                            items.append(dict(q=QcT[rows, h // 2, t * P:(t + 1) * P], k=KcT[rows, kv, :], nk=nk,
                                              scale=1.0, bias=None))
                            pvs.append(dict(items=[len(items) - 1], nk=nk, ob=4 + len(pvs) % 2, dv=64,
                                            v=[Vc[:, kt, kv * 64:kv * 64 + 64] for kt in kts],
                                            dst=O1[:, t, h * 64:h * 64 + 64]))
                    else:
                        for h in range(8):
                            items.append(dict(q=QdT[0:MLA_QK, h, t * P:(t + 1) * P], k=KdT[0:MLA_QK, h, :], nk=nk,
                                              scale=float(MLA_QK) ** -0.5, bias=None))
                            pvs.append(dict(items=[len(items) - 1], nk=nk, ob=4 + len(pvs) % 2, dv=64,
                                            v=[Vd[:, kt, h * 64:h * 64 + 64] for kt in kts],
                                            dst=O1[:, t, 512 + h * 64:512 + h * 64 + 64]))
                    gp["pv1"] = len(pvs)
                    gp["sub"] = layer == 0 and half == 1
                    gp["otok"] = (O0 if layer == 0 else O1)[:, t, half * 512:(half + 1) * 512]
                    groups.append(gp)
            for j, pv in enumerate(pvs):
                for i in pv["items"]:
                    items[i]["pv"] = j
            for gi, gp in enumerate(groups):
                gp["e"] = gi
                gp["subs_upto"] = sum(1 for q in groups[:gi + 1] if q["sub"])
            return dict(items=items, pvs=pvs, groups=groups)

        plans = {"A0": att_plan(0), "A1": att_plan(1)}
        SBANK = (0, 1, 7)
        DONE_AT = 6

        def closes(pl, i):
            return [gp for gp in pl["groups"] if pl["pvs"][gp["pv1"] - 1]["items"][-1] == i - DONE_AT]

        def pv_at(pl, i):
            return [j for j, pv in enumerate(pl["pvs"]) if pv["items"][-1] == i]

        NSTEP = {nm: len(pl["items"]) + DONE_AT + 2 for nm, pl in plans.items()}

        block = ctx.enter_context(nc.Block())

        @block.sync
        def _(sp):
            def load(g, dst, src, wait=True):
                if g >= RING and wait:
                    sp.wait_ge(*released[g - RING])
                sp.dma_start(dst, src).then_inc(slot_full[slot_of(g)], 16)

            def cols(w, c0, n):
                return w[:, c0:c0 + n].rearrange("(k p) n -> p k n", p=P)

            sp.dma_start(cond[:, :], a["cond"]).then_inc(s_cond, 16)
            sp.dma_start(xT[:, :, 0:S_LAT], a["xT"].rearrange("(k p) n -> p k n", p=P)).then_inc(s_x, 16)
            sp.dma_start(xT[:, :, S_LAT:S_ALL], a["ctxT"].rearrange("(k p) n -> p k n", p=P)).then_inc(s_x, 16)
            square = {"A0a": (a["ada_w"][0], 0), "A0b": (a["ada_w"][0], 2048), "A1": (a["ada_w"][1], 0),
                      "W0": (a["ev_w_in"], 0), "O0": (a["ev_w_out"], 0), "W1": (a["od_w_in"], 0),
                      "O1": (a["od_w_out"], 0)}
            for g, (nm, j) in enumerate(order):
                if (nm, j) == ("W1", 2):
                    load(g, rslot(g)[:, 0:KT * 160].rearrange("p (a b) -> p a b", b=160), cols(a["od_w_in"], 1024, 160))
                elif nm in square:
                    w, c0 = square[nm]
                    load(g, slot3(g, 512), cols(w, c0 + 512 * j, 512))
                elif nm == "F0":
                    load(g, slot3(g, 256)[:, 0:KT, :], cols(a["ffn_w_gate"], 256 * j, 256))
                    load(g, slot3(g, 256)[:, KT:2 * KT, :], cols(a["ffn_w_up"], 256 * j, 256), wait=False)
                elif nm == "D0":
                    r0 = (j // 4) * HALF_T[0] * P
                    rows = slice(r0, r0 + HALF_T[j // 4] * P)
                    load(g, slot3(g, 256)[:, 0:HALF_T[j // 4], :],
                         a["ffn_w_down"][rows, 256 * (j % 4):256 * (j % 4 + 1)].rearrange("(f p) n -> p f n", p=P))
                else:
                    load(g, uqw, a["mla_w_uq"].rearrange("(k p) n -> p k n", p=P))
                    load(g, ukvw, a["mla_w_ukv"], wait=False)

            w13 = [a[n].rearrange("e (k p) (c n) -> e c p k n", p=P, n=QF * P) for n in ("moe_w1", "moe_w3")]
            w2 = a["moe_w2"].rearrange("e (c f p) n -> e c p f n", p=P, f=QF)

            def expert_chunk(e, c):
                m = mslot[c % MRING]
                if c < 14:
                    return m.rearrange("p (a b) -> p a b", b=QF * P), w13[c % 2][e, c // 2]
                return m.rearrange("p (a b) -> p a b", b=D), w2[e, c - 14]

            def expert_load(e, c, sem_, value):
                sp.wait_ge(sem_, value)
                dst, src = expert_chunk(e, c)
                sp.dma_start(dst, src).then_inc(mslot_full[c % MRING], 16)

            for c in range(MCH):
                if c < MRING:
                    expert_load(0, c, *released[PRE - 1 - (3, 2, 0)[c]])
                else:
                    expert_load(0, c, m_lo, 2 * (c - MRING) + 2)
            sp.wait_ge(items_rd, 1)
            total = sp.value_load(nit[0:1, 0:1], min_val=NE, max_val=NE * ROUNDS)
            with sp.Fori(1, total) as n:
                e = n % NE
                for c in range(MCH):
                    expert_load(e, c, m_lo, n * NU + 2 * (c - MRING) + 2)
            sp.wait_ge(m_add, total + 1)
            sp.dma_start(out.rearrange("(k p) n -> p k n", p=P), xT[:, :, 0:S_LAT]).then_inc(s_out, 16)
            sp.wait_ge(s_out, 16)

        @block.gpsimd
        def _(pool):
            ch = Chain(pool, p_step)
            pool.memset(ones[:, :], 1.0).then_inc(s_ones, 1)
            rp = a["rpb"]
            pool.wait_ge(slot_full[3], 16)
            for rr in range(2):
                for h in range(8):
                    off = (h * RPB_DR + 1 - rr) * RPB_ROW + GRID_W - 1
                    pool.dma_start(bt[rr * 64:rr * 64 + 64, h, :, :],
                                   bass.AP(rp.tensor, off, [[2 * GRID_W - 2, 64], [RPB_ROW, 6], [1, 64]])).then_inc(s_bt, 16)
            pool.wait_ge(gain_rd, 1)

            def rotate(nm):
                s = proj[nm]
                for un in units[nm]:
                    if not un["groups"]:
                        continue
                    if un.get("assembled"):
                        pool.wait_ge(s["normed"], un["nth_assembled"])
                    else:
                        pool.wait_ge(s["taken"], un["x"] + 1)
                    for gr in un["groups"]:
                        nh, hd = gr["nh"], gr["hd"]
                        gb = gr["gain"].unsqueeze(1).to_broadcast([P, nh, hd])
                        if gr["rope"] is None and nm == "UQ":
                            continue
                        if gr["rope"] is None:
                            for o in gr["outs"]:
                                ch.after(pool.tensor_tensor(o, gr["dst"], gb, ALU.mult))
                            continue
                        cos, sin, r0, rl = gr["rope"]
                        if nm != "UQ":
                            ch.after(pool.tensor_tensor(gr["dst"], gr["dst"], gb, ALU.mult))
                        q = rl // 4
                        x = gr["dst"][:, :, r0:r0 + rl]
                        va = ra[:, 0:nh * rl].rearrange("p (h d) -> p h d", d=rl)
                        vb = rb[:, 0:nh * rl].rearrange("p (h d) -> p h d", d=rl)
                        pool.tensor_tensor(va, x, cos.unsqueeze(1).to_broadcast([P, nh, rl]), ALU.mult)
                        x4 = x.rearrange("p h (a c q) -> p h a c q", a=2, c=2)
                        b4 = vb.rearrange("p h (a c q) -> p h a c q", a=2, c=2)
                        s4 = sin.rearrange("p (a c q) -> p a c q", a=2, c=2)
                        for c in range(2):
                            for ax in range(2):
                                ins = pool.tensor_tensor(b4[:, :, ax, c, :], x4[:, :, ax, 1 - c, :],
                                                         s4[:, ax, c, :].unsqueeze(1).to_broadcast([P, nh, q]), ALU.mult)
                        ch.after(ins)
                        for o in gr["outs"]:
                            ch.after(pool.tensor_tensor(o[:, :, r0:r0 + rl], va, vb, ALU.add))
                    pool.sem_inc(s["rotated"], 1)

            rotate("L0")
            for f in range(FT):
                pool.wait_ge(f_hh, f + 1)
                pool.tensor_tensor(hidl[:, kept(f), :], hbuf[f % 2], hidh[:, kept(f), :].bitcast(F32), ALU.subtract)\
                    .then_inc(f_hl, 1)
            rotate("L1")
            rotate("UQ")

        @block.scalar
        def _(act):
            ch = Chain(act, a_step)
            act.dma_start(adab[:, :, :].rearrange("p a b -> p (a b)"), a["adab"]).then_inc(s_cst, 16)
            act.dma_start(ng[:, :, :, :].rearrange("p a b c -> p (a b c)"), a["ng"]).then_inc(s_cst, 16)
            act.dma_start(cst[:, :], a["cst"]).then_inc(s_cst, 16)
            act.dma_start(vec[:, :], a["vec"].partition_broadcast(P)).then_inc(s_cst, 16)
            act.dma_start(rtr[:, :, :], a["moe_router"].rearrange("(k p) n -> p k n", p=P)).then_inc(s_cst, 16)
            act.wait_ge(s_cond, 16)
            act.activation(scond[:, :], cond[:, :], ACT.Silu).then_inc(s_scond, 1)

            def root(nm, nt, summed=1):
                s = norm[nm]
                act.wait_ge(s["summed"], summed)
                act.activation(rt[:, 0:nt], ps[6][:, 0:nt], ACT.Sqrt, bias=eps[:, 0:1], scale=1.0 / D)\
                   .then_inc(s["root"], 1)

            def shift(nm, l, w, nt):
                s = norm[nm]
                n = 0
                for c in range(nt // S_LAT):
                    for k in range(KT):
                        n += 1
                        act.wait_ge(s["scaled"], n)
                        hv = hT[:, k, c * S_LAT:(c + 1) * S_LAT]
                        act.activation(hv, hv, ACT.Identity, bias=ada[:, l, 24 * w + k, c:c + 1])\
                           .then_inc(s["ready"], 1)

            def proj_act(nm):
                s = proj[nm]

                def squares(un):
                    v = un["v"]
                    if un.get("assembled"):
                        act.wait_ge(s["taken"], un["x"] + 1)
                    else:
                        act.wait_ge(s["done"], un["x"] + 1)
                    if v >= 2:
                        act.wait_ge(s["reduced"], v - 1)
                    n = un["sq"].shape[1]
                    act.activation(sq[v % 2][:, 0:n], un["sq"], ACT.Square).then_inc(s["squared"], 1)

                def root(un):
                    v = un["v"]
                    act.wait_ge(s["reduced"], v + 1)
                    o = 0
                    for gr in un["groups"]:
                        ins = act.activation(rt8[:, v % 4, o:o + gr["nh"]], ss[:, v % 4, o:o + gr["nh"]], ACT.Sqrt,
                                             bias=eps[:, 0:1], scale=1.0 / gr["hd"])
                        o += gr["nh"]
                    ins.then_inc(s["root"], 1)

                def store(un):
                    v = un["v"]
                    act.wait_ge(s["turned"], v + 1)
                    bank = ps[4 + v % 2]
                    dst, rows = un["store"]
                    n = dst.shape[1]
                    ins = act.activation(dst, bank[0:rows, 0:n * P].rearrange("p (a b) -> p a b", b=P), ACT.Copy)
                    if "store2" in un:
                        d2, n2 = un["store2"]
                        ins = act.activation(d2, bank[:, n * P:(n + n2) * P].rearrange("p (a b) -> p a b", b=P), ACT.Copy)
                    ins.then_inc(s["stored"], 1)

                us = units[nm]
                for x in range(len(us) + 3):
                    if x < len(us) and us[x]["groups"]:
                        squares(us[x])
                        root(us[x])
                    if x >= 3 and us[x - 3]["groups"]:
                        store(us[x - 3])

            def att_act(nm):
                s, pl = att[nm], plans[nm]
                nst = 0
                for i in range(NSTEP[nm]):
                    if i < len(pl["items"]):
                        it = pl["items"][i]
                        act.wait_ge(s["max"], i + 1)
                        if i >= 4:
                            act.wait_ge(s["turned"], pl["items"][i - 4]["pv"] + 1)
                        act.activation(prob[i % 4][:, 0:it["nk"]], ps[SBANK[i % 3]][:, 0:it["nk"]], ACT.Exp,
                                       bias=nmx[:, i % 64:i % 64 + 1], scale=it["scale"],
                                       accum_out=sums[:, i % 64:i % 64 + 1]).then_inc(s["exp"], 1)
                    for j in pv_at(pl, i - 3):
                        nk = pl["pvs"][j]["nk"]
                        act.wait_ge(s["turned"], j + 1)
                        if j >= 2:
                            act.wait_ge(s["pv"], j - 1)
                        act.activation(probT[j % 2][:, 0:nk], ps[2 + j % 2][:, 0:nk], ACT.Copy).then_inc(s["copied"], 1)
                    for gp in closes(pl, i):
                        if gp["sub"]:
                            act.wait_ge(s["out"], gp["pv1"])
                            act.activation(sq[gp["e"] % 2], gp["otok"], ACT.Square).then_inc(s["osq"], 1)
                            act.wait_ge(s["ored"], gp["subs_upto"])
                            act.activation(rt8[:, 0, 0:4], ss[:, 0, 0:4], ACT.Sqrt, bias=eps[:, 0:1], scale=1.0 / P)\
                               .then_inc(s["oroot"], 1)
                    for gp in closes(pl, i - 1):
                        e = gp["e"]
                        act.wait_ge(s["oturned"], e + 1)
                        act.activation(hT[:, 4 * gp["half"]:4 * gp["half"] + 4, gp["t"] * P:(gp["t"] + 1) * P],
                                       ps[6][:, :].rearrange("p (a b) -> p a b", b=P), ACT.Copy)\
                           .then_inc(s["ostored"], 1)

            act.wait_ge(s_x, 32)
            for k in range(KT):
                if k >= 4:
                    act.wait_ge(norm["n00"]["summed"], k - 3)
                act.activation(sq[k % 4], xT[:, k, :], ACT.Square).then_inc(norm["n00"]["square"], 1)
            act.wait_ge(eps_set, 1)
            root("n00", S_ALL, KT)
            for j in range(4):
                act.wait_ge(ada_used, j + 1)
                if j >= 2:
                    act.wait_ge(ada_tr, j - 1)
                act.activation(adar[0:2, j % 2, :], ps[j % 2][0:2, :], ACT.Copy).then_inc(ada_row, 1)
            shift("n00", 0, 0, S_ALL)
            act.wait_ge(lam_in, 1)
            act.activation(lamt[:, 2:4], lamt[:, 0:2], ACT.Exp).then_inc(lam_ex, 1)
            act.wait_ge(gain_rd, 1)
            proj_act("L0")
            att_act("A0")

            def unit_high(u):
                g, w = unit_src[u]
                if u % 4 == 0:
                    act.wait_ge(slot_full[slot_of(g)], 16 * loads_upto(g))
                if u >= UF:
                    act.wait_ge(f_used, u - UF + 1)
                act.activation(unit_parts(u)[0], w, ACT.Copy).then_inc(f_hi, 1)

            for u in range(UF):
                unit_high(u)
            root("n01", S_ALL)
            for k in range(KT):
                for c in range(2):
                    tc = slice(c * S_LAT, (c + 1) * S_LAT)
                    act.wait_ge(norm["n01"]["scaled"], 2 * k + c + 1)
                    act.activation(hTh[:, k, tc], hraw[:, k, tc], ACT.Identity, bias=ada[:, 0, 24 + k, c:c + 1])\
                       .then_inc(norm["n01"]["ready"], 1)
            for u in range(UF, NUF + UF + 1):
                if u - UF - 1 in up_at:
                    f = up_at[u - UF - 1]
                    act.wait_ge(mul_rd, 2 + f + 1)
                    act.activation(hidh[:, kept(f), :], hbuf[f % 2], ACT.Copy).then_inc(f_hh, 1)
                if u < NUF:
                    unit_high(u)
                if u - UF in gate_at:
                    f = gate_at[u - UF]
                    act.wait_ge(f_used, u - UF + 1)
                    if f >= 2:
                        act.wait_ge(mul_rd, 2 + f - 1)
                    act.activation(sq[f % 2], ps[2 * (f % 2)][:, :], ACT.Silu).then_inc(silu_rd, 1)
            root("n10", S_ALL)
            shift("n10", 1, 0, S_ALL)
            proj_act("L1")
            proj_act("UQ")
            att_act("A1")
            root("n11", S_LAT)
            shift("n11", 1, 1, S_LAT)
            for t in range(2):
                for hh in range(2):
                    act.wait_ge(tok_t, 2 * t + hh + 1)
                    act.activation(htok[:, t, hh * 512:(hh + 1) * 512], ps[2 * t + hh][:, :], ACT.Copy).then_inc(tok_rd, 1)
            act.wait_ge(rt_ein, 1)
            act.activation(ro[:, 8, 0, 0:2], ro[:, 7, 0, 0:2], ACT.Exp).then_inc(rt_ex, 1)
            act.wait_ge(items_rd, 1)
            total = act.value_load(nit[0:1, 0:1], min_val=NE, max_val=NE * ROUNDS)
            act.wait_ge(m_init, 1)

            def tokens_high(n):
                for hh in range(2):
                    act.wait_ge(m_gat, hh + 1 if n is None else n * 2 + (hh + 1))
                    act.activation(xgr[:, 0, 4 * hh:4 * hh + 4, :], v3(ps[4 + hh][:, :], CAP), ACT.Copy)\
                       .then_inc(m_xh, 1)

            def sum_copy(n):
                act.wait_ge(m_pe, n * NU + URING)
                act.activation(ytok[:, 0:512], ps[0][:, :], ACT.Copy).then_inc(m_ya, 1)

            tokens_high(None)
            with act.Fori(0, total) as n:
                for h in range(NU):
                    if h == 3:
                        sum_copy(n)
                    j = (h - 6) // 4
                    if h % 4 == 2 and 0 <= j < 7:
                        act.wait_ge(m_pe, n * NU + (4 * j + 4 + URING))
                        act.activation(sg[:, j % 2, :], ps[4 + 2 * (j % 2)][:, :], ACT.Silu).then_inc(m_silu, 1)
                    j = (h - 10) // 4
                    if h % 4 == 2 and 0 <= j < 7:
                        act.wait_ge(m_t, n * 7 + (j + 1))
                        act.activation(hidr[:, 0, QF * j:QF * j + QF, :], v3(ps[2 + j % 2][:, :], CAP), ACT.Copy)\
                           .then_inc(m_hh, 1)
                    if h == 37:
                        tokens_high(n + 1)
                    if h % 2 == 0:
                        c = h // 2
                        act.wait_ge(mslot_full[c % MRING], n * 112 + 16 * (c // MRING + 1))
                    act.wait_ge(m_pe, n * NU + (h + 1))
                    act.activation(whi[:, h % URING, :], mslot[(h // 2) % MRING][:, (h % 2) * UNIT:(h % 2 + 1) * UNIT],
                                   ACT.Copy).then_inc(m_hi, 1)
            sum_copy(total)

        @block.vector
        def _(dve):
            ch = Chain(dve, d_step)
            dve.memset(eps[:, :], EPS).then_inc(eps_set, 1)
            dve.wait_ge(s_cst, 80)
            for n in ("na_q_g", "diff_q_g", "gqa_q_g"):
                dve.tensor_scalar(vv(n), vv(n), HD ** -0.5, None, ALU.mult)
            dve.tensor_scalar(vv("diff_subln_g"), vv("diff_subln_g"), 1.0 - LAM_INIT, None, ALU.mult).then_inc(gain_rd, 1)
            dots = tn[2]
            ch.after(dve.tensor_tensor(dots[:, 0:64], vv("diff_lq1"), vv("diff_lk1"), ALU.mult))
            ch.after(dve.tensor_tensor(dots[:, 64:128], vv("diff_lq2"), vv("diff_lk2"), ALU.mult))
            dve.tensor_reduce(lamt[:, 0:2], v3(dots[:, 0:128], 64), AX.X, ALU.add).then_inc(lam_in, 1)

            def lam_dve():
                dve.wait_ge(lam_ex, 1)
                ch.after(dve.tensor_tensor(lamt[:, 4:5], lamt[:, 3:4], lamt[:, 2:3], ALU.subtract))
                ch.after(dve.tensor_scalar(lamt[:, 5:6], lamt[:, 4:5], -LAM_INIT, None, ALU.add))

            def bias_dve():
                dve.wait_ge(s_bt, 16 * 16)
                btv = bt[:, :, :, :].rearrange("p h u c -> p (h u) c")
                ch.after(dve.tensor_tensor(btv, btv, cv("mask").unsqueeze(1).to_broadcast([P, 48, GRID_W]), ALU.add))

            adam = ada[:, :, :, :].rearrange("p l m c -> p (l m) c")
            adabm = adab[:, :, :].rearrange("p l m -> p (l m)")

            def acc_step(g, par, nq, k, q, base):
                if k == 0 and q == 0:
                    dve.wait_ge(slot_full[slot_of(g)], 16 * loads_upto(g))
                w = slot3(g, 512)[:, k, :]
                d = acc[:, 2 * par + q, :]
                col = scond[:, 2 * k + q:2 * k + q + 1]
                if k == 0:
                    ins = dve.tensor_scalar(d, w, col, None, ALU.mult)
                else:
                    dve.wait_ge(acc_st, base + nq * (k - 1) + q + 1)
                    ins = dve.scalar_tensor_tensor(out=d, in0=w, scalar=col, in1=d, op0=ALU.mult, op1=ALU.add)
                if k < KT - 1:
                    ins.then_inc(acc_st, 1)
                elif q == nq - 1:
                    ins.then_inc(acc_rd, 1)

            def acc_take(n, m, nq):
                dve.wait_ge(sum_rd, n + 1)
                ms = slice(m, m + 4)
                dve.tensor_tensor(adam[:, ms, 0:nq], ps[6 + n % 2][:, 0:8].rearrange("p (m c) -> p m c", c=2)[:, :, 0:nq],
                                  adabm[:, ms].unsqueeze(2).to_broadcast([P, 4, nq]), ALU.add).then_inc(take_rd, 1)

            def mod(l, w, nc_=2):
                ch.after(dve.scalar_tensor_tensor(out=amod[:, l, w, :, 0:nc_], in0=ada[:, l, 24 * w + 8:24 * w + 16, 0:nc_],
                                                  scalar=1.0, in1=ng[:, w, l, :].unsqueeze(2).to_broadcast([P, KT, nc_]),
                                                  op0=ALU.add, op1=ALU.mult))

            def norm_recip(nm, nt):
                dve.wait_ge(norm[nm]["root"], 1)
                ch.after(dve.reciprocal(rstd[:, 0:nt], rt[:, 0:nt]))

            def norm_dve(nm, l, w, nt):
                s = norm[nm]
                if nm != "n00":
                    norm_recip(nm, nt)
                for c in range(nt // S_LAT):
                    for k in range(KT):
                        tc = slice(c * S_LAT, (c + 1) * S_LAT)
                        dve.scalar_tensor_tensor(out=hT[:, k, tc], in0=xT[:, k, tc], scalar=amod[:, l, w, k, c:c + 1],
                                                 in1=rstd[:, tc], op0=ALU.mult, op1=ALU.mult).then_inc(s["scaled"], 1)

            def proj_dve(nm, between=lambda x: None):
                s, us = proj[nm], units[nm]

                def take(x, un):
                    if un["copies"]:
                        if un["groups"] and not un.get("assembled"):
                            dve.wait_ge(s["squared"], un["v"] + 1)
                        else:
                            dve.wait_ge(s["done"], x + 1)
                        for d, sr in un["copies"]:
                            ins = dve.tensor_copy(d, sr)
                        if un.get("assembled") or not un["groups"]:
                            ins.then_inc(s["taken"], 1)

                def reduce(un):
                    if un["groups"]:
                        v = un["v"]
                        dve.wait_ge(s["squared"], v + 1)
                        o = 0
                        for gr in un["groups"]:
                            lo, hi = gr["sq"]
                            ins = dve.tensor_reduce(ss[:, v % 4, o:o + gr["nh"]],
                                                    sq[v % 2][:, lo:hi].rearrange("p (h d) -> p h d", d=gr["hd"]),
                                                    AX.X, ALU.add)
                            o += gr["nh"]
                        ins.then_inc(s["reduced"], 1)

                def second(un):
                    v = un["v"]
                    dve.wait_ge(s["root"], v + 1)
                    nh = sum(gr["nh"] for gr in un["groups"])
                    ch.after(dve.reciprocal(rs8[:, v % 4, 0:nh], rt8[:, v % 4, 0:nh]))
                    if v >= 3:
                        dve.wait_ge(s["turned"], v - 2)
                    o = 0
                    for gr in un["groups"]:
                        ins = dve.tensor_tensor(gr["dst"], gr["src"],
                                                rs8[:, v % 4, o:o + gr["nh"]].unsqueeze(2)
                                                .to_broadcast([P, gr["nh"], gr["hd"]]), ALU.mult)
                        o += gr["nh"]
                        if s is proj["UQ"]:
                            ch.after(ins)
                            ins = dve.tensor_tensor(gr["dst"], gr["dst"],
                                                    gr["gain"].unsqueeze(1).to_broadcast([P, gr["nh"], gr["hd"]]), ALU.mult)
                    ins.then_inc(s["normed" if un.get("assembled") else "taken"], 1)

                pend = None
                for x, un in enumerate(us):
                    ahead = pend is not None and bool(pend.get("assembled"))
                    if ahead:
                        take(x, un)
                    if pend is not None:
                        second(pend)
                        pend = None
                    if not ahead:
                        take(x, un)
                    reduce(un)
                    if un["groups"]:
                        pend = un
                    between(x)
                if pend is not None:
                    second(pend)

            def att_dve(nm):
                s, pl = att[nm], plans[nm]
                nsub = 0
                for i in range(NSTEP[nm]):
                    if i < len(pl["items"]):
                        it = pl["items"][i]
                        c = i % 64
                        bank = ps[SBANK[i % 3]]
                        dve.wait_ge(s["score"], i + 1)
                        if it["bias"] is not None:
                            b3 = bank[:, 0:S_LAT].rearrange("p (r c) -> p r c", c=GRID_W)
                            ch.after(dve.tensor_tensor(b3, b3, it["bias"], ALU.add))
                        ch.after(dve.reduce_max(mx[:, c:c + 1], bank[:, 0:it["nk"]], AX.X))
                        dve.tensor_scalar(nmx[:, c:c + 1], mx[:, c:c + 1], -it["scale"], None, ALU.mult)\
                           .then_inc(s["max"], 1)
                    if 1 <= i <= len(pl["items"]):
                        q = i - 1
                        c = q % 64
                        dve.wait_ge(s["exp"], q + 1)
                        ch.after(dve.reciprocal(rsum[:, c:c + 1], sums[:, c:c + 1]))
                        for j in pv_at(pl, q):
                            pv = pl["pvs"][j]
                            if len(pv["items"]) == 2:
                                c0 = pv["items"][0] % 64
                                p0 = prob[pv["items"][0] % 4][:, 0:pv["nk"]]
                                p1 = prob[q % 4][:, 0:pv["nk"]]
                                dve.tensor_scalar(p0, p0, rsum[:, c0:c0 + 1], None, ALU.mult)
                                ch.after(dve.tensor_tensor(rsum[:, c:c + 1], rsum[:, c:c + 1], lamt[:, 5:6], ALU.mult))
                                dve.scalar_tensor_tensor(out=p1, in0=p1, scalar=rsum[:, c:c + 1], in1=p0,
                                                         op0=ALU.mult, op1=ALU.add).then_inc(s["mixed"], 1)
                    for j in pv_at(pl, i - 5):
                        pv = pl["pvs"][j]
                        o = ps[pv["ob"]][:, 0:pv["dv"]]
                        dve.wait_ge(s["pv"], j + 1)
                        if len(pv["items"]) == 2:
                            dve.tensor_copy(pv["dst"], o).then_inc(s["out"], 1)
                        else:
                            c = pv["items"][0] % 64
                            dve.tensor_scalar(pv["dst"], o, rsum[:, c:c + 1], None, ALU.mult).then_inc(s["out"], 1)
                    for gp in closes(pl, i):
                        if gp["sub"]:
                            nsub += 1
                            dve.wait_ge(s["osq"], nsub)
                            dve.tensor_reduce(ss[:, 0, 0:4], v3(sq[gp["e"] % 2], P), AX.X, ALU.add).then_inc(s["ored"], 1)
                            dve.wait_ge(s["oroot"], nsub)
                            ch.after(dve.reciprocal(rs8[:, 0, 0:4], rt8[:, 0, 0:4]))
                            o3 = v3(gp["otok"], P)
                            ch.after(dve.tensor_tensor(o3, o3,
                                                       rs8[:, 0, 0:4].unsqueeze(2).to_broadcast([P, 4, P]), ALU.mult))
                            dve.tensor_tensor(o3, o3, vv("diff_subln_g").unsqueeze(1).to_broadcast([P, 4, P]),
                                              ALU.mult).then_inc(s["otok"], 1)

            def out_dve(nm, l, nc_, after):
                s = outp[nm]
                nt = nc_ * S_LAT
                for d in range(KT):
                    dve.wait_ge(s["done"], d + 1)
                    for c in range(nc_):
                        tc = slice(c * S_LAT, (c + 1) * S_LAT)
                        ins = dve.scalar_tensor_tensor(out=xT[:, d, tc], in0=ps[d % 4][:, tc],
                                                       scalar=ada[:, l, 16 + d, c:c + 1], in1=xT[:, d, tc],
                                                       op0=ALU.mult, op1=ALU.add)
                    ins.then_inc(s["added"], 1)
                    dve.wait_ge(s["added"], d + 1)
                    x = xT[:, d, 0:nt]
                    if d == 0:
                        ch.after(dve.tensor_tensor(sq[0][:, 0:nt], x, x, ALU.mult))
                        continue
                    ch.after(dve.tensor_tensor(sq[1][:, 0:nt], x, x, ALU.mult))
                    ins = dve.tensor_tensor(sq[0][:, 0:nt], sq[0][:, 0:nt], sq[1][:, 0:nt], ALU.add)
                    if d == KT - 1:
                        ins.then_inc(norm[after]["square"], 1)
                    else:
                        ch.after(ins)

            norm_recip("n00", S_ALL)
            dve.wait_ge(ada_tr, 4)
            dve.tensor_tensor(adam[:, 0:16, :], ps[7][:, 0:32].rearrange("p (m c) -> p m c", c=2),
                              adabm[:, 0:16].unsqueeze(2).to_broadcast([P, 16, 2]), ALU.add).then_inc(ada_rd, 1)
            dve.wait_ge(ada_rd, 1)
            mod(0, 0)
            norm_dve("n00", 0, 0, S_ALL)
            lam_dve()
            steps = [(c, k, q) for c in range(8) for k in range(KT) for q in range(2)]

            def between(x):
                n = len(units["L0"])
                for c, k, q in steps[len(steps) * x // n:len(steps) * (x + 1) // n]:
                    if k == 0 and q == 0 and c >= 2:
                        acc_take(c - 2, 16 + 4 * (c - 2), 2)
                    acc_step(at["A0b", c], c % 2, 2, k, q, c * 2 * (KT - 1))
                if x == 10:
                    bias_dve()

            proj_dve("L0", between)
            acc_take(6, 40, 2)
            acc_take(7, 44, 2)
            dve.wait_ge(take_rd, 8)
            mod(0, 1)
            att_dve("A0")

            def unit_low(u):
                hi, lo = unit_parts(u)
                dve.wait_ge(f_hi, u + 1)
                dve.tensor_tensor(lo, unit_src[u][1], hi.bitcast(F32), ALU.subtract).then_inc(f_lo, 1)

            chunk_at = {first_unit("F0", c): c for c in range(FT // 2)}
            chunk_at[first_unit("D0", 4)] = FT // 2

            def modulate(v):
                c = chunk_at.get(v - v % 4)
                if v == first_unit("D0", 7):
                    acc_take(18, 88, 1)
                    dve.wait_ge(take_rd, 19)
                    mod(1, 0)
                if c is None:
                    return
                nq = 2 if c < 4 else 1
                if v % 4 == 0 and c >= 2:
                    acc_take(8 + c - 2, 48 + 4 * (c - 2), 2 if c - 2 < 4 else 1)
                base = (KT - 1) * (8 * 2 + 2 * min(c, 4) + max(c - 4, 0))
                for k in (2 * (v % 4), 2 * (v % 4) + 1):
                    for z in range(nq):
                        acc_step(at["A1", c], c % 2, nq, k, z, base)

            dve.sem_inc(mul_rd, 2)
            for u in range(UF):
                unit_low(u)
            for v in range(UF + 1):
                modulate(v)
            out_dve("O0", 0, 2, "n01")
            dve.wait_ge(norm["n01"]["root"], 1)
            ch.after(dve.reciprocal(rstd, rt))
            for n in range(2 * KT + 2):
                if n < 2 * KT:
                    k, c = n // 2, n % 2
                    tc = slice(c * S_LAT, (c + 1) * S_LAT)
                    dve.scalar_tensor_tensor(out=hraw[:, k, tc], in0=xT[:, k, tc], scalar=amod[:, 0, 1, k, c:c + 1],
                                             in1=rstd[:, tc], op0=ALU.mult, op1=ALU.mult)\
                        .then_inc(norm["n01"]["scaled"], 1)
                if n >= 2:
                    k, c = (n - 2) // 2, n % 2
                    tc = slice(c * S_LAT, (c + 1) * S_LAT)
                    dve.wait_ge(norm["n01"]["ready"], n - 1)
                    dve.scalar_tensor_tensor(out=hTl[:, k, tc], in0=hraw[:, k, tc], scalar=ada[:, 0, 24 + k, c:c + 1],
                                             in1=hTh[:, k, tc].bitcast(F32), op0=ALU.add, op1=ALU.subtract)\
                        .then_inc(n01_low, 1)
            for u in range(UF, NUF + UF + 1):
                if u - UF - 1 in up_at:
                    f = up_at[u - UF - 1]
                    dve.wait_ge(silu_rd, f + 1)
                    dve.wait_ge(f_used, u - UF)
                    if f >= 2:
                        dve.wait_ge(f_hl, f - 1)
                    dve.tensor_tensor(hbuf[f % 2], sq[f % 2], ps[2 * (f % 2) + 1][:, :], ALU.mult).then_inc(mul_rd, 1)
                if u - UF - 1 in down_at:
                    n = down_at[u - UF - 1]
                    d = n % KT
                    dve.wait_ge(f_used, u - UF)
                    for c in range(2):
                        tc = slice(c * S_LAT, (c + 1) * S_LAT)
                        ins = dve.scalar_tensor_tensor(out=xT[:, d, tc], in0=ps[4 + n % 2][:, tc],
                                                       scalar=ada[:, 0, 40 + d, c:c + 1], in1=xT[:, d, tc],
                                                       op0=ALU.mult, op1=ALU.add)
                    ins.then_inc(dn_add, 1)
                    if n >= KT:
                        dve.wait_ge(dn_add, n + 1)
                        x = xT[:, d, :]
                        ch.after(dve.tensor_tensor(sq[1 if d else 0], x, x, ALU.mult))
                        if d:
                            ins = dve.tensor_tensor(sq[0], sq[0], sq[1], ALU.add)
                            if d == KT - 1:
                                ins.then_inc(norm["n10"]["square"], 1)
                            else:
                                ch.after(ins)
                if u < NUF:
                    unit_low(u)
                modulate(u + 1)
            norm_dve("n10", 1, 0, S_ALL)
            acc_take(19, 92, 1)
            dve.wait_ge(take_rd, 20)
            mod(1, 1, 1)
            proj_dve("L1")
            proj_dve("UQ")
            att_dve("A1")
            out_dve("O1", 1, 1, "n11")
            norm_dve("n11", 1, 1, S_LAT)

            def R(i):
                return ro[:, i, :, :]

            def B(ap):
                return ap.unsqueeze(2).to_broadcast([P, 2, NE])

            col = [ro[:, 16 + i, 0, 0:2] for i in range(8)]
            rank = cv("rank").unsqueeze(1).to_broadcast([P, 2, NE])
            dve.wait_ge(rt_mm, 1)
            ch.after(dve.tensor_copy(R(0), ps[5][:, 0:2 * NE].rearrange("p (t e) -> p t e", e=NE)))

            def best(src, eq, one, m):
                ch.after(dve.tensor_reduce(m, src, AX.X, ALU.max))
                ch.after(dve.tensor_tensor(eq, src, B(m), ALU.is_equal))
                ch.after(dve.tensor_tensor(eq, eq, rank, ALU.mult))
                ch.after(dve.tensor_reduce(col[7], eq, AX.X, ALU.max))
                ch.after(dve.tensor_tensor(one, eq, B(col[7]), ALU.is_equal))

            best(R(0), R(1), R(2), col[0])
            ch.after(dve.scalar_tensor_tensor(out=R(3), in0=R(2), scalar=-3e38, in1=R(0), op0=ALU.mult, op1=ALU.add))
            best(R(3), R(1), R(4), col[1])
            dve.tensor_tensor(R(5), R(2), R(4), ALU.add).then_inc(rt_sel, 1)
            dve.tensor_tensor(ro[:, 7, 0, 0:2], col[1], col[0], ALU.subtract).then_inc(rt_ein, 1)
            dve.wait_ge(rt_ex, 1)
            ch.after(dve.tensor_scalar(col[2], ro[:, 8, 0, 0:2], 1.0, None, ALU.add))
            ch.after(dve.reciprocal(col[3], col[2]))
            ch.after(dve.tensor_tensor(col[4], col[3], ro[:, 8, 0, 0:2], ALU.mult))
            ch.after(dve.tensor_tensor(R(9), R(2), B(col[3]), ALU.mult))
            ch.after(dve.tensor_tensor(R(10), R(4), B(col[4]), ALU.mult))
            ch.after(dve.tensor_tensor(R(11), R(9), R(10), ALU.add))
            dve.wait_ge(rt_pos, 1)
            dve.memset(posr[:, :, NI - 1:NI], 0.0)
            dve.memset(gat[:, :, NI - 1:NI], 0.0)
            dve.memset(chs[:, :, NI - 1:NI], 0.0)
            for r in range(ROUNDS):
                rs = slice(r * NE, (r + 1) * NE)
                dve.tensor_scalar(posr[:, :, rs], ps[4][:, 0:2 * NE].rearrange("p (t e) -> p t e", e=NE),
                                  -float(r * CAP), None, ALU.add)
                dve.tensor_copy(gat[:, :, rs], R(11))
                dve.tensor_copy(chs[:, :, rs], R(5))
            ch.after(dve.reduce_max(col[5][:, 0:1], ps[4][:, 2 * NE:3 * NE], AX.X))
            ch.after(dve.tensor_scalar(col[5][:, 1:2], col[5][:, 0:1], float(CAP), float(NE), ALU.is_gt, ALU.mult))
            assert ROUNDS == 2
            dve.tensor_scalar(nit[:, 0:1], col[5][:, 1:2], float(NE), None, ALU.add).then_inc(items_rd, 1)
            dve.wait_ge(items_rd, 1)
            total = dve.value_load(nit[0:1, 0:1], min_val=NE, max_val=NE * ROUNDS)
            pf = posr[:, :, :].rearrange("p t n -> p (t n)")
            gf = gat[:, :, :].rearrange("p t n -> p (t n)")
            cf = chs[:, :, :].rearrange("p t n -> p (t n)")
            dve.memset(ps[0][:, :], 0.0)
            dve.memset(ps[1][:, :], 0.0)
            dve.memset(pgT[:, :], 0.0).then_inc(m_init, 1)
            dve.sem_inc(m_mul, 2)

            def choose(dst, m, table):
                for t in range(2):
                    pc = pf[:, t * NI:t * NI + 1] if m is None else pf[:, bass.ds(m + t * NI, 1)]
                    tc = table[:, t * NI:t * NI + 1] if m is None else table[:, bass.ds(m + t * NI, 1)]
                    ins = dve.tensor_scalar(dst[:, t, :], cv("iota"), pc, tc, ALU.is_equal, ALU.mult)
                return ins

            def tokens_low(n):
                for hh in range(2):
                    dve.wait_ge(m_xh, hh + 1 if n is None else n * 2 + (hh + 1))
                    dve.tensor_tensor(xgr[:, 1, 4 * hh:4 * hh + 4, :], v3(ps[4 + hh][:, :], CAP),
                                      xgr[:, 0, 4 * hh:4 * hh + 4, :].bitcast(F32), ALU.subtract).then_inc(m_xl, 1)

            def sum_copy(n):
                dve.wait_ge(m_pe, n * NU + URING)
                dve.tensor_copy(ytok[:, 512:1024], ps[1][:, :]).then_inc(m_yb, 1)

            def add(n, i):
                dve.wait_ge(m_sc, n * 4 + (i + 1))
                for q in range(2):
                    d = 2 * i + q
                    ins = dve.scalar_tensor_tensor(out=xT[:, d, 0:S_LAT], in0=ps[i][:, q * S_LAT:(q + 1) * S_LAT],
                                                   scalar=ada[:, 1, 40 + d, 0:1], in1=xT[:, d, 0:S_LAT],
                                                   op0=ALU.mult, op1=ALU.add)
                if i == 3:
                    ins.then_inc(m_add, 1)

            choose(sel, None, cf).then_inc(m_sel, 1)
            tokens_low(None)
            with dve.Fori(0, total) as n:
                for h in range(NU):
                    if h == 3:
                        sum_copy(n)
                    if 5 <= h < 9:
                        add(n, h - 5)
                    j = (h - 6) // 4
                    if h % 4 == 2 and 0 <= j < 7:
                        dve.wait_ge(m_silu, n * 7 + (j + 1))
                        dve.tensor_tensor(hidtok[:, j % 2, :], sg[:, j % 2, :], ps[5 + 2 * (j % 2)][:, :], ALU.mult)\
                           .then_inc(m_mul, 1)
                    j = (h - 10) // 4
                    if h % 4 == 2 and 0 <= j < 7:
                        dve.wait_ge(m_hh, n * 7 + (j + 1))
                        hs = slice(QF * j, QF * j + QF)
                        dve.tensor_tensor(hidr[:, 1, hs, :], v3(ps[2 + j % 2][:, :], CAP),
                                          hidr[:, 0, hs, :].bitcast(F32), ALU.subtract).then_inc(m_hl, 1)
                    if h == 9:
                        choose(gsel, n, gf).then_inc(m_gsel, 1)
                    if h == 17:
                        dve.wait_ge(m_pgt, n + 1)
                        dve.tensor_copy(pgT[:, :], ps[0][:, 0:S_LAT]).then_inc(m_pg, 1)
                    if h == 29:
                        choose(sel, n + 1, cf).then_inc(m_sel, 1)
                    if h == 37:
                        tokens_low(n + 1)
                    dve.wait_ge(m_hi, n * NU + (h + 1))
                    dve.tensor_tensor(wlo[:, h % URING, :], mslot[(h // 2) % MRING][:, (h % 2) * UNIT:(h % 2 + 1) * UNIT],
                                      whi[:, h % URING, :].bitcast(F32), ALU.subtract).then_inc(m_lo, 1)
            sum_copy(total)
            for i in range(4):
                add(total, i)

        @block.tensor
        def _(pe):
            def arrived(g):
                pe.wait_ge(slot_full[slot_of(g)], 16 * loads_upto(g))

            def norm_pe(nm, nt, total):
                s = norm[nm]
                pe.wait_ge(s["square"], 1)
                pe.matmul(ps[6][:, 0:nt], ones[:, :], total[:, 0:nt], start=True, stop=True).then_inc(s["summed"], 1)

            def ada_first():
                def turn(j):
                    pe.wait_ge(ada_row, j + 1)
                    for q in range(4):
                        c = 2 * (4 * j + q)
                        ins = pe.transpose(ps[7][:, c:c + 2], adar[0:2, j % 2, q * P:(q + 1) * P], ident[0:2, 0:2])
                    ins.then_inc(ada_tr, 1)

                for j in range(4):
                    arrived(at["A0a", j])
                    if j >= 2:
                        pe.wait_ge(ada_row, j - 1)
                    w = slot3(at["A0a", j], 512)
                    for k in range(KT):
                        ins = pe.matmul(ps[j % 2][0:2, :], scond[:, 2 * k:2 * k + 2], w[:, k, :],
                                        start=(k == 0), stop=(k == KT - 1))
                    ins.then_inc(ada_used, 1)
                    if j == 0:
                        pe.wait_ge(s_cst, 80)
                    else:
                        turn(j - 1)
                turn(3)

            def ada_sum(n, par, nq, i=None):
                pe.wait_ge(acc_rd, n + 1 if i is None else i * 2 + (n + 1))
                for m in range(4):
                    for q in range(nq):
                        c = 2 * m + q
                        ins = pe.matmul(ps[6 + n % 2][:, c:c + 1], acc[:, 2 * par + q, m * P:(m + 1) * P], ones[:, 0:1],
                                        start=True, stop=True)
                ins.then_inc(sum_rd, 1)

            def proj_pe(nm, between=lambda x: None):
                s, us = proj[nm], units[nm]

                def turn(un):
                    v = un["v"]
                    pe.wait_ge(s["rotated"], v + 1)
                    if v >= 2:
                        pe.wait_ge(s["stored"], v - 1)
                    for c, src in enumerate(un["turn"]):
                        w = src.shape[1]
                        ins = pe.transpose(ps[4 + v % 2][0:w, c * P:(c + 1) * P], src, ident)
                    ins.then_inc(s["turned"], 1)

                for x in range(len(us) + LAGT):
                    if x < len(us):
                        un = us[x]
                        if x == 0 or us[x - 1]["g"] != un["g"]:
                            arrived(un["g"])
                        if nm != "UQ":
                            pe.wait_ge(norm["n00" if nm == "L0" else "n10"]["ready"], KT if un["t"] < 2 else 2 * KT)
                        if x >= 4:
                            pe.wait_ge(s["taken"], x - 3)
                        for k in range(len(un["lhs"])):
                            ins = pe.matmul(ps[un["bank"]][:, 0:un["width"]], un["lhs"][k], un["w"][k],
                                            start=(k == 0), stop=(k == len(un["lhs"]) - 1))
                        ins.then_inc(s["done"], 1)
                    if x >= LAGT and us[x - LAGT]["groups"]:
                        turn(us[x - LAGT])
                    between(x)

            def att_pe(nm, nproj):
                s, pl = att[nm], plans[nm]
                for i in range(NSTEP[nm]):
                    if i < len(pl["items"]):
                        it = pl["items"][i]
                        if i >= 3:
                            pe.wait_ge(s["exp"], i - 2)
                        pe.matmul(ps[SBANK[i % 3]][:, 0:it["nk"]], it["q"], it["k"], start=True, stop=True)\
                          .then_inc(s["score"], 1)
                    for j in pv_at(pl, i - 4):
                        pv = pl["pvs"][j]
                        pe.wait_ge(s["copied"], j + 1)
                        if j >= 2:
                            pe.wait_ge(s["out"], j - 1)
                        nkt = pv["nk"] // P
                        for c in range(nkt):
                            ins = pe.matmul(ps[pv["ob"]][:, 0:pv["dv"]],
                                            probT[j % 2][:, c * P:(c + 1) * P], pv["v"][c],
                                            start=(c == 0), stop=(c == nkt - 1))
                        ins.then_inc(s["pv"], 1)
                    for j in pv_at(pl, i - 3):
                        pv = pl["pvs"][j]
                        if len(pv["items"]) == 2:
                            pe.wait_ge(s["mixed"], sum(1 for q in pl["pvs"][:j + 1] if len(q["items"]) == 2))
                        else:
                            pe.wait_ge(s["exp"], pv["items"][0] + 1)
                        if j >= 2:
                            pe.wait_ge(s["copied"], j - 1)
                        src = prob[pv["items"][-1] % 4]
                        for c in range(pv["nk"] // P):
                            ins = pe.transpose(ps[2 + j % 2][:, c * P:(c + 1) * P], src[:, c * P:(c + 1) * P], ident)
                        ins.then_inc(s["turned"], 1)
                    for gp in closes(pl, i - 1):
                        e = gp["e"]
                        if gp["sub"]:
                            pe.wait_ge(s["otok"], gp["subs_upto"])
                        else:
                            pe.wait_ge(s["out"], gp["pv1"])
                        if e >= 1:
                            pe.wait_ge(s["ostored"], e)
                        for c in range(4):
                            ins = pe.transpose(ps[6][:, c * P:(c + 1) * P], gp["otok"][:, c * P:(c + 1) * P], ident)
                        ins.then_inc(s["oturned"], 1)

            def out_pe(nm, an, nt):
                s = outp[nm]
                pe.wait_ge(att[an]["ostored"], len(plans[an]["groups"]))
                for d in range(KT):
                    g = at[nm, d // 4]
                    if d % 4 == 0:
                        arrived(g)
                    if d >= 4:
                        pe.wait_ge(s["added"], d - 3)
                    w = slot3(g, 512)
                    for k in range(KT):
                        ins = pe.matmul(ps[d % 4][:, 0:nt], w[:, k, (d % 4) * P:(d % 4 + 1) * P], hT[:, k, 0:nt],
                                        start=(k == 0), stop=(k == KT - 1))
                    ins.then_inc(s["done"], 1)

            pe.wait_ge(s_ones, 1)
            for k in range(KT):
                pe.wait_ge(norm["n00"]["square"], k + 1)
                pe.matmul(ps[6][:, :], ones[:, :], sq[k % 4], start=(k == 0), stop=(k == KT - 1))\
                  .then_inc(norm["n00"]["summed"], 1)
            pe.wait_ge(s_scond, 1)
            ada_first()

            def between(x):
                for c in range(8):
                    if x == min(3 * c + 4, len(units["L0"])):
                        ada_sum(c, c % 2, 2)

            proj_pe("L0", between)
            pe.wait_ge(take_rd, 8)
            pe.wait_ge(proj["L0"]["stored"], NV["L0"])
            pe.wait_ge(proj["L0"]["taken"], len(units["L0"]))
            att_pe("A0", "L0")
            out_pe("O0", "A0", S_ALL)
            norm_pe("n01", S_ALL, sq[0])

            def split3(bank, wh, wl, xh, xl, first, last):
                pe.matmul(bank, wh, xh, start=first, stop=False)
                pe.matmul(bank, wl, xh, start=False, stop=False)
                return pe.matmul(bank, wh, xl, start=False, stop=last)

            def gate_up(c, nq, i=None):
                for q in range(2):
                    f = 2 * c + q
                    pe.wait_ge(mul_rd, f + 1 if i is None else i * 4 + (f + 1))
                    for z in range(2):
                        u = first_unit("F0", c) + 2 * q + z
                        pe.wait_ge(f_lo, u + 1 if i is None else i * 8 + (u + 1))
                        wh, wl = unit_parts(u)
                        for k in range(KT):
                            if u == 0:
                                pe.wait_ge(n01_low, 2 * k + 2)
                            ins = split3(ps[2 * q + z][:, :], wh[:, k, :], wl[:, k, :], hTh[:, k, :], hTl[:, k, :],
                                         k == 0, k == KT - 1)
                        ins.then_inc(f_used, 1)
                ada_sum(8 + c, c % 2, nq, i)

            def down(half):
                f0, nf = half * HALF_T[0], HALF_T[half]
                for j in range(4 * half, 4 * half + 4):
                    for q in range(2):
                        n = 2 * j + q
                        if n >= 2:
                            pe.wait_ge(dn_add, n - 1)
                        for z in range(2):
                            u = first_unit("D0", j) + 2 * q + z
                            pe.wait_ge(f_lo, u + 1)
                            pe.wait_ge(f_hl, f0 + (z + 1) * nf // 2)
                            wh, wl = unit_parts(u)
                            for k in range(nf // 2):
                                fk = z * nf // 2 + k
                                ins = split3(ps[4 + n % 2][:, :], wh[:, k, :], wl[:, k, :], hidh[:, fk, :],
                                             hidl[:, fk, :], fk == 0, fk == nf - 1)
                            ins.then_inc(f_used, 1)

            with pe.Fori(0, 2) as i:
                for j in range(2):
                    gate_up(j, 2, i)
            for c in (4, 5):
                gate_up(c, 1)
            down(0)
            with pe.Fori(0, 2) as i:
                for j in range(2):
                    gate_up(6 + j, 1, i)
            gate_up(10, 1)
            down(1)

            ada_sum(19, 1, 1)
            norm_pe("n10", S_ALL, sq[0])
            proj_pe("L1")
            pe.wait_ge(proj["L1"]["stored"], NV["L1"])
            pe.wait_ge(proj["L1"]["taken"], len(units["L1"]))
            proj_pe("UQ")
            pe.wait_ge(proj["UQ"]["stored"], NV["UQ"])
            pe.wait_ge(proj["UQ"]["taken"], len(units["UQ"]))
            att_pe("A1", "UQ")
            out_pe("O1", "A1", S_LAT)
            norm_pe("n11", S_LAT, sq[0])
            pe.wait_ge(norm["n11"]["ready"], KT)
            for t in range(2):
                for k in range(KT):
                    pe.matmul(ps[5][:, t * NE:(t + 1) * NE], hT[:, k, t * P:(t + 1) * P], rtr[:, k, :],
                              start=(k == 0), stop=(k == KT - 1)) if not (t == 1 and k == KT - 1) else \
                        pe.matmul(ps[5][:, t * NE:(t + 1) * NE], hT[:, k, t * P:(t + 1) * P], rtr[:, k, :],
                                  start=False, stop=True).then_inc(rt_mm, 1)
            for t in range(2):
                for hh in range(2):
                    for q in range(4):
                        ins = pe.transpose(ps[2 * t + hh][:, q * P:(q + 1) * P],
                                           hT[:, 4 * hh + q, t * P:(t + 1) * P], ident)
                    ins.then_inc(tok_t, 1)
            pe.wait_ge(rt_sel, 1)
            up = cv("upper")
            ch0, ch1 = ro[:, 5, 0, :], ro[:, 5, 1, :]
            pe.matmul(ps[4][:, 0:NE], up, ch0, start=True, stop=True)
            pe.matmul(ps[4][:, NE:2 * NE], ones[:, :], ch0, start=True, stop=False)
            pe.matmul(ps[4][:, NE:2 * NE], up, ch1, start=False, stop=True)
            pe.matmul(ps[4][:, 2 * NE:3 * NE], ones[:, :], ch0, start=True, stop=False)
            pe.matmul(ps[4][:, 2 * NE:3 * NE], ones[:, :], ch1, start=False, stop=True).then_inc(rt_pos, 1)
            pe.wait_ge(tok_rd, 4)
            pe.wait_ge(items_rd, 1)
            total = pe.value_load(nit[0:1, 0:1], min_val=NE, max_val=NE * ROUNDS)
            pe.sem_inc(m_pe, URING)

            def gather(n):
                pe.wait_ge(m_sel, 1 if n is None else n + 1)
                for hh in range(2):
                    for q in range(4):
                        d = 4 * hh + q
                        for t in range(2):
                            ins = pe.matmul(ps[4 + hh][:, q * CAP:(q + 1) * CAP], htok[:, t, d * P:(d + 1) * P],
                                            sel[:, t, :], start=(t == 0), stop=(t == 1))
                    ins.then_inc(m_gat, 1)

            def scatter(n):
                for d in range(KT):
                    if d == 0:
                        pe.wait_ge(m_ya, n + 1)
                        pe.wait_ge(m_yb, n + 1)
                    ins = pe.matmul(ps[d // 2][:, (d % 2) * S_LAT:(d % 2 + 1) * S_LAT],
                                    ytok[:, d * P:(d + 1) * P], pgT[:, :], start=True, stop=True)
                    if d % 2 == 1:
                        ins.then_inc(m_sc, 1)

            gather(None)
            pe.wait_ge(m_init, 1)
            with pe.Fori(0, total) as n:
                for h in range(NU):
                    c, half = h // 2, h % 2
                    hi, lo = whi[:, h % URING, :], wlo[:, h % URING, :]
                    if h == 0:
                        pe.wait_ge(m_xl, n * 2 + 2)
                    pe.wait_ge(m_lo, n * NU + (h + 1))
                    if c < 14:
                        j, part = c // 2, c % 2
                        if part == 0 and half == 0 and j != 1:
                            pe.wait_ge(m_mul, n * 7 + (2 if j == 0 else j + 1))
                        bank = ps[4 + 2 * (j % 2) + part]
                        for k in range(4):
                            kk = 4 * half + k
                            ws = slice(k * 512, (k + 1) * 512)
                            pe.matmul(bank[:, :], xgr[:, 0, kk, :], hi[:, ws], start=(kk == 0), stop=False)
                            pe.matmul(bank[:, :], xgr[:, 0, kk, :], lo[:, ws], start=False, stop=False)
                            ins = pe.matmul(bank[:, :], xgr[:, 1, kk, :], hi[:, ws], start=False, stop=(kk == KT - 1))
                        ins.then_inc(m_pe, 1)
                    else:
                        j = c - 14
                        if h == 28:
                            pe.wait_ge(m_pg, n + 1)
                        if half == 0:
                            pe.wait_ge(m_hl, n * 7 + (j + 1))
                        for q in range(2):
                            f = QF * j + 2 * half + q
                            for z in range(2):
                                ws = slice(q * D + z * 512, q * D + z * 512 + 512)
                                pe.matmul(ps[z][:, :], hidr[:, 0, f, :], hi[:, ws], start=(f == 0), stop=False)
                                pe.matmul(ps[z][:, :], hidr[:, 0, f, :], lo[:, ws], start=False, stop=False)
                                ins = pe.matmul(ps[z][:, :], hidr[:, 1, f, :], hi[:, ws], start=False,
                                                stop=(f == FTE - 1))
                        ins.then_inc(m_pe, 1)
                    if h == 1:
                        scatter(n)
                    if h == 12:
                        pe.wait_ge(m_gsel, n + 1)
                        pe.wait_ge(m_add, n + 1)
                        for t in range(2):
                            ins = pe.transpose(ps[0][:, t * P:(t + 1) * P], gsel[:, t, :], ident)
                        ins.then_inc(m_pgt, 1)
                    j = (h - 6) // 4
                    if h % 4 == 2 and 0 <= j < 7:
                        pe.wait_ge(m_mul, n * 7 + (j + 3))
                        if j < 2:
                            pe.wait_ge(m_add, n + 1)
                        else:
                            pe.wait_ge(m_hl, n * 7 + (j - 1))
                        for q in range(QF):
                            ins = pe.transpose(ps[2 + j % 2][:, q * P:(q + 1) * P], hidtok[:, j % 2, q * P:(q + 1) * P],
                                               ident)
                        ins.then_inc(m_t, 1)
                    if h == 32:
                        pe.wait_ge(m_mul, n * 7 + 9)
                        gather(n + 1)
            scatter(total)


def kernel(**inputs):
    import concourse.bacc as _bacc
    from concourse.bass_utils import run_bass_kernel_spmd as _run

    x = {k: np.asarray(v) for k, v in inputs.items()}

    def tiles(v):
        v = v.reshape(v.shape[:-1] + (v.shape[-1] // P, P))
        return np.moveaxis(v, -1, 0)

    rpb = np.zeros((8, RPB_DR, 2 * GRID_W - 1), np.float32)
    lo = GRID_W - NA_WIN_W
    rpb[:, :, lo:lo + 2 * NA_WIN_W - 1] = x["na_rpb"][0][:, NA_WIN_H - 4:NA_WIN_H + 3]
    rpb = np.tile(rpb, (1, 1, GRID_W))
    arrays = {
        "xT": x["x"][0].T, "ctxT": x["ctx"][0].T,
        "cond": tiles(np.stack([x["c"][0], x["c_ctx"]])).transpose(0, 2, 1).reshape(P, 16),
        "adab": tiles(x["ada_b"]).reshape(P, 96),
        "ng": tiles(np.stack([x["norm1_g"], x["norm2_g"]])).reshape(P, 32),
        "vec": np.concatenate([x[n].reshape(-1) for n, _ in VEC]),
        "cst": shape_constants(), "rpb": rpb,
        "ada_w": x["ada_w"], "moe_router": x["moe_router"][0],
    }
    for n in ("ev_w_in", "ev_w_out", "ffn_w_gate", "ffn_w_up", "ffn_w_down", "od_w_in", "od_w_out",
              "mla_w_uq", "mla_w_ukv", "moe_w1", "moe_w3", "moe_w2"):
        arrays[n] = x[n][0]
    nc = _bacc.Bacc("TRN2", target_bir_lowering=False, num_devices=1)
    feed, aps = {}, {}
    for n, v in arrays.items():
        v = np.ascontiguousarray(v)
        feed[f"in_{n}"] = v
        aps[n] = nc.dram_tensor(f"in_{n}", v.shape, F32, kind="ExternalInput").ap()
    o = nc.dram_tensor("out_T", (D, S_LAT), F32, kind="ExternalOutput").ap()
    build_kernel(nc, aps, o)
    r = _run(nc, [feed], core_ids=[0])
    return np.ascontiguousarray(r.results[0]["out_T"].T)[None]
```
